# Optimizing a Trainium2 kernel written in Bass

```python
import jax, jax.numpy as jnp
from jax import lax
import numpy as np

D_MODEL = 1024
BATCH = 1
SEQ = 256
DEPTH = 2
DEC_BATCH = 8
DEC_SEQ = 8
PAST_LEN = 1024
PAGE_SIZE = 128

BRANCH_W = 512
N_BRANCH = 4
A_HEADS = 4
A_DK = 128
A_DV = 128
B_HEADS = 8
B_Q_RANK = 384
B_KV_RANK = 256
B_NOPE = 64
B_ROPE = 32
B_VDIM = 64
C_CH = 512
C_WIDTH = 31
D_HEADS = 4
D_DK = 128
D_DV = 128
FFN_HIDDEN = -(-8 * D_MODEL // (3 * 256)) * 256
CHUNK = 128
Q_BLOCK = 128
ROPE_BASE = 10000.0
LN_EPS = 1e-5
RMS_EPS = 1e-6
DEEPNORM_ALPHA = (2 * DEPTH) ** 0.25
DEEPNORM_BETA = (8 * DEPTH) ** -0.25
CACHE_W = B_KV_RANK + B_ROPE
IN_SIZES = (A_HEADS * A_DK, A_HEADS * A_DK, A_HEADS * A_DV, A_HEADS * A_DV, A_HEADS, A_HEADS,
            B_Q_RANK, B_KV_RANK, B_ROPE,
            2 * C_CH,
            D_HEADS * D_DK, D_HEADS * D_DK, D_HEADS * D_DV, D_HEADS * D_DV,
            N_BRANCH * D_MODEL)
IN_OFFSETS = tuple(int(o) for o in np.cumsum(IN_SIZES)[:-1])
N_IN = int(sum(IN_SIZES))
A_F_OFFSET = IN_OFFSETS[4]

kernel_name = 'hybrid_mlstm_mla_conv_retention_decode_step'

def layer_norm(x, g=None, b=None):
    xf = x.astype(jnp.float32)
    mu = jnp.mean(xf, axis=-1, keepdims=True)
    var = jnp.mean(jnp.square(xf - mu), axis=-1, keepdims=True)
    y = (xf - mu) * lax.rsqrt(var + LN_EPS)
    if g is not None:
        y = y * g + b
    return y

def rms_norm(x, g):
    xf = x.astype(jnp.float32)
    return xf * lax.rsqrt(jnp.mean(xf * xf, axis=-1, keepdims=True) + RMS_EPS) * g

def rotary(x, pos):
    d = x.shape[-1]
    inv = ROPE_BASE ** (-jnp.arange(0, d, 2, dtype=jnp.float32) / d)
    ang = pos.astype(jnp.float32)[:, None] * inv[None, :]
    cos = jnp.cos(ang)[None, :, None, :]
    sin = jnp.sin(ang)[None, :, None, :]
    x1, x2 = jnp.split(x.astype(jnp.float32), 2, axis=-1)
    return jnp.concatenate([x1 * cos - x2 * sin, x1 * sin + x2 * cos], axis=-1)

def to_chunks(t, L):
    B, T = t.shape[:2]
    return jnp.moveaxis(t.reshape((B, T // L, L) + t.shape[2:]), 1, 0)

def from_chunks(t):
    nc, B, L = t.shape[:3]
    return jnp.moveaxis(t, 0, 1).reshape((B, nc * L) + t.shape[3:])

def mlstm_chunk(carry, inp):
    C, n, m = carry
    q, k, v, ig, lf = inp
    L = q.shape[1]
    b = jnp.cumsum(lf, axis=1)
    inter = b + m[:, None, :]
    intra = b[:, :, None, :] - b[:, None, :, :] + ig[:, None, :, :]
    causal = jnp.tril(jnp.ones((L, L), dtype=bool))[None, :, :, None]
    intra = jnp.where(causal, intra, -jnp.inf)
    m_t = jnp.maximum(inter, jnp.max(intra, axis=2))
    w_inter = jnp.exp(inter - m_t)
    s = jnp.einsum('bqhd,bshd->bqsh', q, k) * jnp.exp(intra - m_t[:, :, None, :])
    num = jnp.einsum('bqsh,bshv->bqhv', s, v) + w_inter[..., None] * jnp.einsum('bqhd,bhdv->bqhv', q, C)
    den = jnp.sum(s, axis=2) + w_inter * jnp.einsum('bqhd,bhd->bqh', q, n)
    h = num / jnp.maximum(jnp.abs(den), jnp.exp(-m_t))[..., None]
    bL = b[:, -1]
    m_new = m_t[:, -1]
    w_c = jnp.exp(bL + m - m_new)
    w_s = jnp.exp(bL[:, None, :] - b + ig - m_new[:, None, :])
    C_new = w_c[..., None, None] * C + jnp.einsum('bsh,bshd,bshv->bhdv', w_s, k, v)
    n_new = w_c[..., None] * n + jnp.einsum('bsh,bshd->bhd', w_s, k)
    return (C_new, n_new, m_new), h

def mlstm(q, k, v, ig, lf, C0, n0, m0):
    L = min(CHUNK, q.shape[1])
    xs = (to_chunks(q, L), to_chunks(k, L), to_chunks(v, L), to_chunks(ig, L), to_chunks(lf, L))
    (C, n, m), h = lax.scan(mlstm_chunk, (C0, n0, m0), xs)
    return from_chunks(h), C, n, m

def retention(q, k, v, S0):
    log_gamma = jnp.log(1.0 - 2.0 ** (-5.0 - jnp.arange(D_HEADS, dtype=jnp.float32)))
    L = min(CHUNK, q.shape[1])
    j = jnp.arange(L, dtype=jnp.float32)
    diff = j[:, None] - j[None, :]
    decay = jnp.where((diff >= 0)[..., None], jnp.exp(jnp.maximum(diff, 0.0)[..., None] * log_gamma), 0.0)
    w_in = jnp.exp((j + 1.0)[:, None] * log_gamma)
    w_st = jnp.exp((L - 1.0 - j)[:, None] * log_gamma)
    w_S = jnp.exp(L * log_gamma)

    def chunk(S, inp):
        qc, kc, vc = inp
        s = jnp.einsum('bqhd,bshd->bqsh', qc, kc) * decay[None]
        o = jnp.einsum('bqsh,bshv->bqhv', s, vc) + w_in[None, :, :, None] * jnp.einsum('bqhd,bhdv->bqhv', qc, S)
        S_new = w_S[None, :, None, None] * S + jnp.einsum('sh,bshd,bshv->bhdv', w_st, kc, vc)
        return S_new, o

    S, o = lax.scan(chunk, S0, (to_chunks(q, L), to_chunks(k, L), to_chunks(v, L)))
    return from_chunks(o), S

def conv_module(glu_in, buf, w, b, g, beta):
    glu_in = glu_in.astype(jnp.float32)
    u = glu_in[..., :C_CH] * jax.nn.sigmoid(glu_in[..., C_CH:])
    full = jnp.concatenate([buf.astype(jnp.float32), u], axis=1)
    y = lax.conv_general_dilated(full, w.astype(jnp.float32)[:, None, :], window_strides=(1,), padding='VALID',
                                 dimension_numbers=('NWC', 'WIO', 'NWC'), feature_group_count=C_CH)
    y = jax.nn.silu(layer_norm(y + b, g, beta))
    return y, full[:, -(C_WIDTH - 1):]

def mla_prompt_attention(q_abs, q_pe, ckv, kpe):
    T = q_abs.shape[1]
    L = min(Q_BLOCK, T)
    scale = (B_NOPE + B_ROPE) ** -0.5
    kpos = jnp.arange(T)

    def block(args):
        ql, qp, i = args
        qpos = i * L + jnp.arange(L)
        s = (jnp.einsum('bqhr,bkr->bhqk', ql, ckv) + jnp.einsum('bqhp,bkp->bhqk', qp, kpe)) * scale
        s = jnp.where((kpos[None, :] <= qpos[:, None])[None, None], s, -jnp.inf)
        p = jax.nn.softmax(s.astype(jnp.float32), axis=-1)
        return jnp.einsum('bhqk,bkr->bqhr', p, ckv)

    o = lax.map(block, (to_chunks(q_abs, L), to_chunks(q_pe, L), jnp.arange(T // L)))
    return from_chunks(o)

def mla_sample_attention(q_abs, q_pe, ckv, kpe, past):
    T = q_abs.shape[1]
    P = past.shape[1]
    scale = (B_NOPE + B_ROPE) ** -0.5
    pc = past[..., :B_KV_RANK].astype(jnp.float32)
    pp = past[..., B_KV_RANK:].astype(jnp.float32)
    s_past = (jnp.einsum('bqhr,bkr->bhqk', q_abs, pc) + jnp.einsum('bqhp,bkp->bhqk', q_pe, pp)) * scale
    s_new = (jnp.einsum('bqhr,bkr->bhqk', q_abs, ckv) + jnp.einsum('bqhp,bkp->bhqk', q_pe, kpe)) * scale
    s_new = jnp.where(jnp.tril(jnp.ones((T, T), dtype=bool))[None, None], s_new, -jnp.inf)
    p = jax.nn.softmax(jnp.concatenate([s_past, s_new], axis=-1).astype(jnp.float32), axis=-1)
    return jnp.einsum('bhqk,bkr->bqhr', p[..., :P], pc) + jnp.einsum('bhqk,bkr->bqhr', p[..., P:], ckv)

def mixer_branches(u, pos, lw, st, mla_past):
    B, T, _ = u.shape
    f32 = jnp.float32
    C0, n0, m0, buf0, S0 = st
    z = u @ lw['w_in'] + lw['b_in']
    (a_q, a_k, a_v, a_o, a_i, a_f, b_q, b_kv, b_kr, c_glu,
     d_q, d_k, d_v, d_g, gates) = jnp.split(z, IN_OFFSETS, axis=-1)

    def heads(t, h):
        return t.reshape(B, T, h, -1).astype(f32)

    qa = heads(a_q, A_HEADS) * A_DK ** -0.5
    h_a, C1, n1, m1 = mlstm(qa, heads(a_k, A_HEADS), heads(a_v, A_HEADS), a_i.astype(f32),
                            jax.nn.log_sigmoid(a_f.astype(f32)), C0, n0, m0)
    y_a = jax.nn.sigmoid(a_o) * layer_norm(h_a).reshape(B, T, -1)

    qb = (rms_norm(b_q, lw['q_norm']) @ lw['w_uq']).reshape(B, T, B_HEADS, B_NOPE + B_ROPE)
    q_pe = rotary(qb[..., B_NOPE:], pos)
    q_abs = jnp.einsum('bthn,rhn->bthr', qb[..., :B_NOPE], lw['w_uk'])
    ckv = rms_norm(b_kv, lw['kv_norm'])
    kpe = rotary(b_kr[:, :, None, :], pos)[:, :, 0, :]
    new_rows = jnp.concatenate([ckv, kpe], axis=-1)
    if mla_past is None:
        o_lat = mla_prompt_attention(q_abs, q_pe, ckv, kpe)
    else:
        o_lat = mla_sample_attention(q_abs, q_pe, ckv, kpe, mla_past)
    y_b = jnp.einsum('bthr,rhv->bthv', o_lat, lw['w_uv']).reshape(B, T, -1)

    y_c, buf1 = conv_module(c_glu, buf0, lw['conv_w'], lw['conv_b'], lw['conv_ln_g'], lw['conv_ln_b'])

    qd = rotary(heads(d_q, D_HEADS), pos)
    kd = rotary(heads(d_k, D_HEADS), pos) * D_DK ** -0.5
    o_d, S1 = retention(qd, kd, heads(d_v, D_HEADS), S0)
    y_d = jax.nn.silu(d_g) * layer_norm(o_d).reshape(B, T, -1)

    ys = jnp.stack([y_a, y_b, y_c, y_d], axis=2)
    proj = jnp.einsum('btnw,nwd->btnd', ys, lw['w_branch'])
    g = jax.nn.sigmoid(gates.reshape(B, T, N_BRANCH, D_MODEL))
    out = jnp.sum(g * proj, axis=2) @ lw['w_out']
    return out, (new_rows, C1, n1, m1, buf1, S1)

def trunk_layer(x, c, pos, lw, st, mla_past):
    mod = jax.nn.silu(c) @ lw['w_ada'] + lw['b_ada']
    sh1, sc1, g1, sh2, sc2, g2 = jnp.split(mod[:, None, :], 6, axis=-1)
    u = x * (1.0 + sc1) + sh1
    mix, new_st = mixer_branches(u, pos, lw, st, mla_past)
    x = layer_norm(DEEPNORM_ALPHA * x + g1 * mix, lw['ln1_g'], lw['ln1_b'])
    u2 = x * (1.0 + sc2) + sh2
    f = (jax.nn.silu(u2 @ lw['w1']) * (u2 @ lw['w3'])) @ lw['w2']
    x = layer_norm(DEEPNORM_ALPHA * x + g2 * f, lw['ln2_g'], lw['ln2_b'])
    return x, new_st

def setup_inputs(seed: int = 0) -> dict:
    key = jax.random.key(seed)
    counter = [0]

    def nk():
        counter[0] += 1
        return jax.random.fold_in(key, counter[0])

    def nrm(shape, scale=1.0):
        return jax.random.normal(nk(), shape, jnp.float32) * scale

    def gain(shape):
        return 1.0 + nrm(shape, 0.02)

    n_pages = PAST_LEN // PAGE_SIZE
    n_pool = (DEC_BATCH * n_pages * 5) // 4
    page_table = jax.random.permutation(nk(), n_pool)[: DEC_BATCH * n_pages].reshape(DEC_BATCH, n_pages).astype(jnp.int32)
    b_in = nrm((DEPTH, N_IN), 0.02).at[:, A_F_OFFSET:A_F_OFFSET + A_HEADS].add(jnp.linspace(3.0, 6.0, A_HEADS))
    return {
        'x_prompt': nrm((BATCH, SEQ, D_MODEL)),
        'x_sample': nrm((DEC_BATCH, DEC_SEQ, D_MODEL)),
        'cache_mla': nrm((DEPTH, n_pool, PAGE_SIZE, CACHE_W)),
        'state_mlstm_C': nrm((DEPTH, DEC_BATCH, A_HEADS, A_DK, A_DV), 0.5),
        'state_mlstm_n': nrm((DEPTH, DEC_BATCH, A_HEADS, A_DK), 0.5),
        'state_mlstm_m': nrm((DEPTH, DEC_BATCH, A_HEADS), 0.5),
        'state_conv': nrm((DEPTH, DEC_BATCH, C_WIDTH - 1, C_CH), 0.5),
        'state_ret': nrm((DEPTH, DEC_BATCH, D_HEADS, D_DK, D_DV)),
        'page_table': page_table,
        'c_prompt': nrm((BATCH, D_MODEL)),
        'c_sample': nrm((DEC_BATCH, D_MODEL)),
        'w_ada': nrm((DEPTH, D_MODEL, 6 * D_MODEL), 0.5 * D_MODEL ** -0.5),
        'b_ada': nrm((DEPTH, 6 * D_MODEL), 0.02),
        'w_in': nrm((DEPTH, D_MODEL, N_IN), D_MODEL ** -0.5),
        'b_in': b_in,
        'mla_q_norm': gain((DEPTH, B_Q_RANK)),
        'mla_w_uq': nrm((DEPTH, B_Q_RANK, B_HEADS * (B_NOPE + B_ROPE)), B_Q_RANK ** -0.5),
        'mla_kv_norm': gain((DEPTH, B_KV_RANK)),
        'mla_w_uk': nrm((DEPTH, B_KV_RANK, B_HEADS, B_NOPE), B_KV_RANK ** -0.5),
        'mla_w_uv': nrm((DEPTH, B_KV_RANK, B_HEADS, B_VDIM), B_KV_RANK ** -0.5),
        'conv_w': nrm((DEPTH, C_WIDTH, C_CH), C_WIDTH ** -0.5),
        'conv_b': nrm((DEPTH, C_CH), 0.02),
        'conv_ln_g': gain((DEPTH, C_CH)),
        'conv_ln_b': nrm((DEPTH, C_CH), 0.02),
        'w_branch': nrm((DEPTH, N_BRANCH, BRANCH_W, D_MODEL), BRANCH_W ** -0.5),
        'w_out': nrm((DEPTH, D_MODEL, D_MODEL), DEEPNORM_BETA * D_MODEL ** -0.5),
        'ln1_g': gain((DEPTH, D_MODEL)),
        'ln1_b': nrm((DEPTH, D_MODEL), 0.02),
        'w_ffn1': nrm((DEPTH, D_MODEL, FFN_HIDDEN), D_MODEL ** -0.5),
        'w_ffn3': nrm((DEPTH, D_MODEL, FFN_HIDDEN), D_MODEL ** -0.5),
        'w_ffn2': nrm((DEPTH, FFN_HIDDEN, D_MODEL), DEEPNORM_BETA * FFN_HIDDEN ** -0.5),
        'ln2_g': gain((DEPTH, D_MODEL)),
        'ln2_b': nrm((DEPTH, D_MODEL), 0.02),
    }

def reference(x_prompt, x_sample, cache_mla, state_mlstm_C, state_mlstm_n, state_mlstm_m, state_conv, state_ret,
              page_table, c_prompt, c_sample, w_ada, b_ada, w_in, b_in, mla_q_norm, mla_w_uq, mla_kv_norm,
              mla_w_uk, mla_w_uv, conv_w, conv_b, conv_ln_g, conv_ln_b, w_branch, w_out, ln1_g, ln1_b,
              w_ffn1, w_ffn3, w_ffn2, ln2_g, ln2_b):
    f32 = jnp.float32
    dt = x_prompt.dtype
    Bp, Tp = x_prompt.shape[:2]
    Bd, Td = x_sample.shape[:2]
    past_len = page_table.shape[1] * PAGE_SIZE
    pos_p = jnp.arange(Tp)
    pos_d = past_len + jnp.arange(Td)
    xp, xd = x_prompt, x_sample
    p_states = [[] for _ in range(6)]
    d_states = [[] for _ in range(6)]
    for l in range(DEPTH):
        lw = {'w_ada': w_ada[l], 'b_ada': b_ada[l], 'w_in': w_in[l], 'b_in': b_in[l],
              'q_norm': mla_q_norm[l], 'w_uq': mla_w_uq[l], 'kv_norm': mla_kv_norm[l],
              'w_uk': mla_w_uk[l], 'w_uv': mla_w_uv[l], 'conv_w': conv_w[l], 'conv_b': conv_b[l],
              'conv_ln_g': conv_ln_g[l], 'conv_ln_b': conv_ln_b[l], 'w_branch': w_branch[l],
              'w_out': w_out[l], 'ln1_g': ln1_g[l], 'ln1_b': ln1_b[l], 'w1': w_ffn1[l], 'w3': w_ffn3[l],
              'w2': w_ffn2[l], 'ln2_g': ln2_g[l], 'ln2_b': ln2_b[l]}
        st_p = (jnp.zeros((Bp, A_HEADS, A_DK, A_DV), f32), jnp.zeros((Bp, A_HEADS, A_DK), f32),
                jnp.zeros((Bp, A_HEADS), f32), jnp.zeros((Bp, C_WIDTH - 1, C_CH), f32),
                jnp.zeros((Bp, D_HEADS, D_DK, D_DV), f32))
        xp, new_p = trunk_layer(xp, c_prompt, pos_p, lw, st_p, None)
        past = cache_mla[l][page_table].reshape(Bd, past_len, cache_mla.shape[-1])
        st_d = (state_mlstm_C[l].astype(f32), state_mlstm_n[l].astype(f32), state_mlstm_m[l].astype(f32),
                state_conv[l].astype(f32), state_ret[l].astype(f32))
        xd, new_d = trunk_layer(xd, c_sample, pos_d, lw, st_d, past)
        for i in range(6):
            p_states[i].append(new_p[i])
            d_states[i].append(new_d[i])
    ps = [jnp.stack(s, axis=0).astype(dt) for s in p_states]
    ds = [jnp.stack(s, axis=0).astype(dt) for s in d_states]
    y_prompt = xp.astype(dt)
    y_sample = xd.astype(dt)
    return (y_prompt, y_sample, ps[0], ds[0], ps[1], ds[1], ps[2], ds[2], ps[3], ds[3], ps[4], ds[4], ps[5], ds[5])


_drawn_inputs = setup_inputs


def setup_inputs(seed=0):
    import zlib

    import numpy as np

    out = dict(_drawn_inputs(seed))
    spreads = {}
    factors = {'cache_mla': 8.0,
     'mla_q_norm': 8.0,
     'mla_w_uq': 4.593,
     'mla_kv_norm': 3.2,
     'mla_w_uk': 5.456,
     'conv_b': 8.0,
     'conv_ln_g': 8.0,
     'conv_ln_b': 8.0}
    for name, (base, spread) in spreads.items():
        noise = np.random.default_rng([zlib.crc32(name.encode()), seed]).standard_normal(out[name].shape)
        drawn = base * np.exp(spread * noise) if base else spread * noise
        out[name] = __import__('jax').numpy.asarray(drawn.astype(out[name].dtype))
    for name, factor in factors.items():
        out[name] = (out[name] * factor).astype(out[name].dtype)
    return out
```

```python
from contextlib import ExitStack

import numpy as np

import concourse.bass as bass
from concourse import mybir
from concourse.alu_op_type import AluOpType as ALU

F32 = mybir.dt.float32
I32 = mybir.dt.int32
ACT = mybir.ActivationFunctionType
AX = mybir.AxisListType.X

P = 128
D_MODEL, SEQ, DEPTH, NB, TS, PAST, PAGE = 1024, 256, 2, 8, 8, 1024, 128
NS = NB * TS
T = SEQ + NS
KC = D_MODEL // P
H = 4
BH, NOPE, ROPE, VD = 8, 64, 32, 64
QR, KVR = 384, 256
CW, CCH = 31, 512
HID = 2816
FT = HID // P
NPG = PAST // PAGE
POOL = NB * NPG * 5 // 4
ALPHA = (2 * DEPTH) ** 0.25
LN_EPS, RMS_EPS = 1e-5, 1e-6
QSCALE = P ** -0.5
BSCALE = (NOPE + ROPE) ** -0.5
NEG = -1.0e30
TOK = [(0, 128), (128, 128), (256, NS)]
W = 129
SAMP = slice(SEQ, T)

OFF = {}
_at = 0
for _n, _w in (("aq", 512), ("ak", 512), ("av", 512), ("ao", 512), ("ai", 4), ("af", 4), ("bq", QR), ("bkv", KVR),
               ("bkr", ROPE), ("ca", CCH), ("cg", CCH), ("dq", 512), ("dk", 512), ("dv", 512), ("dg", 512),
               ("gates", 4 * D_MODEL)):
    OFF[_n] = _at
    _at += _w

GATE_ORDER = (0, 2, 3, 1)
BLOCKS = ([("ada", a) for a in range(8)] + [("in", "small", "kv0"), ("in", "kv1", "bq0"), ("in", "bq1", "bq2")]
          + [("uq",), ("uk",), ("ukT",)]
          + [("in", f"{x}{i}", f"{x}{i + 1}") for x in ("ak", "aq", "av", "ao") for i in (0, 2)]
          + [("in", f"cg{j}", f"ca{j}") for j in range(4)]
          + [("in", f"{x}{i}", f"{x}{i + 1}") for x in ("dk", "dq", "dv", "dg") for i in (0, 2)])
for _n in GATE_ORDER[:2]:
    for _h in (0, 4):
        BLOCKS += [("in", f"g{_n}_{_h}", f"g{_n}_{_h + 1}"), ("in", f"g{_n}_{_h + 2}", f"g{_n}_{_h + 3}"), ("branch", _n, _h)]


SLOTS = [[("gate", 3, 0), ("gate", 3, 2)],
         [("branch", 3, 0), ("ada", 8), ("ada", 9)],
         [("gate", 3, 4), ("ada", 10), ("ada", 11)],
         [("gate", 3, 6), ("ada", 12), ("ada", 13)],
         [("branch", 3, 4), ("ada", 14)],
         [("gate", 1, 0), ("ada", 15)],
         [("gate", 1, 2), ("ada", 16)],
         [("gate", 1, 4)],
         [("gate", 1, 6), ("ada", 17)]]
SLOT_START = []
for _slot in SLOTS:
    SLOT_START.append(len(BLOCKS))
    for _u in _slot:
        BLOCKS += [("in", f"g{_u[1]}_{_u[2]}", f"g{_u[1]}_{_u[2] + 1}") if _u[0] == "gate" else _u]
BLOCKS += [("branch", 1, 0), ("branch", 1, 4)]
BLOCKS += [("out", i) for i in range(4)] + [("ada", a) for a in range(18, 24)]
BLOCKS += [("ffn", j) for j in range(FT)] + [("ffn2", i) for i in range(11)]
NBLK = len(BLOCKS)
RING = 3

TILES = (["small", "kv0", "kv1", "bq0", "bq1", "bq2"] + [f"{x}{i}" for x in ("aq", "ak", "av", "ao", "ca", "cg", "dq", "dk", "dv", "dg") for i in range(4)]
         + [f"g{n}_{i}" for n in range(4) for i in range(8)])
BIAS = {n: 48 + i for i, n in enumerate(TILES)}
SM = {}
_at = 48 + len(TILES)
for _n, _w in (("qn", 3), ("kvn", 2), ("cb", 4), ("clg", 4), ("clb", 4), ("ln1g", 8), ("ln1b", 8), ("ln2g", 8), ("ln2b", 8), ("cw", 4 * CW)):
    SM[_n] = _at
    _at += _w
NSM = _at


def tile_columns(name):
    if name == "small":
        return [(0, OFF["ai"], 4), (32, OFF["af"], 4), (64, OFF["bkr"], 32)]
    if name[:2] == "kv":
        return [(0, OFF["bkv"] + P * int(name[2]), P)]
    if name[0] == "g":
        n, i = name[1:].split("_")
        return [(0, OFF["gates"] + D_MODEL * int(n) + P * int(i), P)]
    return [(0, OFF[name[:2]] + P * int(name[2]), P)]


def constants():
    f = np.float32
    c = {}
    c["ident"] = np.eye(P, dtype=f)
    c["ones"] = np.ones((P, P), f)
    pos = np.concatenate([np.arange(SEQ), np.tile(PAST + np.arange(TS), NB)]).astype(f)

    def rot(d, reps):
        inv = (f(10000.0) ** (-np.arange(0, d, 2, dtype=f) / f(d))).astype(f)
        ang = (pos[None, :] * inv[:, None]).astype(f)
        cos, sin = np.cos(ang.astype(np.float64)), np.sin(ang.astype(np.float64))
        return np.tile(np.concatenate([cos, cos]), (reps, 1)).astype(f), np.tile(np.concatenate([-sin, sin]), (reps, 1)).astype(f)

    c["cosD"], c["sinD"] = rot(P, 1)
    c["cosB"], c["sinB"] = rot(ROPE, 4)
    m = np.arange(P)
    c["swapD"] = (m[:, None] == (m[None, :] + 64) % P).astype(f)
    c["swapB"] = (m[:, None] == (m[None, :] // 32) * 32 + (m[None, :] + 16) % 32).astype(f)
    tri = (m[:, None] <= m[None, :]).astype(f)
    s = np.arange(NS)
    tri_s = np.zeros((P, NS), f)
    tri_s[:NS] = ((s[:, None] // TS == s[None, :] // TS) & (s[:, None] <= s[None, :]))
    c["causal"] = np.concatenate([tri, np.ones((P, P), f), tri, tri_s], 1)
    lg = np.log(1.0 - 2.0 ** (-5.0 - np.arange(H)))
    dec = np.zeros((P, H, 320))
    diff = m[None, :] - m[:, None]
    for h in range(H):
        dec[:, h, 0:128] = np.where(diff >= 0, np.exp(np.maximum(diff, 0) * lg[h]), 0)
        dec[:, h, 128:256] = np.exp((diff + 128) * lg[h])
        d8 = s[None, :] - s[:, None]
        dec[:NS, h, 256:320] = np.where(tri_s[:NS] > 0, np.exp(np.maximum(d8, 0) * lg[h]), 0)
    c["decay"] = (dec * QSCALE).reshape(P, -1).astype(f)
    c["w_in_ret"] = np.tile(np.exp((np.arange(TS) + 1.0)[None, :] * lg[:, None]).reshape(1, H * TS), (P, 1)).astype(f)
    wst = np.zeros((P, 3, H))
    for t in range(2):
        wst[:, t] = np.exp((SEQ - 1 - 128 * t - m)[:, None] * lg[None, :])
    wst[:NS, 2] = np.exp((TS - 1 - s % TS)[:, None] * lg[None, :])
    c["w_st"] = (wst * QSCALE).reshape(P, -1).astype(f)
    bm = np.zeros((P, NB), f)
    bm[s, s // TS] = 1
    c["batch"] = bm
    neg = np.where(m[None, :] <= m[:, None], 0, NEG)
    c["negP"] = np.concatenate([np.zeros((P, P)), neg], 1).astype(f)
    ns = np.full((P, NB, NS), NEG)
    q = np.arange(NS) % TS
    for b in range(NB):
        ok = (s[None, :] // TS == b) & (s[None, :] % TS <= q[:, None])
        ns[:NS, b] = np.where(ok, 0, NEG)
    c["negS"] = ns.reshape(P, -1).astype(f)
    reset = np.ones((P, T), f)
    reset[:, 0] = 0
    reset[:, SEQ::TS] = 0
    c["reset"] = reset
    c["eps"] = np.tile(np.array([[LN_EPS, RMS_EPS, 1.0, 0.0]], f), (P, 1))
    return c


CONST = constants()
CAT = {}
_at = 0
for _n, _a in CONST.items():
    CAT[_n] = (_at, _a.shape[1])
    _at += _a.shape[1]
NCONST = _at
WS_GAMMA = {n: [float(np.exp(n * np.log(1.0 - 2.0 ** (-5.0 - h)))) for h in range(H)] for n in (TS,)}


class Counts:

    def __init__(self, nc, ctx, known):
        self.nc, self.ctx, self.known = nc, ctx, known
        self.sems, self.value, self.total = {}, {}, {}
        self.waited, self.last = {}, {}

    def sem(self, name):
        if name not in self.sems:
            self.sems[name] = self.ctx.enter_context(self.nc.semaphore(name))
        return self.sems[name]

    def ev(self, name, label, by=1):
        self.total[name] = self.total.get(name, 0) + by
        assert (name, label) not in self.value, (name, label)
        self.value[name, label] = self.total[name]
        self.last[name.split("_")[0]] = (name, self.total[name])
        return self.sem(name), by

    def at(self, name, label):
        return self.sem(name), self.known[name, label] if self.known else 1


def decoder_program(nc, a, known):
    ctx = ExitStack()
    with ctx:
        def sb(name, shape, dt=F32):
            return ctx.enter_context(nc.sbuf_tensor(name, shape, dt))

        C = Counts(nc, ctx, known)
        ev, at = C.ev, C.at

        def in_turn(eng, prefix):
            name, value = C.last.get(prefix, (None, 0))
            if name and C.waited.get((eng, name), 0) < value:
                eng.wait_ge(C.sem(name), value)
                C.waited[eng, name] = value

        const = sb("const", [P, NCONST])

        def cs(name):
            o, n = CAT[name]
            return const[:, o:o + n]

        ident, ones = cs("ident"), cs("ones")
        smallw = sb("smallw", [P, NSM])

        def sw(name, i=0, n=1):
            o = (SM[name] if name in SM else BIAS[name]) + i
            return smallw[:, o:o + n]

        x = sb("x", [P, KC, T])
        u = sb("u", [P, KC, T])
        acc = sb("acc", [P, KC, T])
        ring = sb("ring", [P, RING, 2048])
        y = sb("y", [P, 4, 4, T])
        mod = sb("mod", [P, 48, 9])
        siluc = sb("siluc", [P, KC, 9])
        rowb = sb("rowb", [9, 2, 256])
        ckv = sb("ckv", [P, 2, T])
        kpe = sb("kpe", [P, T])
        ckvtok = sb("ckvtok", [P, 3, KVR])
        q96 = sb("q96", [P, BH, T])
        gsum = q96
        qabs = sb("qabs", [P, 2, NB, NS])
        qpes = sb("qpes", [P, NB, NS])
        wuv = sb("wuv", [P, 2, BH * VD])
        gt = sb("gt", [P, 4, T])
        tmp = sb("tmp", [P, 2, T])
        std = sb("std", [P, T])
        stats = sb("stats", [P, 128])
        pages = sb("pages", [1, NB * NPG], I32)
        arena = sb("arena", [P, 17600])

        used = [0]

        def part(n, shape, names, rows=P, start=None):
            o = used[0] if start is None else start
            v = arena[:, o:o + n].rearrange(f"p ({names}) -> p {names}", **shape) if shape else arena[:, o:o + n]
            if start is None:
                used[0] += n
            assert o + n <= 17600
            return v

        qm = part(H * T, dict(h=H, t=T), "h t")
        km = part(H * T, dict(h=H, t=T), "h t")
        vm = part(H * T, dict(h=H, t=T), "h t")
        ktok = part(3 * 512, dict(n=3, h=H, d=P), "n h d")
        vtok = part(3 * H * W, dict(n=3, h=H, d=W), "n h d")
        state = part(NB * H * W, dict(b=NB, h=H, d=W), "b h d")
        eb = part(2 * 448, dict(r=2, t=448), "r t")
        wb = part(2 * 448, dict(r=2, t=448), "r t")
        hh = part(3 * 512, dict(n=3, h=H, d=P), "n h d")
        kmb = part(2 * 512, dict(r=2, d=512), "r d")
        qz = part(8 * 264, None, None)
        hh0 = used[0] - 2 * 512 - 8 * 264 - 3 * 512
        grow = part(6 * T, dict(r=6, t=T), "r t", start=hh0)[0:4]
        r4 = part(T, None, None, start=hh0 + 6 * T)
        bqz = part(3 * T, dict(c=3, t=T), "c t", start=0)
        sq5 = part(5 * T, dict(c=5, t=T), "c t", start=3 * T)
        qr = part(2 * T, dict(c=2, t=T), "c t", start=8 * T)
        krz = part(T, None, None, start=10 * T)
        used[0] = 0
        cache = part(2 * NPG * 512, dict(r=2, g=NPG, f=512), "r g f")
        ropeT = part(2 * NPG * P, dict(r=2, g=NPG, f=P), "r g f")
        pb = part(2 * 1088, dict(r=2, f=1088), "r f")
        pT = part(2 * 576, dict(r=2, f=576), "r f")
        olat = part(2 * KVR, dict(r=2, f=KVR), "r f")
        olatT = part(2 * BH * NS, dict(c=2, h=BH, t=NS), "c h t")
        hid = arena[:, 0:FT * T].rearrange("p (j t) -> p j t", j=FT)

        accf = acc[:].rearrange("p k t -> p (k t)")
        vlat = accf[:, 0:1024].rearrange("p (n f) -> p n f", n=2)
        pp = accf[:, 1024:1536].rearrange("p (r f) -> p r f", r=2)
        ppT = accf[:, 1536:2304].rearrange("p (r f) -> p r f", r=2)
        yf = y[:].rearrange("p n k t -> p (n k t)")
        k96 = yf[:, 2 * 1280:2 * 1280 + BH * SEQ].rearrange("p (h t) -> p h t", h=BH)
        ucp = accf[:, 0:4 * 286].rearrange("p (j t) -> p j t", j=4)
        ucs = accf[:, 1144:1144 + 4 * NB * 38].rearrange("p (j b t) -> p j b t", j=4, b=NB)
        sqc = accf[:, 0:4 * T].rearrange("p (j t) -> p j t", j=4)
        growk = sb("growk", [4, 2, T])
        m0 = sb("m0", [4, NB])
        mout = sb("mout", [4, 9])
        col4 = sb("col4", [P, 3, 100])
        wint = sb("wint", [P, H, NS])
        cnp = vm[:].rearrange("p h t -> p (h t)")[:, 0:H * W].rearrange("p (h d) -> p h d", h=H)

        zps = [ctx.enter_context(nc.psum_tensor(f"zps{i}", [P, 512], F32)) for i in range(3)]
        mps = [ctx.enter_context(nc.psum_tensor(f"mps{i}", [P, 512], F32)) for i in range(5)]
        banks = {}

        pre = {n: ctx.enter_context(nc.semaphore(n)) for n in ("pre_dma", "pre_act")}
        with nc.Block() as block:
            @block.sync
            def _(sp):
                sp.dma_start(const[:], a["consts"]).then_inc(pre["pre_dma"], 16)
                sp.dma_start(x[:], a["x"]).then_inc(pre["pre_dma"], 16)
                sp.dma_start(mod[:, 0:KC, :], a["c"]).then_inc(pre["pre_dma"], 16)
                sp.dma_start(pages[:], a["pages"]).then_inc(pre["pre_dma"], 16)
                sp.wait_ge(pre["pre_dma"], 64)

            @block.scalar
            def _(act):
                act.wait_ge(pre["pre_dma"], 64)
                nc.scalar.activation(siluc[:], mod[:, 0:KC, :], ACT.Silu).then_inc(pre["pre_act"], 1)
                act.wait_ge(pre["pre_act"], 1)
        nc.all_engine_barrier()

        with nc.Fori(0, DEPTH) as layer:
            with nc.Block() as block:
                block_end = {}

                @block.tensor
                def _(pe):
                    zi, mi, bi, turned = [0], [0], [0], [0]
                    zfree, mfree = [None] * 3, [None] * 5

                    def bank(kind, name, freed_by):
                        i, frees, tiles = (zi, zfree, zps) if kind == "z" else (mi, mfree, mps)
                        n = i[0] % len(tiles)
                        i[0] += 1
                        if frees[n]:
                            pe.wait_ge(*at(*frees[n]))
                        frees[n] = freed_by
                        banks[name] = tiles[n]
                        return tiles[n]

                    def weights(want):
                        n = bi[0]
                        assert BLOCKS[n] == want, (BLOCKS[n], want)
                        bi[0] += 1
                        pe.wait_ge(C.sem(f"w_landed{n % RING}"), 16 * (n // RING + 1))
                        return n, ring[:, n % RING, :]

                    def group(kind, name, freed_by, mms, out=None):
                        ps = bank(kind, name, freed_by)
                        o = ps[:, 0:T] if out is None else out(ps)
                        for i, (l, r) in enumerate(mms):
                            last = nc.tensor.matmul(o, l, r, start=i == 0, stop=i == len(mms) - 1)
                        last.then_inc(*ev("pe_" + kind, name))

                    uk = [u[:, k, :] for k in range(KC)]

                    def in_tiles(names, free, first=False):
                        n, w = weights(("in",) + names)
                        for j, name in enumerate(names):
                            ps = bank("z", name, free[j])
                            for k in range(KC):
                                if first and j == 0:
                                    pe.wait_ge(*at("dve_u", ("p", k)))
                                last = nc.tensor.matmul(ps[:, 0:T], w[:, (j * KC + k) * P:(j * KC + k + 1) * P], uk[k],
                                                        start=k == 0, stop=k == KC - 1)
                            last.then_inc(*ev("pe_z", name))
                        block_end[n] = ("pe_z", names[-1])

                    def ada(a0, a1, through=True):
                        def turn(i):
                            turned[0] = i + 1
                            pe.wait_ge(*at("act_mod", i))
                            ps = bank("m", ("adaT", i), ("dve_mod", i))
                            for j in range(2):
                                last = nc.tensor.transpose(ps[:, 9 * j:9 * j + 9], rowb[0:9, i % 2, j * P:(j + 1) * P], ident[0:9, 0:9])
                            last.then_inc(*ev("pe_m", ("adaT", i)))
                        for i in range(a0, a1):
                            n, w = weights(("ada", i))
                            group("z", ("ada", i), ("act_mod", i), [(siluc[:, k, :], w[:, k * 256:(k + 1) * 256]) for k in range(KC)],
                                  lambda ps: ps[0:9, 0:256])
                            block_end[n] = ("pe_z", ("ada", i))
                            if turned[0] < i:
                                turn(i - 1)
                        if through:
                            turn(a1 - 1)

                    ada(0, 8)
                    in_tiles(("small", "kv0"), [("dve_s", "kr"), ("act_b", ("sq", 0))], first=True)
                    in_tiles(("kv1", "bq0"), [("act_b", ("sq", 1)), ("act_b", ("sq", 2))])
                    in_tiles(("bq1", "bq2"), [("act_b", ("sq", 3)), ("act_b", ("sq", 4))])
                    pe.wait_ge(*at("dve_s", "kr"))
                    group("m", "kr_swap", ("dve_b", "kr t2"), [(cs("swapB")[64:96, 64:96], krz[64:96, :])], lambda ps: ps[64:96, 0:T])
                    pe.wait_ge(*at("act_b", ("sq", 1)))
                    group("m", "rms_kv", ("act_b", "std kv"), [(ones, sq5[:, k, :]) for k in range(2)])
                    pe.wait_ge(*at("act_b", ("sq", 4)))
                    group("m", "rms_bq", ("act_b", "std bq"), [(ones, sq5[:, k, :]) for k in range(2, 5)])

                    n, w = weights(("uq",))
                    n2, w2 = weights(("uk",))
                    pe.wait_ge(*at("dve_b", ("bq", 2)))
                    for j in range(6):
                        src = [(w[:, (3 * j + k) * P:(3 * j + k + 1) * P] if 3 * j + k < 16 else
                                w2[:, 1024 + (3 * j + k - 16) * P:1024 + (3 * j + k - 15) * P], bqz[:, k, :]) for k in range(3)]
                        group("z", ("uq", j), ("dve_q", ("odd", j)) if j < 4 else ("act_q", ("qr", j - 4)), src)
                    block_end[n] = ("pe_z", ("uq", 5))
                    pe.wait_ge(*at("dve_b", ("ckv", 1)))
                    for t, (t0, tn) in enumerate(TOK):
                        ps = bank("m", ("ckvT", t), ("act_q", ("ckvtok", t)))
                        for c in range(2):
                            last = nc.tensor.transpose(ps[0:tn, c * P:(c + 1) * P], ckv[:, c, t0:t0 + tn], ident)
                        last.then_inc(*ev("pe_m", ("ckvT", t)))
                    for r in range(2):
                        pe.wait_ge(*at("act_q", ("qr", r)))
                        group("m", ("qr_swap", r), ("dve_q", ("t2", r)), [(cs("swapB"), qr[:, r, :])])
                    for j in range(4):
                        group("z", ("kn", j), ("dve_q", ("kodd", j)),
                              [(w2[:, c * 512 + j * P:c * 512 + (j + 1) * P], ckv[:, c, 0:SEQ]) for c in range(2)], lambda ps: ps[:, 0:SEQ])
                    block_end[n2] = ("pe_z", ("kn", 3))
                    pe.wait_ge(C.sem("in_wuv"), 16)
                    for t in range(2):
                        group("z", ("vt", t), ("act_q", ("vlat", t)), [(ckv[:, c, t * P:(t + 1) * P], wuv[:, c, :]) for c in range(2)],
                              lambda ps: ps[:, :])
                    n, w = weights(("ukT",))
                    pe.wait_ge(*at("dve_q", ("odd", 3)))
                    for c in range(2):
                        ps = bank("z", ("qa", c), ("dve_q", ("qabs", c)))
                        for h in range(BH):
                            last = nc.tensor.matmul(ps[:, h * NS:(h + 1) * NS], w[0:64, h * KVR + c * P:h * KVR + (c + 1) * P],
                                                    q96[0:64, h, SAMP], start=True, stop=True)
                        last.then_inc(*ev("pe_z", ("qa", c)))
                    block_end[n] = ("pe_z", ("qa", 1))

                    def prompt_scores(h):
                        if h == 0:
                            pe.wait_ge(*at("dve_q", "qpes"))
                            pe.wait_ge(*at("pool_k", "kpe all"))
                            pe.wait_ge(*at("dve_q", ("kodd", 3)))
                        for i in range(2):
                            group("m", ("ps", h, i), ("dve_pa", ("s", h, i)), [(q96[0:96, h, i * P:(i + 1) * P], k96[0:96, h, 0:(i + 1) * P])],
                                  lambda ps: ps[:, 0:(i + 1) * P])

                    def prompt_values(h):
                        for i in range(2):
                            pe.wait_ge(*at("dve_pa", ("norm", h, i)))
                            ps = bank("m", ("ppT", h, i), ("act_pa", ("ppT", h, i)))
                            for k in range(i + 1):
                                last = nc.tensor.transpose(ps[:, k * P:(k + 1) * P], pp[:, i, k * P:(k + 1) * P], ident)
                            last.then_inc(*ev("pe_m", ("ppT", h, i)))

                    def prompt_out(h):
                        if h == 0:
                            pe.wait_ge(*at("act_q", ("vlat", 1)))
                        o = 64 * (h % 2)
                        ps = bank("m", ("po", h), ("act_pa", ("yb", h)))
                        pe.wait_ge(*at("act_pa", ("ppT", h, 1)))
                        s = ppT[:, h % 2, :]
                        nc.tensor.matmul(ps[o:o + 64, 0:SEQ], vlat[:, 0, h * VD:(h + 1) * VD], s[:, 0:SEQ], start=True, stop=False)
                        nc.tensor.matmul(ps[o:o + 64, P:SEQ], vlat[:, 1, h * VD:(h + 1) * VD], s[:, SEQ:SEQ + P], start=False,
                                         stop=True).then_inc(*ev("pe_m", ("po", h)))

                    steps = []
                    for h in range(BH + 2):
                        steps.append((h,))
                    for i, (xx, j) in enumerate([(x_, j_) for x_ in ("ak", "aq", "av", "ao") for j_ in (0, 2)]):
                        fr = "dve_a" if xx == "aq" else "act_a"
                        in_tiles((f"{xx}{j}", f"{xx}{j + 1}"), [(fr, (xx, j)), (fr, (xx, j + 1))])
                        prompt_scores(i)
                        if i >= 1:
                            prompt_values(i - 1)
                        if i >= 2:
                            prompt_out(i - 2)
                    prompt_values(BH - 1)
                    prompt_out(BH - 2)
                    prompt_out(BH - 1)

                    def to_tokens(X, t):
                        t0, tn = TOK[t]
                        for s, src in (("k", km), ("v", vm)):
                            if t == 0:
                                pe.wait_ge(*at("dve_dk" if X == "d" and s == "k" else f"act_{X}", (X + s, 3)))
                            ps = bank("m", (X, s + "T", t), (f"act_{X}t" if s == "k" else f"dve_{X}t", (s, t)))
                            for h in range(H):
                                last = nc.tensor.transpose(ps[0:tn, h * P:(h + 1) * P], src[:, h, t0:t0 + tn], ident)
                            last.then_inc(*ev("pe_m", (X, s + "T", t)))

                    def scores(X, h):
                        if h == 0:
                            pe.wait_ge(*at("dve_a" if X == "a" else "dve_dk", (X + "q", 3)))
                        ps = bank("m", (X, "st", h), (f"dve_{X}w", ("w2", h)))
                        nc.tensor.matmul(ps[:, 0:256], km[:, h, 0:P], qm[:, h, 0:SEQ], start=True, stop=True)
                        nc.tensor.matmul(ps[:, 256:384], km[:, h, P:SEQ], qm[:, h, P:SEQ], start=True, stop=True)
                        nc.tensor.matmul(ps[0:NS, 384:448], km[:, h, SAMP], qm[:, h, SAMP], start=True,
                                         stop=True).then_inc(*ev("pe_m", (X, "st", h)))

                    def outputs(X, hp, width):
                        pe.wait_ge(*at(f"dve_{X}t", ("v", 2)))
                        if hp == 0:
                            pe.wait_ge(*at(f"dve_{X}w", "qz"))
                            pe.wait_ge(C.sem(f"in_state_{X}"), 16)
                        for t in range(3):
                            ps = bank("m", (X, "num", t, hp), (f"dve_{X}h", ("h", t, hp)))
                            for i in range(2):
                                h = 2 * hp + i
                                pe.wait_ge(*at(f"dve_{X}w", ("w2", h)))
                                w_, o = wb[:, h % 2, :], ps[0:TOK[t][1], i * width:(i + 1) * width]
                                if t == 0:
                                    mms = [(w_[:, 0:P], vtok[:, 0, h, 0:width])]
                                elif t == 1:
                                    mms = [(w_[:, P:256], vtok[:, 0, h, 0:width]), (w_[:, 256:384], vtok[:, 1, h, 0:width])]
                                else:
                                    mms = [(w_[0:NS, 384:448], vtok[0:NS, 2, h, 0:width])]
                                    mms += [(qz[:, b * 256 + h * NS:b * 256 + (h + 1) * NS], state[:, b, h, 0:width]) for b in range(NB)]
                                for k, (l, r) in enumerate(mms):
                                    last = nc.tensor.matmul(o, l, r, start=k == 0, stop=k == len(mms) - 1)
                            last.then_inc(*ev("pe_m", (X, "num", t, hp)))

                    def turn_heads(X, t):
                        t0, tn = TOK[t]
                        pe.wait_ge(*at(f"dve_{X}h", ("n", t, 3)))
                        ps = bank("m", (X, "hT", t), (f"dve_{X}y", t))
                        for h in range(H):
                            last = nc.tensor.transpose(ps[:, h * P:h * P + tn], hh[0:tn, t, h, :], ident[0:tn, 0:tn])
                        last.then_inc(*ev("pe_m", (X, "hT", t)))

                    def state_prompt(X, width):
                        for hp in range(2):
                            pe.wait_ge(*at(f"pool_{X}k", 1))
                            ps = bank("m", (X, "cp", hp), (f"act_{X}c", hp))
                            for i in range(2):
                                h = 2 * hp + i
                                for t in range(2):
                                    last = nc.tensor.matmul(ps[:, i * width:(i + 1) * width], ktok[:, t, h, :], vtok[:, t, h, 0:width],
                                                            start=t == 0, stop=t == 1)
                            last.then_inc(*ev("pe_m", (X, "cp", hp)))

                    def state_sample(X, b, width):
                        pe.wait_ge(*at(f"pool_{X}m", b))
                        for hp in range(2):
                            ps = bank("m", (X, "cs", b, hp), (f"dve_{X}c", (b, 2 * hp + 1)))
                            for i in range(2):
                                h = 2 * hp + i
                                last = nc.tensor.matmul(ps[:, i * width:(i + 1) * width], kmb[0:NS, b % 2, h * P:(h + 1) * P],
                                                        vtok[0:NS, 2, h, 0:width], start=True, stop=True)
                            last.then_inc(*ev("pe_m", (X, "cs", b, hp)))

                    def gate_columns():
                        pe.wait_ge(*at("dve_g", "r4"))
                        pe.wait_ge(*at("pool_z", "r4"))
                        for t, (t0, tn) in enumerate(TOK):
                            ps = bank("m", ("g4T", t), ("act_g", ("exp", t)))
                            nc.tensor.transpose(ps[0:tn, 0:100], r4[0:100, t0:t0 + tn], ident[0:100, 0:100]).then_inc(*ev("pe_m", ("g4T", t)))
                        ps = bank("m", "wint", ("act_g", "wint"))
                        for h in range(H):
                            last = nc.tensor.matmul(ps[:, h * NS:(h + 1) * NS], ident[0:4, h:h + 1].to_broadcast([4, P]), growk[0:4, 1, SAMP],
                                                    start=True, stop=True)
                        last.then_inc(*ev("pe_m", "wint"))

                    def gate_row(h):
                        group("m", ("rb", h), ("dve_aw", ("e2", h)), [(ident[0:4, h:h + 1].to_broadcast([4, P]), growk[0:4, 0, :])])

                    def conv_tiles(j):
                        in_tiles((f"cg{j}", f"ca{j}"), [("act_c", ("sg", j)), ("dve_c", ("glu2", j))])

                    gate_columns()
                    conv_tiles(0)
                    for t in range(3):
                        to_tokens("a", t)
                    gate_row(0)
                    scores("a", 0)
                    gate_row(1)
                    scores("a", 1)
                    conv_tiles(1)
                    outputs("a", 0, W)
                    gate_row(2)
                    scores("a", 2)
                    gate_row(3)
                    scores("a", 3)
                    conv_tiles(2)
                    outputs("a", 1, W)
                    state_prompt("a", W)
                    conv_tiles(3)
                    for t in range(3):
                        turn_heads("a", t)
                    for b in range(NB):
                        state_sample("a", b, W)

                    def swap(x_, h):
                        pe.wait_ge(*at("act_dz", (x_, h)))
                        group("m", ("sw", x_, h), ("dve_dk", ("t2", x_, h)), [(cs("swapD"), tmp[:, h % 2, :])])
                    for x_ in ("dk", "dq", "dv", "dg"):
                        for j in (0, 2):
                            s = "act_dz" if x_ in ("dk", "dq") else "act_d"
                            in_tiles((f"{x_}{j}", f"{x_}{j + 1}"), [(s, (x_, j)), (s, (x_, j + 1))])
                            if s == "act_dz":
                                swap(x_, j)
                                swap(x_, j + 1)

                    def channel_sum(name, src, k, ready, freed_by):
                        pe.wait_ge(*at(*ready))
                        group("m", name, freed_by, [(ones, src[:, j, :]) for j in range(k)])

                    def gate(n, i):
                        in_tiles((f"g{n}_{i}", f"g{n}_{i + 1}"), [("act_gt", (n, i)), ("act_gt", (n, i + 1))])

                    def branch(n, half):
                        k, w = weights(("branch", n, half))
                        pe.wait_ge(*at(*{0: ("dve_ay", 2), 2: ("act_cy", 3), 3: ("dve_dy", 2), 1: ("act_s", "ys")}[n]))
                        if n == 1:
                            pe.wait_ge(*at("act_pa", ("yb", BH - 1)))
                        for i in range(4):
                            group("z", ("br", n, half + i), ("dve_br", (n, half + i)),
                                  [(w[:, (i * 4 + c) * P:(i * 4 + c + 1) * P], y[:, n, c, :]) for c in range(4)])
                        block_end[k] = ("pe_z", ("br", n, half + 3))

                    def gated(n, half):
                        gate(n, half)
                        gate(n, half + 2)
                        branch(n, half)

                    def slot(b):
                        for kind, *which in SLOTS[b]:
                            if kind == "gate":
                                gate(*which)
                            elif kind == "branch":
                                branch(*which)
                            else:
                                ada(which[0], which[0] + 1, through=False)

                    def sample_scores(b):
                        r = b % 2
                        pe.wait_ge(C.sem(f"in_cache{r}"), 16 * 2 * NPG * (b // 2 + 1))
                        for g in range(2):
                            group("m", ("ss", b, g), ("act_s", ("e", b, g)),
                                  [(qabs[:, 0, b, :], cache[:, r, 4 * g:4 * g + 4, 0:P]),
                                   (qabs[:, 1, b, :], cache[:, r, 4 * g:4 * g + 4, P:2 * P]),
                                   (qpes[64:96, b, :], ropeT[64:96, r, 4 * g:4 * g + 4, :])], lambda ps: ps[0:NS, :])
                        group("m", ("ss", b, 2), ("dve_s2", ("new", b)),
                              [(qabs[:, 0, b, :], ckv[:, 0, SAMP]), (qabs[:, 1, b, :], ckv[:, 1, SAMP]), (qpes[64:96, b, :], kpe[64:96, SAMP])],
                              lambda ps: ps[0:NS, 0:NS])

                    def sample_turn(b):
                        pe.wait_ge(*at("act_s", ("e", b, 2)))
                        ps = bank("m", ("sT", b), ("act_s", ("pT", b)))
                        for k in range(NPG):
                            last = nc.tensor.transpose(ps[:, k * NS:(k + 1) * NS], pb[0:NS, b % 2, k * P:(k + 1) * P], ident[0:NS, 0:NS])
                        last.then_inc(*ev("pe_m", ("sT", b)))
                        ps = bank("m", ("snT", b), ("dve_s2", ("pnT", b)))
                        nc.tensor.transpose(ps[0:NS, 0:NS], pb[0:NS, b % 2, PAST:PAST + NS], ident[0:NS, 0:NS]).then_inc(*ev("pe_m", ("snT", b)))

                    def sample_values(b):
                        r = b % 2
                        pe.wait_ge(*at("act_s", ("pT", b)))
                        pe.wait_ge(*at("dve_s2", ("pnT", b)))
                        group("m", ("so", b), ("dve_s2", ("o", b)),
                              [(pT[:, r, k * NS:(k + 1) * NS], cache[:, r, k, 2 * P:4 * P]) for k in range(NPG)]
                              + [(pT[0:NS, r, 512:576], ckvtok[0:NS, 2, :])], lambda ps: ps[0:NS, 0:KVR])

                    def sample_back(b):
                        pe.wait_ge(*at("dve_s2", ("o", b)))
                        ps = bank("m", ("soT", b), ("act_s", ("oT", b)))
                        for c in range(2):
                            last = nc.tensor.transpose(ps[:, c * NS:(c + 1) * NS], olat[0:NS, b % 2, c * P:(c + 1) * P], ident[0:NS, 0:NS])
                        last.then_inc(*ev("pe_m", ("soT", b)))

                    def sample_out():
                        pe.wait_ge(*at("act_s", ("oT", NB - 1)))
                        ps = bank("m", "ys", ("act_s", "ys"))
                        for h in range(BH):
                            o = 64 * (h % 2)
                            for c in range(2):
                                last = nc.tensor.matmul(ps[o:o + 64, (h // 2) * NS:(h // 2 + 1) * NS], wuv[:, c, h * VD:(h + 1) * VD],
                                                        olatT[:, c, h, :], start=c == 0, stop=c == 1)
                        last.then_inc(*ev("pe_m", "ys"))

                    gated(0, 0)
                    for t in range(3):
                        to_tokens("d", t)
                    scores("d", 0)
                    scores("d", 1)
                    pe.wait_ge(*at("pool_c", ("sum", CW - 1)))
                    channel_sum("conv sum", y[:, 2], 4, ("dve_c", ("tap", 3, CW - 1)), ("dve_c", ("mu", 3)))
                    gated(0, 4)
                    outputs("d", 0, P)
                    scores("d", 2)
                    scores("d", 3)
                    channel_sum("conv var", sqc, 4, ("act_cy", ("sq", 3)), ("act_cy", "std"))
                    outputs("d", 1, P)
                    state_prompt("d", P)
                    gated(2, 0)
                    for t in range(3):
                        turn_heads("d", t)
                    for b in range(NB):
                        state_sample("d", b, P)
                    gated(2, 4)
                    for b in range(NB):
                        if b >= 2:
                            sample_back(b - 2)
                        if b >= 1:
                            sample_turn(b - 1)
                        sample_scores(b)
                        if b >= 1:
                            sample_values(b - 1)
                        slot(b)
                    sample_back(NB - 2)
                    sample_turn(NB - 1)
                    sample_values(NB - 1)
                    slot(NB)
                    sample_back(NB - 1)
                    sample_out()
                    branch(1, 0)
                    branch(1, 4)

                    for i in range(4):
                        n, w = weights(("out", i))
                        pe.wait_ge(*at("dve_br", (1, 7)))
                        for j in range(2):
                            d = 2 * i + j
                            group("z", ("wo", d), ("dve_r", ("g", 1, d)), [(w[:, (j * KC + k) * P:(j * KC + k + 1) * P], gsum[:, k, :]) for k in range(KC)])
                        block_end[n] = ("pe_z", ("wo", 2 * i + 1))

                    def norm_sums(which, filler1, filler2):
                        pe.wait_ge(*at("dve_r", ("r", which, KC - 1)))
                        group("m", ("mean", which), ("dve_r", ("mu", which, KC - 1)), [(ones, u[:, k, :]) for k in range(KC)])
                        if filler1:
                            ada(*filler1)
                        pe.wait_ge(*at("act_n", ("sq", which, KC - 1)))
                        group("m", ("var", which), ("act_n", ("std", which)), [(ones, acc[:, k, :]) for k in range(KC)])
                        if filler2:
                            ada(*filler2)

                    norm_sums(1, (18, 20), (20, 24))

                    for j in range(FT):
                        n, w = weights(("ffn", j))
                        for i in range(2):
                            name = (("f1", "f3")[i], j)
                            ps = bank("z", name, ("act_f", j) if i == 0 else ("dve_f", j))
                            for k in range(KC):
                                if j == 0 and i == 0:
                                    pe.wait_ge(*at("dve_u2", ("p", k)))
                                last = nc.tensor.matmul(ps[:, 0:T], w[:, (i * KC + k) * P:(i * KC + k + 1) * P], acc[:, k, :], start=k == 0, stop=k == KC - 1)
                            last.then_inc(*ev("pe_z", name))
                        block_end[n] = ("pe_z", ("f3", j))
                    pe.wait_ge(*at("dve_f", FT - 1))
                    n, w = None, None
                    for d in range(KC):
                        ps = bank("z", ("fo", d), ("dve_r", ("g", 2, d)))
                        for j in range(FT):
                            i = d * FT + j
                            if i % 16 == 0:
                                n, w = weights(("ffn2", i // 16))
                            last = nc.tensor.matmul(ps[:, 0:T], w[:, (i % 16) * P:(i % 16 + 1) * P], hid[:, j, :], start=j == 0, stop=j == FT - 1)
                            if j == FT - 1:
                                last.then_inc(*ev("pe_z", ("fo", d)))
                            elif i % 16 == 15:
                                last.then_inc(*ev("pe_z", ("ffn2", i // 16)))
                            if i % 16 == 15:
                                block_end[n] = ("pe_z", ("fo", d) if j == FT - 1 else ("ffn2", i // 16))
                    norm_sums(2, None, None)
                    assert bi[0] == NBLK

                @block.sync
                def _(sp):
                    lay = bass.ds(layer, 1)

                    def dram(name, *rest):
                        return a[name][(lay,) + tuple(slice(None) for _ in range(len(a[name].shape) - 1))]

                    def of(ap, names):
                        return ap.rearrange(f"l {names} -> (l {names.split()[0]}) " + " ".join(names.split()[1:]))

                    sp.dma_start(smallw[:], of(dram("small"), "p f")).then_inc(C.sem("in_small"), 16)

                    def load_block(n):
                        if n >= RING:
                            sp.wait_ge(*at(*block_end[n - RING]))
                        src = a["wpack"][lay, n:n + 1, :, :].rearrange("l n p f -> (l n p) f")
                        sp.dma_start(ring[:, n % RING, :], src).then_inc(C.sem(f"w_landed{n % RING}"), 16)

                    def load_pages(b):
                        r = b % 2
                        if b >= 2:
                            sp.wait_ge(*at("pe_m", ("so", b - 2)))
                        else:
                            sp.wait_ge(*at("dve_dc", (NB - 1, 3)))
                            sp.wait_ge(*at("dve_dy", 2))
                            sp.wait_ge(C.sem("out_state_d"), 16 * 2)
                        for g in range(NPG):
                            pg = sp.value_load(pages[0:1, b * NPG + g:b * NPG + g + 1], min_val=0, max_val=POOL - 1)
                            sp.dma_start(cache[:, r, g, :], a["cache"][lay, bass.ds(pg, 1), :, :].rearrange("l n p f -> (l n p) f")
                                         ).then_inc(C.sem(f"in_cache{r}"), 16)
                            sp.dma_start(ropeT[64:96, r, g, :], a["rope"][lay, bass.ds(pg, 1), :, :].rearrange("l n p f -> (l n p) f")
                                         ).then_inc(C.sem(f"in_cache{r}"), 16)

                    first_gate = BLOCKS.index(("in", "g0_0", "g0_1"))
                    for n in range(NBLK):
                        load_block(n)
                        if n == 3:
                            sp.dma_start(m0[:], of(dram("m0"), "h b")).then_inc(C.sem("in_m0"), 16)
                            sp.dma_start(wuv[:], of(dram("wuv"), "p c f")).then_inc(C.sem("in_wuv"), 16)
                        if BLOCKS[n] == ("in", "ak0", "ak1"):
                            sp.dma_start(state[:], of(dram("stateA"), "p b h d")).then_inc(C.sem("in_state_a"), 16)
                        if BLOCKS[n] == ("in", "ao2", "ao3"):
                            sp.wait_ge(*at("pe_m", ("po", BH - 1)))
                            sp.dma_start(ucs[:, :, :, 0:CW - 1], of(dram("hist"), "p j b t")).then_inc(C.sem("in_hist"), 16)
                            sp.wait_ge(*at("dve_b", ("ckv", 1)))
                            sp.wait_ge(*at("dve_b", "kpe"))
                            sp.dma_start(of(dram("o_rows_c"), "p c t"), ckv[:]).then_inc(C.sem("out_rows"), 16)
                            sp.dma_start(of(dram("o_rows_k"), "p t"), kpe[64:96, :]).then_inc(C.sem("out_rows"), 16)
                        if n == BLOCKS.index(("in", "dg2", "dg3")):
                            sp.wait_ge(*at("act_ac", 1))
                            sp.dma_start(of(dram("o_cn_p"), "p h d"), cnp).then_inc(C.sem("out_state_a"), 16)
                            sp.wait_ge(*at("dve_ac", (NB - 1, 3)))
                            sp.dma_start(of(dram("o_cn_s"), "p b h d"), state[:]).then_inc(C.sem("out_state_a"), 16)
                            sp.wait_ge(*at("dve_g", "mout"))
                            sp.dma_start(of(dram("o_m"), "h b"), mout[:]).then_inc(C.sem("out_m"), 16)
                            sp.wait_ge(*at("dve_c", ("glu2", 3)))
                            sp.dma_start(of(dram("o_conv_p"), "p j t"), ucp[:, :, SEQ:SEQ + CW - 1]).then_inc(C.sem("out_conv"), 16)
                            sp.dma_start(of(dram("o_conv_s"), "p j b t"), ucs[:, :, :, TS:TS + CW - 1]).then_inc(C.sem("out_conv"), 16)
                            sp.wait_ge(C.sem("out_state_a"), 32)
                            sp.dma_start(state[:, :, :, 0:P], of(dram("stateD"), "p b h d")).then_inc(C.sem("in_state_d"), 16)
                        if BLOCKS[n] == ("branch", 2, 4):
                            sp.wait_ge(*at("act_dc", 1))
                            sp.dma_start(of(dram("o_ret_p"), "p h d"), cnp[:, :, 0:P]).then_inc(C.sem("out_state_d"), 16)
                            sp.wait_ge(*at("dve_dc", (NB - 1, 3)))
                            sp.dma_start(of(dram("o_ret_s"), "p b h d"), state[:, :, :, 0:P]).then_inc(C.sem("out_state_d"), 16)
                            load_pages(0)
                        if n == SLOT_START[0] + 1:
                            load_pages(1)
                        for b in range(2, NB):
                            if n == SLOT_START[b - 1] + RING - 1:
                                load_pages(b)
                    sp.wait_ge(*at("act_n", ("x", 2, KC - 1)))
                    sp.dma_start(a["o_y"], x[:]).then_inc(C.sem("out_y"), 16)
                    sp.wait_ge(C.sem("out_y"), 16)
                    sp.wait_ge(C.sem("out_rows"), 32)
                    sp.wait_ge(C.sem("out_m"), 16)
                    sp.wait_ge(C.sem("out_conv"), 32)
                    sp.wait_ge(C.sem("out_state_a"), 32)
                    sp.wait_ge(C.sem("out_state_d"), 32)

                @block.scalar
                def _(act):
                    act.wait_ge(C.sem("in_small"), 16)

                    def go(sem, label, out, in_, func, **kw):
                        in_turn(act, "act")
                        return nc.scalar.activation(out, in_, func, **kw).then_inc(*ev(sem, label))

                    def z(name):
                        act.wait_ge(*at("pe_z", name))
                        return banks[name]

                    def m(name):
                        act.wait_ge(*at("pe_m", name))
                        return banks[name]

                    def ada(a0, a1):
                        for i in range(a0, a1):
                            ps = z(("ada", i))
                            if i >= 2:
                                act.wait_ge(*at("pe_m", ("adaT", i - 2)))
                            go("act_mod", i, rowb[0:9, i % 2, :], ps[0:9, 0:256], ACT.Copy)

                    ada(0, 8)
                    for i, name in enumerate(("kv0", "kv1", "bq0", "bq1", "bq2")):
                        ps = z(name)
                        go("act_b", ("z", i), ckv[:, i, :] if i < 2 else bqz[:, i - 2, :], ps[:, 0:T], ACT.Identity, bias=sw(name))
                        go("act_b", ("sq", i), sq5[:, i, :], ps[:, 0:T], ACT.Square, bias=sw(name))
                    go("act_b", "std kv", std[:], m("rms_kv")[:, 0:T], ACT.Sqrt, bias=cs("eps")[:, 1:2], scale=1.0 / KVR)
                    go("act_b", "std bq", tmp[:, 0, :], m("rms_bq")[:, 0:T], ACT.Sqrt, bias=cs("eps")[:, 1:2], scale=1.0 / QR)
                    for r in range(2):
                        go("act_q", ("qr", r), qr[:, r, :], z(("uq", 4 + r))[:, 0:T], ACT.Copy)
                    for t, (t0, tn) in enumerate(TOK):
                        go("act_q", ("ckvtok", t), ckvtok[0:tn, t, :], m(("ckvT", t))[0:tn, 0:KVR], ACT.Copy)
                    for t in range(2):
                        go("act_q", ("vlat", t), vlat[:, t, :], z(("vt", t))[:, :], ACT.Copy)
                    act.wait_ge(*at("dve_g", "abs"))
                    go("act_g", "e", grow[:, 2, :], grow[:, 1, :], ACT.Exp, scale=-1.0)
                    act.wait_ge(*at("act_g", "e"))
                    go("act_g", "ln", grow[:, 3, :], grow[:, 2, :], ACT.Ln, bias=cs("eps")[0:4, 2:3])

                    def prompt_exp(h):
                        for i in range(2):
                            act.wait_ge(*at("dve_pa", ("nm", h, i)))
                            go("act_pa", ("e", h, i), pp[:, i, 0:(i + 1) * P], pp[:, i, 0:(i + 1) * P], ACT.Exp,
                               bias=stats[:, 4 + i:5 + i], scale=BSCALE, accum_out=stats[:, 8 + i:9 + i])

                    def prompt_turned(h):
                        if h >= 2:
                            act.wait_ge(*at("pe_m", ("po", h - 2)))
                        go("act_pa", ("ppT", h, 0), ppT[:, h % 2, 0:P], m(("ppT", h, 0))[:, 0:P], ACT.Copy)
                        go("act_pa", ("ppT", h, 1), ppT[:, h % 2, P:3 * P], m(("ppT", h, 1))[:, 0:2 * P], ACT.Copy)

                    def prompt_y(h):
                        o = 64 * (h % 2)
                        go("act_pa", ("yb", h), y[o:o + 64, 1, h // 2, 0:SEQ], m(("po", h))[o:o + 64, 0:SEQ], ACT.Copy)

                    act.wait_ge(*at("pe_z", ("uq", 5)))
                    act.wait_ge(*at("dve_q", ("t1", 1)))
                    for i, (xx, j) in enumerate([(x_, j_) for x_ in ("ak", "aq", "av", "ao") for j_ in (0, 2)]):
                        for h in (j, j + 1):
                            if xx == "ak" or xx == "av":
                                dst = (km if xx == "ak" else vm)[:, h, :]
                                go("act_a", (xx, h), dst, z(f"{xx}{h}")[:, 0:T], ACT.Identity, bias=sw(f"{xx}{h}"))
                            elif xx == "ao":
                                go("act_a", (xx, h), y[:, 0, h, :], z(f"{xx}{h}")[:, 0:T], ACT.Sigmoid, bias=sw(f"{xx}{h}"))
                        prompt_exp(i)
                        if i >= 1:
                            prompt_turned(i - 1)
                        if i >= 2:
                            prompt_y(i - 2)
                    prompt_turned(BH - 1)
                    prompt_y(BH - 2)
                    prompt_y(BH - 1)

                    for t, (t0, tn) in enumerate(TOK):
                        ps = m(("g4T", t))
                        go("act_g", ("col", t), col4[0:tn, t, 0:32], ps[0:tn, 0:32], ACT.Copy)
                        go("act_g", ("exp", t), col4[0:tn, t, 32:100], ps[0:tn, 32:100], ACT.Exp)
                    go("act_g", "wint", wint[:].rearrange("p h t -> p (h t)"), m("wint")[:, 0:H * NS], ACT.Exp)

                    def conv_gate(j):
                        if j >= 4:
                            act.wait_ge(*at("dve_c", ("glu2", j - 4)))
                        go("act_c", ("sg", j), gt[:, j, :], z(f"cg{j}")[:, 0:T], ACT.Sigmoid, bias=sw(f"cg{j}"))

                    def tokens(X, t):
                        tn = TOK[t][1]
                        go(f"act_{X}t", ("k", t), ktok[0:tn, t].rearrange("p h d -> p (h d)"), m((X, "kT", t))[0:tn, :], ACT.Copy)

                    def decay(h):
                        act.wait_ge(*at("dve_aw", ("e2", h)))
                        go("act_aw", ("e1", h), eb[:, h % 2, 0:384], eb[:, h % 2, 0:384], ACT.Exp)
                        go("act_aw", ("e2", h), eb[0:NS, h % 2, 384:448], eb[0:NS, h % 2, 384:448], ACT.Exp)

                    def head_std(X, t):
                        tn = TOK[t][1]
                        act.wait_ge(*at(f"dve_{X}h", ("mv", t, 3)))
                        go(f"act_{X}h", t, stats[0:tn, 64 + 4 * t:68 + 4 * t], stats[0:tn, 32 + 8 * t:40 + 8 * t].rearrange("p (h s) -> p h s", h=H)[:, :, 1],
                           ACT.Sqrt, bias=cs("eps")[0:tn, 0:1])

                    def prompt_state(X, width):
                        for hp in range(2):
                            if hp == 0:
                                act.wait_ge(*at("pe_m", (X, "vT", 2)))
                            go(f"act_{X}c", hp, cnp[:, 2 * hp:2 * hp + 2, 0:width], m((X, "cp", hp))[:, 0:2 * width].rearrange("p (h d) -> p h d", h=2), ACT.Copy)

                    conv_gate(0)
                    for t in range(3):
                        tokens("a", t)
                    decay(0)
                    decay(1)
                    conv_gate(1)
                    decay(2)
                    decay(3)
                    conv_gate(2)
                    prompt_state("a", W)
                    conv_gate(3)
                    for t in range(3):
                        head_std("a", t)

                    for x_ in ("dk", "dq", "dv", "dg"):
                        for h in range(H):
                            if x_ in ("dk", "dq"):
                                i = h + (4 if x_ == "dq" else 0)
                                if i >= 2:
                                    px, ph = ("dk", i - 2) if i < 6 else ("dq", i - 6)
                                    act.wait_ge(*at("dve_dk", ("t2", px, ph)))
                                    act.wait_ge(*at("pe_m", ("sw", px, ph)))
                                go("act_dz", (x_, h), tmp[:, h % 2, :], z(f"{x_}{h}")[:, 0:T], ACT.Identity, bias=sw(f"{x_}{h}"))
                            elif x_ == "dv":
                                if h == 0:
                                    act.wait_ge(C.sem("out_state_a"), 16 * 2)
                                go("act_d", (x_, h), vm[:, h, :], z(f"{x_}{h}")[:, 0:T], ACT.Identity, bias=sw(f"{x_}{h}"))
                            else:
                                go("act_d", (x_, h), y[:, 3, h, :], z(f"{x_}{h}")[:, 0:T], ACT.Silu, bias=sw(f"{x_}{h}"))

                    gate_seq = [(n, d) for n in GATE_ORDER[:3] for d in range(8)]

                    def gates(n, half, count=4):
                        for i in range(half, half + count):
                            if n == GATE_ORDER[3]:
                                dst = acc[:, i, :]
                            else:
                                k = gate_seq.index((n, i))
                                dst = gt[:, k % 4, :]
                                if k >= 4:
                                    act.wait_ge(*at("dve_br", gate_seq[k - 4]))
                                else:
                                    act.wait_ge(*at("dve_c", ("glu2", k)))
                            go("act_gt", (n, i), dst, z(f"g{n}_{i}")[:, 0:T], ACT.Sigmoid, bias=sw(f"g{n}_{i}"))

                    gates(0, 0)
                    for t in range(3):
                        if t == 0:
                            act.wait_ge(*at("pe_m", ("a", "cp", 1)))
                        tokens("d", t)
                    gates(0, 4)
                    for j in range(4):
                        if j == 0:
                            act.wait_ge(C.sem("out_conv"), 32)
                        act.wait_ge(*at("dve_c", ("mu", j)))
                        go("act_cy", ("sq", j), sqc[:, j, :], y[:, 2, j, :], ACT.Square)
                    go("act_cy", "std", std[:], m("conv var")[:, 0:T], ACT.Sqrt, bias=cs("eps")[:, 0:1], scale=1.0 / CCH)
                    for j in range(4):
                        act.wait_ge(*at("dve_c", ("xn", j)))
                        go("act_cy", j, y[:, 2, j, :], y[:, 2, j, :], ACT.Silu, bias=sw("clb", j), scale=sw("clg", j))
                    prompt_state("d", P)
                    gates(2, 0)
                    for t in range(3):
                        head_std("d", t)
                    gates(2, 4)

                    def sample_exp(b):
                        r = b % 2
                        act.wait_ge(*at("dve_s2", ("nm", b)))
                        for g in range(2):
                            if g == 0 and b >= 2:
                                act.wait_ge(*at("pe_m", ("sT", b - 2)))
                            go("act_s", ("e", b, g), pb[0:NS, r, g * 512:(g + 1) * 512], m(("ss", b, g))[0:NS, :], ACT.Exp,
                               bias=stats[0:NS, 100 + r:101 + r], scale=BSCALE, accum_out=stats[0:NS, 104 + 4 * r + g:105 + 4 * r + g])
                        go("act_s", ("e", b, 2), pb[0:NS, r, PAST:PAST + NS], pb[0:NS, r, PAST:PAST + NS], ACT.Exp,
                           bias=stats[0:NS, 100 + r:101 + r], scale=BSCALE, accum_out=stats[0:NS, 106 + 4 * r:107 + 4 * r])

                    def sample_turned(b):
                        if b >= 2:
                            act.wait_ge(*at("pe_m", ("so", b - 2)))
                        go("act_s", ("pT", b), pT[:, b % 2, 0:512], m(("sT", b))[:, :], ACT.Copy)

                    def sample_back(b):
                        ps = m(("soT", b))
                        go("act_s", ("oT", b), olatT[:, :, :, b * TS:(b + 1) * TS], ps[:, 0:2 * NS].rearrange("p (c h t) -> p c h t", c=2, h=BH), ACT.Copy)

                    def slot(b):
                        for kind, *which in SLOTS[b]:
                            if kind == "gate":
                                gates(*which, count=2)
                            elif kind == "ada":
                                ada(which[0], which[0] + 1)

                    for b in range(NB):
                        if b >= 2:
                            sample_back(b - 2)
                        if b >= 1:
                            sample_turned(b - 1)
                        sample_exp(b)
                        slot(b)
                    sample_back(NB - 2)
                    sample_turned(NB - 1)
                    slot(NB)
                    sample_back(NB - 1)
                    go("act_s", "ys", y[:, 1, :, SAMP], m("ys")[:, 0:4 * NS].rearrange("p (j t) -> p j t", j=4), ACT.Copy)

                    def norm(which, filler1, filler2):
                        if filler1:
                            ada(*filler1)
                        for k in range(KC):
                            act.wait_ge(*at("dve_r", ("mu", which, k)))
                            go("act_n", ("sq", which, k), acc[:, k, :], u[:, k, :], ACT.Square)
                        go("act_n", ("std", which), std[:], m(("var", which))[:, 0:T], ACT.Sqrt, bias=cs("eps")[:, 0:1], scale=1.0 / D_MODEL)
                        for k in range(KC):
                            act.wait_ge(*at("dve_r", ("xn", which, k)))
                            go("act_n", ("x", which, k), x[:, k, :], u[:, k, :], ACT.Identity, bias=sw(f"ln{which}b", k))
                        if filler2:
                            ada(*filler2)

                    norm(1, (18, 20), (20, 24))
                    for j in range(FT):
                        if j >= 2:
                            act.wait_ge(*at("dve_f", j - 2))
                        go("act_f", j, gt[:, j % 2, :], z(("f1", j))[:, 0:T], ACT.Silu)
                    norm(2, None, None)

                @block.vector
                def _(dve):
                    dve.wait_ge(C.sem("in_small"), 16)

                    def V():
                        in_turn(dve, "dve")
                        return nc.vector

                    def z(name):
                        dve.wait_ge(*at("pe_z", name))
                        return banks[name]

                    def m(name):
                        dve.wait_ge(*at("pe_m", name))
                        return banks[name]

                    def bc(ap, shape):
                        return ap.to_broadcast(shape)

                    def ada(a0, a1):
                        for i in range(a0, a1):
                            ps = m(("adaT", i))
                            V().tensor_tensor(mod[:, 2 * i:2 * i + 2, :], ps[:, 0:18].rearrange("p (j c) -> p j c", j=2),
                                            smallw[:, 2 * i:2 * i + 2].rearrange("p (j c) -> p j c", c=1).to_broadcast([P, 2, 9]),
                                            ALU.add).then_inc(*ev("dve_mod", i))

                    def modulate(sem, dst, sh, sc):
                        V().tensor_scalar_add(mod[:, sc:sc + 8, :], mod[:, sc:sc + 8, :], 1.0).then_inc(*ev(sem, "sc"))
                        dve.wait_ge(*at(sem, "sc"))

                        def per_batch(o):
                            return mod[:, o:o + 8, 1:9].rearrange("p k (b t) -> p k b t", t=1).to_broadcast([P, KC, NB, TS])
                        ds = dst[:, :, SAMP].rearrange("p k (b t) -> p k b t", b=NB)
                        V().tensor_tensor(ds, x[:, :, SAMP].rearrange("p k (b t) -> p k b t", b=NB), per_batch(sc), ALU.mult).then_inc(*ev(sem, "s1"))
                        dve.wait_ge(*at(sem, "s1"))
                        V().tensor_tensor(ds, ds, per_batch(sh), ALU.add).then_inc(*ev(sem, "s2"))
                        for k in range(KC):
                            V().tensor_scalar(dst[:, k, 0:SEQ], x[:, k, 0:SEQ], mod[:, sc + k, 0:1], mod[:, sh + k, 0:1], ALU.mult,
                                            ALU.add).then_inc(*ev(sem, ("p", k)))

                    ada(0, 8)
                    dve.wait_ge(*at("dve_mod", 7))
                    modulate("dve_u", u, 0, 8)

                    ps = z("small")
                    V().tensor_scalar_add(grow[:, 0, :], ps[0:4, 0:T], sw("small")[0:4]).then_inc(*ev("dve_s", "i"))
                    V().tensor_scalar_add(grow[:, 5, :], ps[32:36, 0:T], sw("small")[32:36]).then_inc(*ev("dve_s", "f"))
                    V().tensor_scalar_add(krz[64:96, :], ps[64:96, 0:T], sw("small")[64:96]).then_inc(*ev("dve_s", "kr"))
                    dve.wait_ge(*at("dve_s", "f"))
                    V().scalar_tensor_tensor(out=grow[:, 1, :], in0=grow[:, 5, :], scalar=-1.0, in1=grow[:, 5, :], op0=ALU.mult, op1=ALU.max).then_inc(*ev("dve_g", "abs"))
                    dve.wait_ge(*at("dve_s", "kr"))
                    V().tensor_tensor(kpe[64:96, :], krz[64:96, :], cs("cosB")[64:96, :], ALU.mult).then_inc(*ev("dve_b", "kr t1"))
                    V().tensor_tensor(krz[64:96, :], m("kr_swap")[64:96, 0:T], cs("sinB")[64:96, :], ALU.mult).then_inc(*ev("dve_b", "kr t2"))
                    dve.wait_ge(*at("dve_b", "kr t2"))
                    V().tensor_tensor(kpe[64:96, :], kpe[64:96, :], krz[64:96, :], ALU.add).then_inc(*ev("dve_b", "kpe"))
                    dve.wait_ge(*at("act_b", "std kv"))
                    V().reciprocal(std[:], std[:]).then_inc(*ev("dve_b", "r kv"))
                    dve.wait_ge(*at("dve_b", "r kv"))
                    for c in range(2):
                        V().scalar_tensor_tensor(out=ckv[:, c, :], in0=ckv[:, c, :], scalar=sw("kvn", c), in1=std[:], op0=ALU.mult,
                                               op1=ALU.mult).then_inc(*ev("dve_b", ("ckv", c)))
                    dve.wait_ge(*at("act_b", "std bq"))
                    V().reciprocal(tmp[:, 1, :], tmp[:, 0, :]).then_inc(*ev("dve_b", "r bq"))
                    dve.wait_ge(*at("dve_b", "r bq"))
                    for c in range(3):
                        V().scalar_tensor_tensor(out=bqz[:, c, :], in0=bqz[:, c, :], scalar=sw("qn", c), in1=tmp[:, 1, :], op0=ALU.mult,
                                               op1=ALU.mult).then_inc(*ev("dve_b", ("bq", c)))
                    for j in range(4):
                        ps = z(("uq", j))
                        V().tensor_copy(q96[0:64, 2 * j, :], ps[0:64, 0:T]).then_inc(*ev("dve_q", ("even", j)))
                        V().tensor_copy(q96[0:64, 2 * j + 1, :], ps[64:128, 0:T]).then_inc(*ev("dve_q", ("odd", j)))
                    for r in range(2):
                        dve.wait_ge(*at("act_q", ("qr", r)))
                        ps = m(("qr_swap", r))
                        V().tensor_tensor(tmp[:, 1, :], ps[:, 0:T], cs("sinB"), ALU.mult).then_inc(*ev("dve_q", ("t2", r)))
                        V().tensor_tensor(tmp[:, 0, :], qr[:, r, :], cs("cosB"), ALU.mult).then_inc(*ev("dve_q", ("t1", r)))
                        dve.wait_ge(*at("dve_q", ("t1", r)))
                        for i in range(4):
                            V().tensor_tensor(q96[64:96, 4 * r + i, :], tmp[32 * i:32 * i + 32, 0, :], tmp[32 * i:32 * i + 32, 1, :],
                                            ALU.add).then_inc(*ev("dve_q", ("rot", r, i)))
                    for j in range(4):
                        ps = z(("kn", j))
                        V().tensor_copy(k96[0:64, 2 * j, :], ps[0:64, 0:SEQ]).then_inc(*ev("dve_q", ("keven", j)))
                        V().tensor_copy(k96[0:64, 2 * j + 1, :], ps[64:128, 0:SEQ]).then_inc(*ev("dve_q", ("kodd", j)))
                    for c in range(2):
                        ps = z(("qa", c))
                        V().tensor_copy(qabs[:, c, :, :].rearrange("p b (h t) -> p h b t", h=BH),
                                      ps[:, :].rearrange("p (h b t) -> p h b t", h=BH, b=NB)).then_inc(*ev("dve_q", ("qabs", c)))
                    dve.wait_ge(*at("dve_q", ("rot", 1, 3)))
                    V().tensor_copy(qpes[64:96, :, :].rearrange("p b (h t) -> p h b t", h=BH),
                                  q96[64:96, :, SAMP].rearrange("p h (b t) -> p h b t", b=NB)).then_inc(*ev("dve_q", "qpes"))

                    dve.wait_ge(*at("act_g", "ln"))
                    lf, g7 = grow[:, 1, :], grow[:, 5, :]
                    V().scalar_tensor_tensor(out=lf, in0=g7, scalar=0.0, in1=grow[:, 3, :], op0=ALU.min, op1=ALU.subtract).then_inc(*ev("dve_g", "lf"))
                    dve.wait_ge(*at("dve_g", "lf"))
                    V().tensor_tensor_scan(grow[:, 2, :], cs("reset")[0:4, :], lf, 0.0, ALU.mult, ALU.add).then_inc(*ev("dve_g", "b"))
                    dve.wait_ge(C.sem("in_m0"), 16)
                    V().tensor_copy(grow[:, 3, :], lf).then_inc(*ev("dve_g", "lf copy"))
                    V().tensor_copy(grow[:, 4, :], grow[:, 0, :]).then_inc(*ev("dve_g", "i copy"))
                    dve.wait_ge(*at("dve_g", "i copy"))
                    first = grow[:, 3, SEQ:T:TS]
                    V().tensor_tensor(mout[:, 1:9], first, m0[:], ALU.add).then_inc(*ev("dve_g", "lf m0"))
                    dve.wait_ge(*at("dve_g", "lf m0"))
                    V().tensor_tensor(grow[:, 4, SEQ:T:TS], mout[:, 1:9], grow[:, 0, SEQ:T:TS], ALU.max).then_inc(*ev("dve_g", "i first"))
                    V().memset(first, NEG).then_inc(*ev("dve_g", "lf first"))
                    dve.wait_ge(*at("dve_g", "lf first"))
                    V().tensor_tensor_scan(g7, grow[:, 3, :], grow[:, 4, :], 0.0, ALU.add, ALU.max).then_inc(*ev("dve_g", "m"))
                    dve.wait_ge(*at("dve_g", "m"))
                    V().tensor_copy(mout[:, 0:1], grow[:, 5, SEQ - 1:SEQ]).then_inc(*ev("dve_g", "mout p"))
                    V().tensor_copy(mout[:, 1:9], grow[:, 5, SEQ + TS - 1:T:TS]).then_inc(*ev("dve_g", "mout"))
                    V().tensor_tensor(growk[:, 0, :], grow[:, 2, :], g7, ALU.subtract).then_inc(*ev("dve_g", "b-m"))
                    dve.wait_ge(*at("dve_g", "b-m"))
                    V().tensor_tensor(growk[:, 1, SAMP].rearrange("p (b t) -> p b t", b=NB), growk[:, 0, SAMP].rearrange("p (b t) -> p b t", b=NB),
                                    m0[:].rearrange("p (b t) -> p b t", t=1).to_broadcast([4, NB, TS]), ALU.add).then_inc(*ev("dve_g", "b-m+m0"))
                    dve.wait_ge(*at("pool_z", "r4"))
                    V().tensor_tensor(grow[:, 3, :], grow[:, 0, :], grow[:, 2, :], ALU.subtract).then_inc(*ev("dve_g", "i-b"))
                    dve.wait_ge(*at("dve_g", "i-b"))
                    V().tensor_copy(r4[0:4, :], grow[:, 3, :]).then_inc(*ev("dve_g", "r4 a"))
                    V().tensor_scalar_mul(r4[64:68, :], g7, -1.0).then_inc(*ev("dve_g", "r4 b"))
                    V().tensor_scalar_add(r4[96:100, 0:SEQ], grow[:, 3, 0:SEQ], growk[:, 0, SEQ - 1:SEQ]).then_inc(*ev("dve_g", "r4 c"))
                    V().tensor_tensor(r4[96:100, SAMP].rearrange("p (b t) -> p b t", b=NB), grow[:, 3, SAMP].rearrange("p (b t) -> p b t", b=NB),
                                    growk[:, 0, SEQ + TS - 1:T:TS].rearrange("p (b t) -> p b t", t=1).to_broadcast([4, NB, TS]),
                                    ALU.add).then_inc(*ev("dve_g", "r4"))

                    def prompt_max(h):
                        for i in range(2):
                            n = (i + 1) * P
                            if h >= 1:
                                dve.wait_ge(*at("pe_m", ("ppT", h - 1, i)))
                            else:
                                dve.wait_ge(*at("pe_m", ("ps", h, i)))
                            V().tensor_tensor(pp[:, i, 0:n], m(("ps", h, i))[:, 0:n], cs("negP")[:, 256 - n:256], ALU.add).then_inc(*ev("dve_pa", ("s", h, i)))
                            dve.wait_ge(*at("dve_pa", ("s", h, i)))
                            V().reduce_max(stats[:, i:i + 1], pp[:, i, 0:n], AX).then_inc(*ev("dve_pa", ("max", h, i)))
                            dve.wait_ge(*at("dve_pa", ("max", h, i)))
                            V().tensor_scalar_mul(stats[:, 4 + i:5 + i], stats[:, i:i + 1], -BSCALE).then_inc(*ev("dve_pa", ("nm", h, i)))

                    def prompt_norm(h):
                        for i in range(2):
                            dve.wait_ge(*at("act_pa", ("e", h, i)))
                            V().reciprocal(stats[:, 12 + i:13 + i], stats[:, 8 + i:9 + i]).then_inc(*ev("dve_pa", ("r", h, i)))
                            dve.wait_ge(*at("dve_pa", ("r", h, i)))
                            V().tensor_scalar_mul(pp[:, i, 0:(i + 1) * P], pp[:, i, 0:(i + 1) * P], stats[:, 12 + i:13 + i]).then_inc(*ev("dve_pa", ("norm", h, i)))

                    for i, (xx, j) in enumerate([(x_, j_) for x_ in ("ak", "aq", "av", "ao") for j_ in (0, 2)]):
                        if xx == "aq":
                            for h in (j, j + 1):
                                V().tensor_scalar(qm[:, h, :], z(f"aq{h}")[:, 0:T], sw(f"aq{h}"), QSCALE, ALU.add, ALU.mult).then_inc(*ev("dve_a", ("aq", h)))
                        prompt_max(i)
                        prompt_norm(i)

                    def tokens(X, t):
                        tn = TOK[t][1]
                        V().tensor_copy(vtok[0:tn, t, :, 0:P], m((X, "vT", t))[0:tn, :].rearrange("p (h d) -> p h d", h=H)).then_inc(*ev(f"dve_{X}t", ("v", t)))

                    def conv_in(j):
                        if j == 0:
                            dve.wait_ge(*at("pe_m", ("po", BH - 1)))
                        dve.wait_ge(*at("act_c", ("sg", j)))
                        ps = z(f"ca{j}")
                        V().scalar_tensor_tensor(out=ucp[:, j, CW - 1:], in0=ps[:, 0:SEQ], scalar=sw(f"ca{j}"), in1=gt[:, j, 0:SEQ], op0=ALU.add,
                                               op1=ALU.mult).then_inc(*ev("dve_c", ("glu1", j)))
                        V().scalar_tensor_tensor(out=ucs[:, j, :, CW - 1:], in0=ps[:, SAMP].rearrange("p (b t) -> p b t", b=NB), scalar=sw(f"ca{j}"),
                                               in1=gt[:, j, SAMP].rearrange("p (b t) -> p b t", b=NB), op0=ALU.add, op1=ALU.mult).then_inc(*ev("dve_c", ("glu2", j)))

                    def decay(h):
                        ps = m(("rb", h))
                        if h >= 2:
                            dve.wait_ge(*at("dve_aw", ("w2", h - 2)))
                        for i, (o, n, src, t, rows_) in enumerate(((0, 256, 0, 0, P), (256, 128, P, 1, P), (384, NS, SEQ, 2, NS))):
                            if i == 0:
                                dve.wait_ge(*at("act_g", ("exp", 2)))
                            V().tensor_scalar(eb[0:rows_, h % 2, o:o + n], ps[0:rows_, src:src + n], col4[0:rows_, t, h:h + 1], 0.0, ALU.add,
                                            ALU.min).then_inc(*ev("dve_aw", (f"e{i}", h)))

                    def weigh(X, h):
                        ps = m((X, "st", h))
                        if X == "a":
                            dve.wait_ge(*at("pool_aw", ("e2", h)))
                            d = eb[:, h % 2, :]
                        else:
                            d = cs("decay")[:, h * 320:(h + 1) * 320]
                        if h >= 2:
                            dve.wait_ge(*at("pe_m", (X, "num", 2, 0)))
                        elif X == "d":
                            dve.wait_ge(*at("pe_m", ("a", "num", 2, 1)))
                        if X == "a":
                            V().tensor_tensor(wb[:, h % 2, 0:384], ps[:, 0:384], d[:, 0:384], ALU.mult).then_inc(*ev("dve_aw", ("w1", h)))
                            ds = d[0:NS, 384:448]
                        else:
                            V().tensor_tensor(wb[:, h % 2, 0:256], ps[:, 0:256], d[:, 0:256], ALU.mult).then_inc(*ev("dve_dw", ("w0", h)))
                            V().tensor_tensor(wb[:, h % 2, 256:384], ps[:, 256:384], d[:, 0:128], ALU.mult).then_inc(*ev("dve_dw", ("w1", h)))
                            ds = d[0:NS, 256:320]
                        V().tensor_tensor(wb[0:NS, h % 2, 384:448], ps[0:NS, 384:448], ds, ALU.mult).then_inc(*ev(f"dve_{X}w", ("w2", h)))

                    def spread_queries(X):
                        dve.wait_ge(*at("pool_z", "qz"))
                        dst = qz.rearrange("p (b x) -> p b x", x=264)[:, :, 0:256].rearrange("p b (h t) -> p h b t", h=H)[:, :, :, 0:TS]
                        src = qm[:, :, SAMP].rearrange("p h (b t) -> p h b t", b=NB)
                        if X == "a":
                            dve.wait_ge(*at("act_g", "wint"))
                            dve.wait_ge(*at("dve_a", ("aq", 3)))
                            w_ = wint[:].rearrange("p h (b t) -> p h b t", b=NB)
                            for h in range(H):
                                V().tensor_tensor(dst[:, h], src[:, h], w_[:, h], ALU.mult).then_inc(*ev("dve_aw", "qz" if h == 3 else ("qz", h)))
                        else:
                            dve.wait_ge(*at("dve_dk", ("dq", 3)))
                            dve.wait_ge(*at("pe_m", ("a", "num", 2, 1)))
                            for h in range(H):
                                w_ = cs("w_in_ret")[:, h * TS:(h + 1) * TS].rearrange("p (b t) -> p b t", b=1).to_broadcast([P, NB, TS])
                                V().tensor_tensor(dst[:, h], src[:, h], w_, ALU.mult).then_inc(*ev("dve_dw", "qz" if h == 3 else ("qz", h)))

                    def head_rows(X, hp, width):
                        for t, (t0, tn) in enumerate(TOK):
                            ps = m((X, "num", t, hp))
                            num = ps[0:tn, 0:2 * width].rearrange("p (h d) -> p h d", h=2)
                            s = f"dve_{X}h"
                            out = hh[0:tn, t, 2 * hp:2 * hp + 2, :]
                            if X == "a":
                                den, rec = stats[0:tn, 80:82], stats[0:tn, 82:84]
                                V().tensor_copy(rec, num[:, :, P]).then_inc(*ev(s, ("dc", t, hp)))
                                dve.wait_ge(*at(s, ("dc", t, hp)))
                                V().scalar_tensor_tensor(out=den, in0=rec, scalar=-1.0, in1=rec, op0=ALU.mult, op1=ALU.max).then_inc(*ev(s, ("abs", t, hp)))
                                dve.wait_ge(*at(s, ("abs", t, hp)))
                                V().tensor_tensor(den, den, col4[0:tn, t, 64 + 2 * hp:66 + 2 * hp], ALU.max).then_inc(*ev(s, ("den", t, hp)))
                                dve.wait_ge(*at(s, ("den", t, hp)))
                                V().reciprocal(rec, den).then_inc(*ev(s, ("rec", t, hp)))
                                dve.wait_ge(*at(s, ("rec", t, hp)))
                                V().tensor_tensor(out, num[:, :, 0:P], rec.rearrange("p (h d) -> p h d", d=1).to_broadcast([tn, 2, P]),
                                                ALU.mult).then_inc(*ev(s, ("h", t, hp)))
                            else:
                                if hp == 0:
                                    dve.wait_ge(*at("pe_m", ("a", "hT", t)))
                                V().tensor_copy(out, num).then_inc(*ev(s, ("h", t, hp)))
                            dve.wait_ge(*at(s, ("h", t, hp)))
                            for i in range(2):
                                h = 2 * hp + i
                                V().bn_stats(stats[0:tn, 112 + 6 * i:118 + 6 * i], hh[0:tn, t, h, :]).then_inc(*ev(s, ("bn", t, h)))
                                dve.wait_ge(*at(s, ("bn", t, h)))
                                V().bn_aggr(stats[0:tn, 32 + 8 * t + 2 * h:34 + 8 * t + 2 * h], stats[0:tn, 112 + 6 * i:118 + 6 * i]).then_inc(*ev(s, ("mv", t, h)))

                    def head_norm(X):
                        s = f"dve_{X}h"
                        for t, (t0, tn) in enumerate(TOK):
                            dve.wait_ge(*at(f"act_{X}h", t))
                            V().reciprocal(stats[0:tn, 64 + 4 * t:68 + 4 * t], stats[0:tn, 64 + 4 * t:68 + 4 * t]).then_inc(*ev(s, ("rs", t)))
                            dve.wait_ge(*at(s, ("rs", t)))
                            for h in range(H):
                                V().tensor_scalar(hh[0:tn, t, h, :], hh[0:tn, t, h, :], stats[0:tn, 32 + 8 * t + 2 * h:33 + 8 * t + 2 * h],
                                                stats[0:tn, 64 + 4 * t + h:65 + 4 * t + h], ALU.subtract, ALU.mult).then_inc(*ev(s, ("n", t, h)))

                    def head_gate(X, n):
                        if X == "a":
                            dve.wait_ge(*at("act_a", ("ao", 3)))
                        else:
                            dve.wait_ge(*at("act_d", ("dg", 3)))
                        for t, (t0, tn) in enumerate(TOK):
                            ps = m((X, "hT", t))[:, :].rearrange("p (h t) -> p h t", h=H)[:, :, 0:tn]
                            V().tensor_tensor(y[:, n, :, t0:t0 + tn], ps, y[:, n, :, t0:t0 + tn], ALU.mult).then_inc(*ev(f"dve_{X}y", t))

                    def state_update(X, width):
                        for b in range(NB):
                            for h in range(H):
                                ps = m((X, "cs", b, h // 2))
                                if X == "a":
                                    dec = wint[:, h, b * TS + TS - 1:b * TS + TS]
                                else:
                                    dec = WS_GAMMA[TS][h]
                                V().scalar_tensor_tensor(out=state[:, b, h, 0:width], in0=state[:, b, h, 0:width], scalar=dec,
                                                       in1=ps[:, (h % 2) * width:(h % 2 + 1) * width], op0=ALU.mult, op1=ALU.add
                                                       ).then_inc(*ev(f"dve_{X}c", (b, h)))

                    spread_queries("a")
                    conv_in(0)
                    for t in range(3):
                        tokens("a", t)
                    for h in (0, 1):
                        decay(h)
                        weigh("a", h)
                    conv_in(1)
                    head_rows("a", 0, W)
                    for h in (2, 3):
                        decay(h)
                        weigh("a", h)
                    conv_in(2)
                    head_rows("a", 1, W)
                    conv_in(3)
                    head_norm("a")
                    head_gate("a", 0)
                    state_update("a", W)

                    def rotate(x_, h):
                        dst = (qm if x_ == "dq" else km)[:, h, :]
                        if h == 0:
                            dve.wait_ge(*at("pe_m", ("a", "st", 3)))
                        dve.wait_ge(*at("act_dz", (x_, h)))
                        V().tensor_tensor(dst, tmp[:, h % 2, :], cs("cosD"), ALU.mult).then_inc(*ev("dve_dk", ("t1", x_, h)))
                        V().tensor_tensor(std[:], m(("sw", x_, h))[:, 0:T], cs("sinD"), ALU.mult).then_inc(*ev("dve_dk", ("t2", x_, h)))
                        dve.wait_ge(*at("dve_dk", ("t2", x_, h)))
                        V().tensor_tensor(dst, dst, std[:], ALU.add).then_inc(*ev("dve_dk", (x_, h)))

                    dve.wait_ge(C.sem("in_hist"), 16)
                    dve.wait_ge(*at("pool_z", "hist"))
                    dve.wait_ge(*at("pe_m", ("ps", BH - 1, 1)))

                    def taps(first, last):
                        for i in range(first, last):
                            j, k = 2 * (i // (2 * CW)) + i % 2, i % (2 * CW) // 2
                            wk = smallw[:, SM["cw"] + j * CW + k:SM["cw"] + j * CW + k + 1]
                            o, src = y[:, 2, j, 0:SEQ], ucp[:, j, k:k + SEQ]
                            if k == 0:
                                dve.wait_ge(*at("dve_c", ("glu1", j)))
                                nc.vector.tensor_scalar(o, src, wk, sw("cb", j), ALU.mult, ALU.add).then_inc(*ev("dve_c", ("tap", j, k)))
                            else:
                                dve.wait_ge(*at("dve_c", ("tap", j, k - 1)))
                                nc.vector.scalar_tensor_tensor(out=o, in0=src, scalar=wk, in1=o, op0=ALU.mult, op1=ALU.add).then_inc(*ev("dve_c", ("tap", j, k)))

                    for i, (x_, h) in enumerate([(x_, h) for x_ in ("dk", "dq") for h in (0, 2)]):
                        rotate(x_, h)
                        rotate(x_, h + 1)
                        taps(12 * i, 12 * (i + 1) if i < 3 else 4 * CW)

                    def gated(n, half):
                        for i in range(4):
                            d = half + i
                            k = d % 4
                            g = acc[:, d, :] if n == GATE_ORDER[3] else gt[:, k, :]
                            dve.wait_ge(*at("act_gt", (n, d)))
                            ps = z(("br", n, d))
                            if n == GATE_ORDER[0]:
                                V().tensor_tensor(gt[:, k, :], ps[:, 0:T], gt[:, k, :], ALU.mult).then_inc(*ev("dve_br", ("first", d)))
                                dve.wait_ge(*at("dve_br", ("first", d)))
                                V().tensor_copy(gsum[:, d, :], gt[:, k, :]).then_inc(*ev("dve_br", (n, d)))
                            else:
                                V().tensor_tensor(g, ps[:, 0:T], g, ALU.mult).then_inc(*ev("dve_br", ("t", n, d)))
                                dve.wait_ge(*at("dve_br", ("t", n, d)))
                                V().tensor_tensor(gsum[:, d, :], gsum[:, d, :], g, ALU.add).then_inc(*ev("dve_br", (n, d)))

                    gated(0, 0)
                    spread_queries("d")
                    for t in range(3):
                        tokens("d", t)
                    weigh("d", 0)
                    weigh("d", 1)
                    ps = m("conv sum")
                    for j in range(4):
                        V().scalar_tensor_tensor(out=y[:, 2, j, :], in0=ps[:, 0:T], scalar=-1.0 / CCH, in1=y[:, 2, j, :], op0=ALU.mult,
                                               op1=ALU.add).then_inc(*ev("dve_c", ("mu", j)))
                    gated(0, 4)
                    head_rows("d", 0, P)
                    weigh("d", 2)
                    weigh("d", 3)
                    dve.wait_ge(*at("act_cy", "std"))
                    V().reciprocal(std[:], std[:]).then_inc(*ev("dve_c", "rs"))
                    dve.wait_ge(*at("dve_c", "rs"))
                    for j in range(4):
                        V().tensor_tensor(y[:, 2, j, :], y[:, 2, j, :], std[:], ALU.mult).then_inc(*ev("dve_c", ("xn", j)))
                    head_rows("d", 1, P)
                    gated(2, 0)
                    head_norm("d")
                    head_gate("d", 3)
                    state_update("d", P)
                    gated(2, 4)

                    def sample_max(b):
                        r = b % 2
                        s = stats[0:NS, :]
                        if b == 0:
                            dve.wait_ge(*at("dve_dc", (NB - 1, 3)))
                        if b >= 2:
                            dve.wait_ge(*at("pe_m", ("snT", b - 2)))
                        V().tensor_tensor(pb[0:NS, r, PAST:PAST + NS], m(("ss", b, 2))[0:NS, 0:NS], cs("negS")[0:NS, b * NS:(b + 1) * NS],
                                        ALU.add).then_inc(*ev("dve_s2", ("new", b)))
                        for g in range(2):
                            V().reduce_max(s[:, 90 + g:91 + g], m(("ss", b, g))[0:NS, :], AX).then_inc(*ev("dve_s2", ("max", b, g)))
                        dve.wait_ge(*at("dve_s2", ("new", b)))
                        V().reduce_max(s[:, 92:93], pb[0:NS, r, PAST:PAST + NS], AX).then_inc(*ev("dve_s2", ("max", b, 2)))
                        dve.wait_ge(*at("dve_s2", ("max", b, 2)))
                        V().reduce_max(s[:, 93:94], s[:, 90:93], AX).then_inc(*ev("dve_s2", ("max", b)))
                        dve.wait_ge(*at("dve_s2", ("max", b)))
                        V().tensor_scalar_mul(s[:, 100 + r:101 + r], s[:, 93:94], -BSCALE).then_inc(*ev("dve_s2", ("nm", b)))

                    def sample_turned(b):
                        r = b % 2
                        if b >= 2:
                            dve.wait_ge(*at("pe_m", ("so", b - 2)))
                        V().tensor_copy(pT[0:NS, r, 512:576], m(("snT", b))[0:NS, 0:NS]).then_inc(*ev("dve_s2", ("pnT", b)))

                    def sample_scaled(b):
                        r = b % 2
                        s = stats[0:NS, :]
                        dve.wait_ge(*at("act_s", ("e", b, 2)))
                        V().reduce_sum(s[:, 94:95], s[:, 104 + 4 * r:107 + 4 * r], AX).then_inc(*ev("dve_s2", ("sum", b)))
                        dve.wait_ge(*at("dve_s2", ("sum", b)))
                        V().reciprocal(s[:, 96 + r:97 + r], s[:, 94:95]).then_inc(*ev("dve_s2", ("r", b)))
                        dve.wait_ge(*at("dve_s2", ("r", b)))
                        if b >= 2:
                            dve.wait_ge(*at("pe_m", ("soT", b - 2)))
                        V().tensor_scalar_mul(olat[0:NS, r, :], m(("so", b))[0:NS, 0:KVR], s[:, 96 + r:97 + r]).then_inc(*ev("dve_s2", ("o", b)))

                    def slot(b):
                        for kind, *which in SLOTS[b]:
                            if kind == "branch":
                                gated(*which)
                            elif kind == "ada" and which[0] > 8:
                                ada(which[0] - 1, which[0])

                    for b in range(NB):
                        if b >= 1:
                            sample_turned(b - 1)
                        sample_max(b)
                        if b >= 1:
                            sample_scaled(b - 1)
                        slot(b)
                    sample_turned(NB - 1)
                    sample_scaled(NB - 1)
                    slot(NB)
                    gated(1, 0)
                    gated(1, 4)

                    def residual(which, name, g, src_x):
                        for d in range(KC):
                            ps = z((name, d))
                            dve.wait_ge(*at("dve_mod", 11 if which == 1 else 23))
                            V().tensor_scalar_mul(tmp[:, d % 2, 0:SEQ], ps[:, 0:SEQ], mod[:, g + d, 0:1]).then_inc(*ev("dve_r", ("gp", which, d)))
                            V().tensor_tensor(tmp[:, d % 2, SAMP].rearrange("p (b t) -> p b t", b=NB), ps[:, SAMP].rearrange("p (b t) -> p b t", b=NB),
                                            mod[:, g + d, 1:9].rearrange("p (b t) -> p b t", t=1).to_broadcast([P, NB, TS]),
                                            ALU.mult).then_inc(*ev("dve_r", ("g", which, d)))
                            dve.wait_ge(*at("dve_r", ("g", which, d)))
                            V().scalar_tensor_tensor(out=u[:, d, :], in0=x[:, d, :], scalar=ALPHA, in1=tmp[:, d % 2, :], op0=ALU.mult,
                                                   op1=ALU.add).then_inc(*ev("dve_r", ("r", which, d)))

                    def norm(which, filler1, filler2):
                        ps = m(("mean", which))
                        for k in range(KC):
                            V().scalar_tensor_tensor(out=u[:, k, :], in0=ps[:, 0:T], scalar=-1.0 / D_MODEL, in1=u[:, k, :], op0=ALU.mult,
                                                   op1=ALU.add).then_inc(*ev("dve_r", ("mu", which, k)))
                        if filler1:
                            ada(filler1[0] - 1, filler1[1])
                        dve.wait_ge(*at("act_n", ("std", which)))
                        V().reciprocal(std[:], std[:]).then_inc(*ev("dve_r", ("rs", which)))
                        dve.wait_ge(*at("dve_r", ("rs", which)))
                        for k in range(KC):
                            V().scalar_tensor_tensor(out=u[:, k, :], in0=u[:, k, :], scalar=sw(f"ln{which}g", k), in1=std[:], op0=ALU.mult,
                                                   op1=ALU.mult).then_inc(*ev("dve_r", ("xn", which, k)))
                        if filler2:
                            ada(*filler2)

                    residual(1, "wo", 16, x)
                    norm(1, (18, 20), (20, 24))
                    dve.wait_ge(*at("act_n", ("x", 1, KC - 1)))
                    dve.wait_ge(*at("dve_mod", 23))
                    dve.wait_ge(*at("pe_m", ("var", 1)))
                    modulate("dve_u2", acc, 24, 32)
                    for j in range(FT):
                        dve.wait_ge(*at("act_f", j))
                        V().tensor_tensor(hid[:, j, :], z(("f3", j))[:, 0:T], gt[:, j % 2, :], ALU.mult).then_inc(*ev("dve_f", j))
                    residual(2, "fo", 40, x)
                    norm(2, None, None)

                @block.gpsimd
                def _(pool):
                    def G():
                        in_turn(pool, "pool")
                        return nc.gpsimd

                    G().memset(r4[:], 0.0).then_inc(*ev("pool_z", "r4"))
                    pool.wait_ge(*at("dve_b", "kpe"))
                    for h in range(BH):
                        G().tensor_copy(k96[64:96, h, :], kpe[64:96, 0:SEQ]).then_inc(*ev("pool_k", "kpe all" if h == BH - 1 else h))
                    G().memset(qz, 0.0).then_inc(*ev("pool_z", "qz"))
                    G().memset(vtok[:, :, :, P:W], 1.0).then_inc(*ev("pool_z", "ones"))
                    pool.wait_ge(*at("pe_m", ("po", BH - 1)))
                    G().memset(ucp[:, :, 0:CW - 1], 0.0).then_inc(*ev("pool_z", "hist"))

                    def weigh_keys(X):
                        for t, (t0, tn) in enumerate(TOK):
                            pool.wait_ge(*at(f"act_{X}t", ("k", t)))
                            if X == "a":
                                pool.wait_ge(*at("act_g", ("exp", t)))
                                w_ = col4[0:tn, t, 96:100]
                            else:
                                w_ = cs("w_st")[0:tn, H * t:H * t + H]
                            G().tensor_tensor(ktok[0:tn, t], ktok[0:tn, t], w_.rearrange("p (h d) -> p h d", d=1).to_broadcast([tn, H, P]),
                                            ALU.mult).then_inc(*ev(f"pool_{X}k", t))

                    def batch_keys(X):
                        pool.wait_ge(*at(f"pool_{X}k", 2))
                        for b in range(NB):
                            if b >= 2:
                                pool.wait_ge(*at("pe_m", (X, "cs", b - 2, 1)))
                            elif X == "d":
                                pool.wait_ge(*at("pe_m", ("a", "cs", NB - 2 + b, 1)))
                            G().tensor_scalar(kmb[0:NS, b % 2, :], ktok[0:NS, 2].rearrange("p h d -> p (h d)"), cs("batch")[0:NS, b:b + 1], None,
                                            ALU.mult).then_inc(*ev(f"pool_{X}m", b))

                    def mask(h):
                        pool.wait_ge(*at("act_aw", ("e2", h)))
                        G().tensor_tensor(eb[:, h % 2, 0:384], eb[:, h % 2, 0:384], cs("causal")[:, 0:384], ALU.mult).then_inc(*ev("pool_aw", ("e1", h)))
                        G().tensor_tensor(eb[0:NS, h % 2, 384:448], eb[0:NS, h % 2, 384:448], cs("causal")[0:NS, 384:448],
                                        ALU.mult).then_inc(*ev("pool_aw", ("e2", h)))

                    mask(0)
                    mask(1)
                    weigh_keys("a")
                    mask(2)
                    mask(3)
                    batch_keys("a")

                    pool.wait_ge(C.sem("in_hist"), 16)
                    pool.wait_ge(*at("dve_c", ("glu2", 3)))
                    pool.wait_ge(*at("dve_aw", ("w2", 3)))
                    conv_s = y[:, 2, :, SAMP].rearrange("p j (b t) -> p j b t", b=NB)
                    for k in range(CW):
                        wk = smallw[:, SM["cw"]:SM["cw"] + 4 * CW].rearrange("p (j b k) -> p j b k", j=4, b=1)[:, :, :, k:k + 1]
                        prod = eb[:, k % 2, 0:4 * NS].rearrange("p (j b t) -> p j b t", j=4, b=NB)
                        if k >= 2:
                            pool.wait_ge(*at("pool_c", ("sum", k - 2)))
                        nc.gpsimd.tensor_tensor(prod, ucs[:, :, :, k:k + TS], wk.to_broadcast([P, 4, NB, TS]), ALU.mult).then_inc(*ev("pool_c", ("prod", k)))
                        pool.wait_ge(*at("pool_c", ("prod", k)))
                        if k == 0:
                            bias = smallw[:, SM["cb"]:SM["cb"] + 4].rearrange("p (j b k) -> p j b k", b=1, k=1).to_broadcast([P, 4, NB, TS])
                            nc.gpsimd.tensor_tensor(conv_s, prod, bias, ALU.add).then_inc(*ev("pool_c", ("sum", k)))
                        else:
                            pool.wait_ge(*at("pool_c", ("sum", k - 1)))
                            nc.gpsimd.tensor_tensor(conv_s, conv_s, prod, ALU.add).then_inc(*ev("pool_c", ("sum", k)))
                    weigh_keys("d")
                    batch_keys("d")

            nc.all_engine_barrier()
            for s in C.sems.values():
                nc.gpsimd.sem_clear(s)
            nc.all_engine_barrier()
        return dict(C.value)


def _f(v):
    return np.asarray(v)


def pack(inp):
    g = {k: _f(v) for k, v in inp.items()}
    L, f = DEPTH, g["x_prompt"].dtype
    out = {}

    def feat(v):
        return v.T.reshape(-1, P, v.shape[0]).transpose(1, 0, 2)

    out["x"] = feat(np.concatenate([g["x_prompt"].reshape(SEQ, -1), g["x_sample"].reshape(NS, -1)]))
    out["c"] = feat(np.concatenate([g["c_prompt"], g["c_sample"]]))
    out["pages"] = g["page_table"].reshape(1, -1)
    out["consts"] = np.concatenate(list(CONST.values()), 1)

    def tiles(v):
        k, m = v.shape
        return v.reshape(k // P, P, m // P, P).transpose(1, 2, 0, 3)

    wp = np.zeros((L, NBLK, P, 2048), f)
    small = np.zeros((L, P, NSM), f)
    for l in range(L):
        w_in, b_in = g["w_in"][l], g["b_in"][l]
        uq = g["mla_w_uq"][l].reshape(QR, BH, NOPE + ROPE)
        uq = tiles(np.concatenate([uq[:, :, :NOPE].reshape(QR, -1), uq[:, :, NOPE:].reshape(QR, -1)], 1)).reshape(P, -1)
        uk = g["mla_w_uk"][l]
        ffn1, ffn3 = tiles(g["w_ffn1"][l]), tiles(g["w_ffn3"][l])
        ffn2 = tiles(g["w_ffn2"][l]).reshape(P, 11, 2048)
        wout = tiles(g["w_out"][l]).reshape(P, 4, 2048)
        for n, b in enumerate(BLOCKS):
            d = wp[l, n]
            if b[0] == "ada":
                d[:] = g["w_ada"][l][:, b[1] * 256:(b[1] + 1) * 256].reshape(KC, P, 256).transpose(1, 0, 2).reshape(P, -1)
            elif b[0] == "in":
                dd = d.reshape(P, 2, KC, P)
                for j, name in enumerate(b[1:]):
                    for at, col, cnt in tile_columns(name):
                        dd[:, j, :, at:at + cnt] = w_in[:, col:col + cnt].reshape(KC, P, cnt).transpose(1, 0, 2)
            elif b[0] == "uq":
                d[:] = uq[:, :2048]
            elif b[0] == "uk":
                d[:, :1024] = uk.reshape(2, P, 512).transpose(1, 0, 2).reshape(P, -1)
                d[:, 1024:1280] = uq[:, 2048:]
            elif b[0] == "ukT":
                d[:64] = uk.transpose(2, 1, 0).reshape(64, -1)
            elif b[0] == "branch":
                d[:] = tiles(g["w_branch"][l, b[1]])[:, b[2]:b[2] + 4].reshape(P, -1)
            elif b[0] == "out":
                d[:] = wout[:, b[1]]
            elif b[0] == "ffn":
                d[:, :1024] = ffn1[:, b[1]].reshape(P, -1)
                d[:, 1024:] = ffn3[:, b[1]].reshape(P, -1)
            elif b[0] == "ffn2":
                d[:] = ffn2[:, b[1]]
        s = small[l]
        s[:, 0:48] = g["b_ada"][l].reshape(48, P).T
        for name in TILES:
            for at, col, cnt in tile_columns(name):
                s[at:at + cnt, BIAS[name]] = b_in[col:col + cnt]
        for name, v in (("qn", "mla_q_norm"), ("kvn", "mla_kv_norm"), ("cb", "conv_b"), ("clg", "conv_ln_g"), ("clb", "conv_ln_b"),
                        ("ln1g", "ln1_g"), ("ln1b", "ln1_b"), ("ln2g", "ln2_g"), ("ln2b", "ln2_b")):
            w = g[v][l]
            s[:, SM[name]:SM[name] + w.size // P] = w.reshape(-1, P).T
        s[:, SM["cw"]:SM["cw"] + 4 * CW] = g["conv_w"][l].T.reshape(4, P, CW).transpose(1, 0, 2).reshape(P, -1)
    out["wpack"], out["small"] = wp, small
    out["wuv"] = g["mla_w_uv"].reshape(L, 2, P, 512).transpose(0, 2, 1, 3)
    cache = g["cache_mla"]
    lat = cache[..., :KVR]
    latT = lat.reshape(L, POOL, P, 2, P).transpose(0, 1, 4, 3, 2).reshape(L, POOL, P, 2 * P)
    out["cache"] = np.concatenate([latT, lat], 3)
    out["rope"] = cache[..., KVR:].transpose(0, 1, 3, 2)
    out["stateA"] = np.concatenate([g["state_mlstm_C"], g["state_mlstm_n"][..., None]], 4).transpose(0, 3, 1, 2, 4)
    out["stateD"] = g["state_ret"].transpose(0, 3, 1, 2, 4)
    out["m0"] = g["state_mlstm_m"].transpose(0, 2, 1)
    out["hist"] = g["state_conv"].reshape(L, NB, CW - 1, 4, P).transpose(0, 4, 3, 1, 2)
    return {k: np.ascontiguousarray(v) for k, v in out.items()}


OUTS = {"o_y": (P, KC, T), "o_rows_c": (DEPTH, P, 2, T), "o_rows_k": (DEPTH, ROPE, T), "o_cn_p": (DEPTH, P, H, W),
        "o_cn_s": (DEPTH, P, NB, H, W), "o_m": (DEPTH, H, 9), "o_conv_p": (DEPTH, P, 4, CW - 1),
        "o_conv_s": (DEPTH, P, 4, NB, CW - 1), "o_ret_p": (DEPTH, P, H, P), "o_ret_s": (DEPTH, P, NB, H, P)}


def kernel(**inputs):
    import concourse.bacc as bacc
    from concourse.bass_utils import run_bass_kernel_spmd

    arrays = pack(inputs)

    def build(known):
        nc = bacc.Bacc("TRN2", target_bir_lowering=False, num_devices=1)
        a = {k: nc.dram_tensor(k + "_dram", v.shape, mybir.dt.from_np(v.dtype), kind="ExternalInput").ap() for k, v in arrays.items()}
        for k, s in OUTS.items():
            a[k] = nc.dram_tensor(k, s, F32, kind="ExternalOutput").ap()
        return nc, decoder_program(nc, a, known)

    _, counted = build({})
    nc, again = build(counted)
    assert counted == again
    r = run_bass_kernel_spmd(nc, [{k + "_dram": v for k, v in arrays.items()}], core_ids=[0]).results[0]

    L = DEPTH
    y = r["o_y"].transpose(2, 1, 0).reshape(T, D_MODEL)
    rows = np.concatenate([r["o_rows_c"].transpose(0, 3, 2, 1).reshape(L, T, KVR), r["o_rows_k"].transpose(0, 2, 1)], 2)
    cn_p, cn_s = r["o_cn_p"].transpose(0, 2, 1, 3)[:, None], r["o_cn_s"].transpose(0, 2, 3, 1, 4)
    m = r["o_m"].transpose(0, 2, 1)
    conv_p = r["o_conv_p"].transpose(0, 3, 2, 1).reshape(L, 1, CW - 1, CCH)
    conv_s = r["o_conv_s"].transpose(0, 3, 4, 2, 1).reshape(L, NB, CW - 1, CCH)
    got = (y[:SEQ].reshape(1, SEQ, D_MODEL), y[SEQ:].reshape(NB, TS, D_MODEL),
           rows[:, :SEQ].reshape(L, 1, SEQ, -1), rows[:, SEQ:].reshape(L, NB, TS, -1),
           cn_p[..., :P], cn_s[..., :P], cn_p[..., P], cn_s[..., P], m[:, 0:1], m[:, 1:], conv_p, conv_s,
           r["o_ret_p"].transpose(0, 2, 1, 3)[:, None], r["o_ret_s"].transpose(0, 2, 3, 1, 4))
    return tuple(np.ascontiguousarray(v) for v in got)
```

```python
from contextlib import ExitStack

import numpy as np

import concourse.bass as bass
from concourse import mybir
from concourse.alu_op_type import AluOpType as ALU

F32 = mybir.dt.float32
F32R = mybir.dt.float32r
I32 = mybir.dt.int32
ACT = mybir.ActivationFunctionType
AX = mybir.AxisListType.X

P = 128
D_MODEL, SEQ, DEPTH, NB, TS, PAST, PAGE = 1024, 256, 2, 8, 8, 1024, 128
NS = NB * TS
T = SEQ + NS
KC = D_MODEL // P
H = 4
BH, NOPE, ROPE, VD = 8, 64, 32, 64
QR, KVR = 384, 256
CW, CCH = 31, 512
HID = 2816
FT = HID // P
NPG = PAST // PAGE
POOL = NB * NPG * 5 // 4
ALPHA = (2 * DEPTH) ** 0.25
LN_EPS, RMS_EPS = 1e-5, 1e-6
QSCALE = P ** -0.5
BSCALE = (NOPE + ROPE) ** -0.5
NEG = -1.0e30
TOK = [(0, 128), (128, 128), (256, NS)]
W = 129
SAMP = slice(SEQ, T)

OFF = {}
_at = 0
for _n, _w in (("aq", 512), ("ak", 512), ("av", 512), ("ao", 512), ("ai", 4), ("af", 4), ("bq", QR), ("bkv", KVR),
               ("bkr", ROPE), ("ca", CCH), ("cg", CCH), ("dq", 512), ("dk", 512), ("dv", 512), ("dg", 512),
               ("gates", 4 * D_MODEL)):
    OFF[_n] = _at
    _at += _w

GATE_ORDER = (0, 2, 3, 1)
A_STREAM = [("ak", 0), ("ak", 2), ("aq", 0), ("aq", 2), ("av", 0), ("av", 2), ("ao", 2)]
BLOCKS = ([("ada", a) for a in range(8)] + [("in", "small", "kv0"), ("in", "kv1", "bq0"), ("in", "bq1", "bq2")]
          + [("in", "ao0", "ao1"), ("uq",), ("uk",), ("ukT",)] + [("in", f"{x}{i}", f"{x}{i + 1}") for x, i in A_STREAM]
          + [("in", f"cg{j}", f"ca{j}") for j in range(4)]
          + [("in", f"{x}{i}", f"{x}{i + 1}") for x in ("dk", "dq", "dv", "dg") for i in (0, 2)])
for _n in GATE_ORDER[:2]:
    for _h in (0, 4):
        BLOCKS += [("in", f"g{_n}_{_h}", f"g{_n}_{_h + 1}"), ("in", f"g{_n}_{_h + 2}", f"g{_n}_{_h + 3}"), ("branch", _n, _h)]


SLOTS = [[("gate", 3, 0)],
         [("ada", 8), ("gate", 3, 2), ("ada", 9)],
         [("ada", 10), ("branch", 3, 0), ("ada", 11)],
         [("ada", 12), ("gate", 3, 4), ("ada", 13)],
         [("ada", 14), ("gate", 3, 6), ("ada", 15)],
         [("ada", 16), ("branch", 3, 4), ("ada", 17)],
         [("gate", 1, 0), ("gate", 1, 2)],
         [("gate", 1, 4)],
         [("gate", 1, 6)]]
SLOT_START = []
for _slot in SLOTS:
    SLOT_START.append(len(BLOCKS))
    for _u in _slot:
        BLOCKS += [("in", f"g{_u[1]}_{_u[2]}", f"g{_u[1]}_{_u[2] + 1}") if _u[0] == "gate" else _u]
BLOCKS += [("branch", 1, 0), ("branch", 1, 4)]
BLOCKS += [("out", i) for i in range(4)] + [("ada", a) for a in range(18, 24)]
BLOCKS += [("ffn", j) for j in range(FT)] + [("ffn2", i) for i in range(11)]
NBLK = len(BLOCKS)
SPLIT = [b for b in BLOCKS if b[0] == "out" or b in [("ada", a) for a in range(8, 18)] or b[0] == "in" and b[1] in [f"g{n}_{i}" for n in GATE_ORDER[1:] for i in range(8)]]
RING = 3

TILES = (["small", "kv0", "kv1", "bq0", "bq1", "bq2"] + [f"{x}{i}" for x in ("aq", "ak", "av", "ao", "ca", "cg", "dq", "dk", "dv", "dg") for i in range(4)]
         + [f"g{n}_{i}" for n in range(4) for i in range(8)])
BIAS = {n: 48 + i for i, n in enumerate(TILES)}
SM = {}
_at = 48 + len(TILES)
for _n, _w in (("qn", 3), ("kvn", 2), ("cb", 4), ("clg", 4), ("clb", 4), ("ln1g", 8), ("ln1b", 8), ("ln2g", 8), ("ln2b", 8), ("cw", 4 * CW)):
    SM[_n] = _at
    _at += _w
NSM = _at


def tile_columns(name):
    if name == "small":
        return [(0, OFF["ai"], 4), (32, OFF["af"], 4), (64, OFF["bkr"], 32)]
    if name[:2] == "kv":
        return [(0, OFF["bkv"] + P * int(name[2]), P)]
    if name[0] == "g":
        n, i = name[1:].split("_")
        return [(0, OFF["gates"] + D_MODEL * int(n) + P * int(i), P)]
    return [(0, OFF[name[:2]] + P * int(name[2]), P)]


def constants():
    f = np.float32
    c = {}
    c["ident"] = np.eye(P, dtype=f)
    c["ones"] = np.ones((P, P), f)
    pos = np.concatenate([np.arange(SEQ), np.tile(PAST + np.arange(TS), NB)]).astype(f)

    def rot(d, reps):
        inv = (f(10000.0) ** (-np.arange(0, d, 2, dtype=f) / f(d))).astype(f)
        ang = (pos[None, :] * inv[:, None]).astype(f)
        cos, sin = np.cos(ang.astype(np.float64)), np.sin(ang.astype(np.float64))
        return np.tile(np.concatenate([cos, cos]), (reps, 1)).astype(f), np.tile(np.concatenate([-sin, sin]), (reps, 1)).astype(f)

    c["cosD"], c["sinD"] = rot(P, 1)
    c["cosB"], c["sinB"] = rot(ROPE, 4)
    m = np.arange(P)
    c["swapD"] = (m[:, None] == (m[None, :] + 64) % P).astype(f)
    c["swapB"] = (m[:, None] == (m[None, :] // 32) * 32 + (m[None, :] + 16) % 32).astype(f)
    tri = (m[:, None] <= m[None, :]).astype(f)
    s = np.arange(NS)
    tri_s = np.zeros((P, NS), f)
    tri_s[:NS] = ((s[:, None] // TS == s[None, :] // TS) & (s[:, None] <= s[None, :]))
    c["causal"] = np.concatenate([tri, np.ones((P, P), f), tri, tri_s], 1)
    lg = np.log(1.0 - 2.0 ** (-5.0 - np.arange(H)))
    dec = np.zeros((P, H, 320))
    diff = m[None, :] - m[:, None]
    for h in range(H):
        dec[:, h, 0:128] = np.where(diff >= 0, np.exp(np.maximum(diff, 0) * lg[h]), 0)
        dec[:, h, 128:256] = np.exp((diff + 128) * lg[h])
        d8 = s[None, :] - s[:, None]
        dec[:NS, h, 256:320] = np.where(tri_s[:NS] > 0, np.exp(np.maximum(d8, 0) * lg[h]), 0)
    c["decay"] = (dec * QSCALE).reshape(P, -1).astype(f)
    c["w_in_ret"] = np.tile(np.exp((np.arange(TS) + 1.0)[None, :] * lg[:, None]).reshape(1, H * TS), (P, 1)).astype(f)
    wst = np.zeros((P, 3, H))
    for t in range(2):
        wst[:, t] = np.exp((SEQ - 1 - 128 * t - m)[:, None] * lg[None, :])
    wst[:NS, 2] = np.exp((TS - 1 - s % TS)[:, None] * lg[None, :])
    c["w_st"] = (wst * QSCALE).reshape(P, -1).astype(f)
    bm = np.zeros((P, NB), f)
    bm[s, s // TS] = 1
    c["batch"] = bm
    neg = np.where(m[None, :] <= m[:, None], 0, NEG)
    c["negP"] = np.concatenate([np.zeros((P, P)), neg], 1).astype(f)
    ns = np.full((P, NB, NS), NEG)
    q = np.arange(NS) % TS
    for b in range(NB):
        ok = (s[None, :] // TS == b) & (s[None, :] % TS <= q[:, None])
        ns[:NS, b] = np.where(ok, 0, NEG)
    c["negS"] = ns.reshape(P, -1).astype(f)
    reset = np.ones((P, T), f)
    reset[:, 0] = 0
    reset[:, SEQ::TS] = 0
    c["reset"] = reset
    c["eps"] = np.tile(np.array([[LN_EPS, RMS_EPS, 1.0, 0.0]], f), (P, 1))
    return c


CONST = constants()
CAT = {}
_at = 0
for _n, _a in CONST.items():
    CAT[_n] = (_at, _a.shape[1])
    _at += _a.shape[1]
NCONST = _at
WS_GAMMA = {n: [float(np.exp(n * np.log(1.0 - 2.0 ** (-5.0 - h)))) for h in range(H)] for n in (TS,)}


class Counts:

    def __init__(self, nc, ctx, known):
        self.nc, self.ctx, self.known = nc, ctx, known
        self.sems, self.value, self.total = {}, {}, {}
        self.waited, self.last = {}, {}

    def sem(self, name):
        if name not in self.sems:
            self.sems[name] = self.ctx.enter_context(self.nc.semaphore(name))
        return self.sems[name]

    def ev(self, name, label, by=1):
        self.total[name] = self.total.get(name, 0) + by
        assert (name, label) not in self.value, (name, label)
        self.value[name, label] = self.total[name]
        self.last[name.split("_")[0]] = (name, self.total[name])
        return self.sem(name), by

    def at(self, name, label):
        return self.sem(name), self.known[name, label] if self.known else 1


def decoder_program(nc, a, known):
    ctx = ExitStack()
    with ctx:
        place = {}

        def sb(name, shape, dt=F32):
            place[name] = (nc.sbuf_base + 31) // 32 * 32
            return ctx.enter_context(nc.sbuf_tensor(name, shape, dt))

        def over(name, shape, where, start=0):
            return nc.alloc_sbuf_tensor_at(name, shape, F32R, offset=place[where] + 4 * start)

        C = Counts(nc, ctx, known)
        ev, at = C.ev, C.at

        def in_turn(eng, prefix):
            name, value = C.last.get(prefix, (None, 0))
            if name and C.waited.get((eng, name), 0) < value:
                eng.wait_ge(C.sem(name), value)
                C.waited[eng, name] = value

        const = sb("const", [P, NCONST])

        def cs(name):
            o, n = CAT[name]
            return const[:, o:o + n]

        ident, ones = cs("ident"), cs("ones")
        smallw = sb("smallw", [P, NSM])

        def sw(name, i=0, n=1):
            o = (SM[name] if name in SM else BIAS[name]) + i
            return smallw[:, o:o + n]

        x = sb("x", [P, KC, T])
        u = sb("u", [P, KC, T])
        acc = sb("acc", [P, KC, T])
        ring = sb("ring", [P, RING, 2048])
        y = sb("y", [P, 4, 4, T])
        q96 = sb("q96", [P, BH, T])
        qabs = sb("qabs", [P, 2, NB, NS])
        mod = sb("mod", [P, 48, 9])
        siluc = sb("siluc", [P, KC, 9])
        c2 = sb("c2", [P, KC, 18], F32R)
        rowb = sb("rowb", [18, 2, 256])
        ckv = sb("ckv", [P, 2, T])
        kpe = sb("kpe", [P, T])
        ckvtok = sb("ckvtok", [P, KVR])
        gsum = q96
        qpes = sb("qpes", [P, NB, NS])
        wuv = sb("wuv", [P, 2, BH * VD])
        gt = sb("gt", [P, 4, T])
        tmp = sb("tmp", [P, 2, T])
        std = sb("std", [P, T])
        stats = sb("stats", [P, 128])
        pages = sb("pages", [1, NB * NPG], I32)
        arena = sb("arena", [P, 17600])

        used = [0]

        def part(n, shape, names, rows=P, start=None):
            o = used[0] if start is None else start
            v = arena[:, o:o + n].rearrange(f"p ({names}) -> p {names}", **shape) if shape else arena[:, o:o + n]
            if start is None:
                used[0] += n
            assert o + n <= 17600
            return v

        qm = part(H * T, dict(h=H, t=T), "h t")
        km = part(H * T, dict(h=H, t=T), "h t")
        vm = part(H * T, dict(h=H, t=T), "h t")
        ktok = part(3 * 512, dict(n=3, h=H, d=P), "n h d")
        vtok = part(3 * H * W, dict(n=3, h=H, d=W), "n h d")
        state = part(NB * H * W, dict(b=NB, h=H, d=W), "b h d")
        eb = part(2 * 448, dict(r=2, t=448), "r t")
        wb = part(2 * 448, dict(r=2, t=448), "r t")
        hh = part(3 * 512, dict(n=3, h=H, d=P), "n h d")
        kmb = part(2 * 512, dict(r=2, d=512), "r d")
        qz = part(8 * 264, None, None)
        hh0 = used[0] - 2 * 512 - 8 * 264 - 3 * 512
        grow = part(6 * T, dict(r=6, t=T), "r t", start=hh0)[0:4]
        r4 = part(T, None, None, start=hh0 + 6 * T)
        bqz = part(3 * T, dict(c=3, t=T), "c t", start=0)
        sq5 = part(5 * T, dict(c=5, t=T), "c t", start=3 * T)
        qr = part(2 * T, dict(c=2, t=T), "c t", start=8 * T)
        krz = part(T, None, None, start=10 * T)
        used[0] = 0
        cache = part(2 * NPG * 640, dict(r=2, g=NPG, f=640), "r g f")
        pb = part(2 * 1088, dict(r=2, f=1088), "r f")
        pT = part(2 * 576, dict(r=2, f=576), "r f")
        olat = part(2 * KVR, dict(r=2, f=KVR), "r f")
        olatT = part(2 * BH * NS, dict(c=2, h=BH, t=NS), "c h t")
        assert place["q96"] == place["y"] + 4 * 16 * T and place["qabs"] == place["q96"] + 4 * BH * T
        whi = [over(f"whi{i}", [P, 2048], "y", 4096 * i) for i in range(2)]
        wlo = [over(f"wlo{i}", [P, 2048], "y", 4096 * i + 2048) for i in range(2)]
        xhi, xlo = over("xhi", [P, KC, T], "u"), over("xlo", [P, KC, T], "acc")
        whx = [over(f"whx{i}", [P, 1024], "arena", 15104 + 1024 * i) for i in range(2)]
        whg = [over(f"whg{i}", [P, 1024], "acc", 1024 * i) for i in range(2)]
        uhi, ulo = over("uhi", [P, KC, T], "x"), over("ulo", [P, KC, T], "u")

        def high_buffer(q):
            return whg if SPLIT[q][0] == "in" and SPLIT[q][1][:2] in ("g2", "g3") else whx

        wlx = over("wlx", [P, RING, 2048], "ring")
        ghi, glo = over("ghi", [P, KC, T], "arena"), over("glo", [P, KC, T], "arena", KC * T)
        hhi, hlo = over("hhi", [P, FT, T], "arena"), over("hlo", [P, FT, T], "arena", FT * T)

        accf = acc[:].rearrange("p k t -> p (k t)")
        vlat = accf[:, 0:1024].rearrange("p (n f) -> p n f", n=2)
        pp = accf[:, 1024:1536].rearrange("p (r f) -> p r f", r=2)
        ppT = accf[:, 1536:2304].rearrange("p (r f) -> p r f", r=2)
        yf = y[:].rearrange("p n k t -> p (n k t)")
        k96 = yf[:, 2 * 1280:2 * 1280 + BH * SEQ].rearrange("p (h t) -> p h t", h=BH)
        ucp = accf[:, 0:4 * 286].rearrange("p (j t) -> p j t", j=4)
        ucs = accf[:, 1144:1144 + 4 * NB * 38].rearrange("p (j b t) -> p j b t", j=4, b=NB)
        sqc = accf[:, 0:4 * T].rearrange("p (j t) -> p j t", j=4)
        growk = sb("growk", [4, 2, T])
        m0 = sb("m0", [4, NB])
        mout = sb("mout", [4, 9])
        col4 = sb("col4", [P, 3, 100])
        wint = sb("wint", [P, H, NS])
        cnp = vm[:].rearrange("p h t -> p (h t)")[:, 0:H * W].rearrange("p (h d) -> p h d", h=H)

        zps = [ctx.enter_context(nc.psum_tensor(f"zps{i}", [P, 512], F32)) for i in range(3)]
        mps = [ctx.enter_context(nc.psum_tensor(f"mps{i}", [P, 512], F32)) for i in range(5)]
        banks = {}

        FIRST_FFN = BLOCKS.index(("ffn", 0))

        def ffn_done(q):
            if q < FT:
                return "pe_z", ("f3", q)
            d, j = divmod(16 * (q - FT) + 15, FT)
            return "pe_z", ("fo", d) if j == FT - 1 else ("ffn2", q - FT)

        FFN_BLOCKS = FT + 11

        pre = {n: ctx.enter_context(nc.semaphore(n)) for n in ("pre_dma", "pre_act", "pre_dve")}
        with nc.Block() as block:
            @block.sync
            def _(sp):
                sp.dma_start(const[:], a["consts"]).then_inc(pre["pre_dma"], 16)
                sp.dma_start(x[:], a["x"]).then_inc(pre["pre_dma"], 16)
                sp.dma_start(mod[:, 0:KC, :], a["c"]).then_inc(pre["pre_dma"], 16)
                sp.dma_start(pages[:], a["pages"]).then_inc(pre["pre_dma"], 16)
                sp.wait_ge(pre["pre_dma"], 64)
                sp.dma_start(a["o_y"], x[:]).then_inc(pre["pre_dma"], 16)

            @block.scalar
            def _(act):
                act.wait_ge(pre["pre_dma"], 64)
                nc.scalar.activation(siluc[:], mod[:, 0:KC, :], ACT.Silu).then_inc(pre["pre_act"], 1)
                act.wait_ge(pre["pre_act"], 1)
                nc.scalar.activation(c2[:, :, 0:9], siluc[:], ACT.Copy).then_inc(pre["pre_act"], 1)
                act.wait_ge(pre["pre_act"], 2)

            @block.vector
            def _(dve):
                dve.wait_ge(pre["pre_act"], 2)
                nc.vector.tensor_tensor(c2[:, :, 9:18], siluc[:], c2[:, :, 0:9], ALU.subtract).then_inc(pre["pre_dve"], 1)
                dve.wait_ge(pre["pre_dve"], 1)
        nc.all_engine_barrier()

        with nc.Fori(0, DEPTH) as layer:
            with nc.Block() as block:
                block_end = {}

                @block.tensor
                def _(pe):
                    zi, mi, bi, turned = [0], [0], [0], [0]
                    zfree, mfree = [None] * 3, [None] * 5

                    def bank(kind, name, freed_by):
                        i, frees, tiles = (zi, zfree, zps) if kind == "z" else (mi, mfree, mps)
                        n = i[0] % len(tiles)
                        i[0] += 1
                        if frees[n]:
                            pe.wait_ge(*at(*frees[n]))
                        frees[n] = freed_by
                        banks[name] = tiles[n]
                        return tiles[n]

                    def weights(want):
                        n = bi[0]
                        assert BLOCKS[n] == want, (BLOCKS[n], want)
                        bi[0] += 1
                        pe.wait_ge(C.sem(f"w_landed{n % RING}"), 16 * (n // RING + 1))
                        return n, ring[:, n % RING, :]

                    def group(kind, name, freed_by, mms, out=None):
                        ps = bank(kind, name, freed_by)
                        o = ps[:, 0:T] if out is None else out(ps)
                        for i, (l, r) in enumerate(mms):
                            last = nc.tensor.matmul(o, l, r, start=i == 0, stop=i == len(mms) - 1)
                        last.then_inc(*ev("pe_" + kind, name))

                    uk = [u[:, k, :] for k in range(KC)]

                    def in_tiles(names, free, first=False, between=None):
                        n, w = weights(("in",) + names)
                        for j, name in enumerate(names):
                            if between and j == 1:
                                between()
                            ps = bank("z", name, free[j])
                            for k in range(KC):
                                if first and j == 0:
                                    pe.wait_ge(*at("dve_u", ("p", k)))
                                last = nc.tensor.matmul(ps[:, 0:T], w[:, (j * KC + k) * P:(j * KC + k + 1) * P], uk[k],
                                                        start=k == 0, stop=k == KC - 1)
                            last.then_inc(*ev("pe_z", name))
                        block_end[n] = ("pe_z", names[-1])

                    def split_tile(q, n, j, name, freed_by, xh, xl, ready=None):
                        o, hi = bank("z", name, freed_by)[:, 0:T], high_buffer(q)[j]
                        pe.wait_ge(*at("act_hq", (q, j)))
                        for k in range(KC):
                            if ready:
                                pe.wait_ge(*at(ready, k))
                            nc.tensor.matmul(o, hi[:, k * P:(k + 1) * P], xh[:, k, :], start=k == 0, stop=False)
                            last = nc.tensor.matmul(o, hi[:, k * P:(k + 1) * P], xl[:, k, :], start=False, stop=False)
                        last.then_inc(*ev("pe_h", (q, j)))
                        pe.wait_ge(*at("pool_l", (q, j)))
                        for k in range(KC):
                            last = nc.tensor.matmul(o, wlx[:, n % RING, (j * KC + k) * P:(j * KC + k + 1) * P], xh[:, k, :], start=False, stop=k == KC - 1)
                        last.then_inc(*ev("pe_z", name))

                    def ada(a0, a1, through=True):
                        def turn(i):
                            turned[0] = i + 1
                            pe.wait_ge(*at("act_mod", i))
                            ps = bank("m", ("adaT", i), ("dve_mod", i))
                            r = 18 if ("ada", i) in SPLIT else 9
                            for j in range(2):
                                last = nc.tensor.transpose(ps[:, r * j:r * j + r], rowb[0:r, i % 2, j * P:(j + 1) * P], ident[0:r, 0:r])
                            last.then_inc(*ev("pe_m", ("adaT", i)))
                        for i in range(a0, a1):
                            n, w = weights(("ada", i))
                            if ("ada", i) in SPLIT:
                                q, ps = SPLIT.index(("ada", i)), bank("z", ("ada", i), ("act_mod", i))
                                for k in range(KC):
                                    if k % 4 == 0:
                                        pe.wait_ge(*at("pool_l", (q, k // 4)))
                                    hi, lo = whx[k // 4][:, k % 4 * 256:(k % 4 + 1) * 256], wlx[:, n % RING, k * 256:(k + 1) * 256]
                                    nc.tensor.matmul(ps[0:18, 0:256], c2[:, k, :], hi, start=k == 0, stop=False)
                                    last = nc.tensor.matmul(ps[0:18, 0:256], c2[:, k, :], lo, start=False, stop=k == KC - 1)
                                last.then_inc(*ev("pe_z", ("ada", i)))
                            else:
                                group("z", ("ada", i), ("act_mod", i), [(siluc[:, k, :], w[:, k * 256:(k + 1) * 256]) for k in range(KC)],
                                      lambda ps: ps[0:9, 0:256])
                            block_end[n] = ("pe_z", ("ada", i))
                            if turned[0] < i:
                                turn(i - 1)
                        if through:
                            turn(a1 - 1)

                    ada(0, 8)
                    in_tiles(("small", "kv0"), [("dve_s", "kr"), ("act_b", ("sq", 0))], first=True)
                    in_tiles(("kv1", "bq0"), [("act_b", ("sq", 1)), ("act_b", ("sq", 2))])
                    in_tiles(("bq1", "bq2"), [("act_b", ("sq", 3)), ("act_b", ("sq", 4))])
                    pe.wait_ge(*at("dve_s", "kr"))
                    group("m", "kr_swap", ("dve_b", "kr t2"), [(cs("swapB")[64:96, 64:96], krz[64:96, :])], lambda ps: ps[64:96, 0:T])
                    pe.wait_ge(*at("act_b", ("sq", 1)))
                    group("m", "rms_kv", ("act_b", "std kv"), [(ones, sq5[:, k, :]) for k in range(2)])

                    def rms_bq():
                        pe.wait_ge(*at("act_b", ("sq", 4)))
                        group("m", "rms_bq", ("act_b", "std bq"), [(ones, sq5[:, k, :]) for k in range(2, 5)])
                    in_tiles(("ao0", "ao1"), [("act_a", ("ao", 0)), ("act_a", ("ao", 1))], between=rms_bq)

                    n, w = weights(("uq",))
                    n2, w2 = weights(("uk",))
                    pe.wait_ge(*at("dve_b", ("bq", 2)))
                    for j in range(6):
                        src = [(w[:, (3 * j + k) * P:(3 * j + k + 1) * P] if 3 * j + k < 16 else
                                w2[:, 1024 + (3 * j + k - 16) * P:1024 + (3 * j + k - 15) * P], bqz[:, k, :]) for k in range(3)]
                        group("z", ("uq", j), ("dve_q", ("odd", j)) if j < 4 else ("act_q", ("qr", j - 4)), src)
                    block_end[n] = ("pe_z", ("uq", 5))
                    pe.wait_ge(*at("dve_b", ("ckv", 1)))
                    ps = bank("m", "ckvT", ("act_q", "ckvtok"))
                    for c in range(2):
                        last = nc.tensor.transpose(ps[0:NS, c * P:(c + 1) * P], ckv[:, c, SAMP], ident)
                    last.then_inc(*ev("pe_m", "ckvT"))
                    for r in range(2):
                        pe.wait_ge(*at("act_q", ("qr", r)))
                        group("m", ("qr_swap", r), ("dve_q", ("t2", r)), [(cs("swapB"), qr[:, r, :])])
                    for j in range(4):
                        group("z", ("kn", j), ("dve_q", ("kodd", j)),
                              [(w2[:, c * 512 + j * P:c * 512 + (j + 1) * P], ckv[:, c, 0:SEQ]) for c in range(2)], lambda ps: ps[:, 0:SEQ])
                    block_end[n2] = ("pe_z", ("kn", 3))
                    pe.wait_ge(C.sem("in_wuv"), 16)
                    for t in range(2):
                        group("z", ("vt", t), ("act_q", ("vlat", t)), [(ckv[:, c, t * P:(t + 1) * P], wuv[:, c, :]) for c in range(2)],
                              lambda ps: ps[:, :])
                    n, w = weights(("ukT",))
                    pe.wait_ge(*at("dve_q", ("odd", 3)))
                    for c in range(2):
                        ps = bank("z", ("qa", c), ("dve_q", ("qabs", c)))
                        for h in range(BH):
                            last = nc.tensor.matmul(ps[:, h * NS:(h + 1) * NS], w[0:64, h * KVR + c * P:h * KVR + (c + 1) * P],
                                                    q96[0:64, h, SAMP], start=True, stop=True)
                        last.then_inc(*ev("pe_z", ("qa", c)))
                    block_end[n] = ("pe_z", ("qa", 1))

                    def prompt_scores(h):
                        if h == 0:
                            pe.wait_ge(*at("dve_q", "qpes"))
                            pe.wait_ge(*at("pool_k", "kpe all"))
                            pe.wait_ge(*at("dve_q", ("kodd", 3)))
                        for i in range(2):
                            group("m", ("ps", h, i), ("dve_pa", ("s", h, i)), [(q96[0:96, h, i * P:(i + 1) * P], k96[0:96, h, 0:(i + 1) * P])],
                                  lambda ps: ps[:, 0:(i + 1) * P])

                    def prompt_values(h):
                        for i in range(2):
                            pe.wait_ge(*at("dve_pa", ("norm", h, i)))
                            ps = bank("m", ("ppT", h, i), ("act_pa", ("ppT", h, i)))
                            for k in range(i + 1):
                                last = nc.tensor.transpose(ps[:, k * P:(k + 1) * P], pp[:, i, k * P:(k + 1) * P], ident)
                            last.then_inc(*ev("pe_m", ("ppT", h, i)))

                    def prompt_out(h):
                        if h == 0:
                            pe.wait_ge(*at("act_q", ("vlat", 1)))
                        o = 64 * (h % 2)
                        ps = bank("m", ("po", h), ("act_pa", ("yb", h)))
                        pe.wait_ge(*at("act_pa", ("ppT", h, 1)))
                        s = ppT[:, h % 2, :]
                        nc.tensor.matmul(ps[o:o + 64, 0:SEQ], vlat[:, 0, h * VD:(h + 1) * VD], s[:, 0:SEQ], start=True, stop=False)
                        nc.tensor.matmul(ps[o:o + 64, P:SEQ], vlat[:, 1, h * VD:(h + 1) * VD], s[:, SEQ:SEQ + P], start=False,
                                         stop=True).then_inc(*ev("pe_m", ("po", h)))

                    def conv_tiles(j):
                        in_tiles((f"cg{j}", f"ca{j}"), [("act_c", ("sg", j)), ("dve_c", ("glu2", j))])

                    for i in range(BH):
                        if i < len(A_STREAM):
                            xx, j = A_STREAM[i]
                            fr = "dve_a" if xx == "aq" else "act_a"
                            in_tiles((f"{xx}{j}", f"{xx}{j + 1}"), [(fr, (xx, j)), (fr, (xx, j + 1))])
                        prompt_scores(i)
                        if i >= 1:
                            prompt_values(i - 1)
                        if i >= 2:
                            prompt_out(i - 2)
                    conv_tiles(0)
                    prompt_values(BH - 1)
                    prompt_out(BH - 2)
                    prompt_out(BH - 1)

                    def to_tokens(X, t):
                        t0, tn = TOK[t]
                        for s, src in (("k", km), ("v", vm)):
                            if t == 0:
                                pe.wait_ge(*at("dve_dk" if X == "d" and s == "k" else f"act_{X}", (X + s, 3)))
                            ps = bank("m", (X, s + "T", t), (f"act_{X}t" if s == "k" else f"dve_{X}t", (s, t)))
                            for h in range(H):
                                last = nc.tensor.transpose(ps[0:tn, h * P:(h + 1) * P], src[:, h, t0:t0 + tn], ident)
                            last.then_inc(*ev("pe_m", (X, s + "T", t)))

                    def scores(X, h):
                        if h == 0:
                            pe.wait_ge(*at("dve_a" if X == "a" else "dve_dk", (X + "q", 3)))
                        ps = bank("m", (X, "st", h), (f"dve_{X}w", ("w2", h)))
                        nc.tensor.matmul(ps[:, 0:256], km[:, h, 0:P], qm[:, h, 0:SEQ], start=True, stop=True)
                        nc.tensor.matmul(ps[:, 256:384], km[:, h, P:SEQ], qm[:, h, P:SEQ], start=True, stop=True)
                        nc.tensor.matmul(ps[0:NS, 384:448], km[:, h, SAMP], qm[:, h, SAMP], start=True,
                                         stop=True).then_inc(*ev("pe_m", (X, "st", h)))

                    def outputs(X, hp, width):
                        pe.wait_ge(*at(f"dve_{X}t", ("v", 2)))
                        if hp == 0:
                            pe.wait_ge(*at(f"dve_{X}w", "qz"))
                            pe.wait_ge(C.sem(f"in_state_{X}"), 16)
                        for t in range(3):
                            ps = bank("m", (X, "num", t, hp), (f"dve_{X}h", ("h", t, hp)))
                            for i in range(2):
                                h = 2 * hp + i
                                pe.wait_ge(*at(f"dve_{X}w", ("w2", h)))
                                w_, o = wb[:, h % 2, :], ps[0:TOK[t][1], i * width:(i + 1) * width]
                                if t == 0:
                                    mms = [(w_[:, 0:P], vtok[:, 0, h, 0:width])]
                                elif t == 1:
                                    mms = [(w_[:, P:256], vtok[:, 0, h, 0:width]), (w_[:, 256:384], vtok[:, 1, h, 0:width])]
                                else:
                                    mms = [(w_[0:NS, 384:448], vtok[0:NS, 2, h, 0:width])]
                                    mms += [(qz[:, b * 256 + h * NS:b * 256 + (h + 1) * NS], state[:, b, h, 0:width]) for b in range(NB)]
                                for k, (l, r) in enumerate(mms):
                                    last = nc.tensor.matmul(o, l, r, start=k == 0, stop=k == len(mms) - 1)
                            last.then_inc(*ev("pe_m", (X, "num", t, hp)))

                    def turn_heads(X, t):
                        t0, tn = TOK[t]
                        pe.wait_ge(*at(f"dve_{X}h", ("n", t, 3)))
                        ps = bank("m", (X, "hT", t), (f"dve_{X}y", t))
                        for h in range(H):
                            last = nc.tensor.transpose(ps[:, h * P:h * P + tn], hh[0:tn, t, h, :], ident[0:tn, 0:tn])
                        last.then_inc(*ev("pe_m", (X, "hT", t)))

                    def state_prompt(X, width):
                        for hp in range(2):
                            pe.wait_ge(*at(f"pool_{X}k", 1))
                            ps = bank("m", (X, "cp", hp), (f"act_{X}c", hp))
                            for i in range(2):
                                h = 2 * hp + i
                                for t in range(2):
                                    last = nc.tensor.matmul(ps[:, i * width:(i + 1) * width], ktok[:, t, h, :], vtok[:, t, h, 0:width],
                                                            start=t == 0, stop=t == 1)
                            last.then_inc(*ev("pe_m", (X, "cp", hp)))

                    def state_sample(X, b, width):
                        pe.wait_ge(*at(f"pool_{X}m", b))
                        for hp in range(2):
                            ps = bank("m", (X, "cs", b, hp), (f"dve_{X}c", (b, 2 * hp + 1)))
                            for i in range(2):
                                h = 2 * hp + i
                                last = nc.tensor.matmul(ps[:, i * width:(i + 1) * width], kmb[0:NS, b % 2, h * P:(h + 1) * P],
                                                        vtok[0:NS, 2, h, 0:width], start=True, stop=True)
                            last.then_inc(*ev("pe_m", (X, "cs", b, hp)))

                    def gate_columns():
                        pe.wait_ge(*at("dve_g", "r4"))
                        pe.wait_ge(*at("pool_z", "r4"))
                        for t, (t0, tn) in enumerate(TOK):
                            ps = bank("m", ("g4T", t), ("act_g", ("exp", t)))
                            nc.tensor.transpose(ps[0:tn, 0:100], r4[0:100, t0:t0 + tn], ident[0:100, 0:100]).then_inc(*ev("pe_m", ("g4T", t)))
                        ps = bank("m", "wint", ("act_g", "wint"))
                        for h in range(H):
                            last = nc.tensor.matmul(ps[:, h * NS:(h + 1) * NS], ident[0:4, h:h + 1].to_broadcast([4, P]), growk[0:4, 1, SAMP],
                                                    start=True, stop=True)
                        last.then_inc(*ev("pe_m", "wint"))

                    def gate_row(h):
                        group("m", ("rb", h), ("dve_aw", ("e2", h)), [(ident[0:4, h:h + 1].to_broadcast([4, P]), growk[0:4, 0, :])])

                    gate_columns()
                    for t in range(3):
                        to_tokens("a", t)
                    gate_row(0)
                    scores("a", 0)
                    gate_row(1)
                    scores("a", 1)
                    conv_tiles(1)
                    outputs("a", 0, W)
                    gate_row(2)
                    scores("a", 2)
                    gate_row(3)
                    scores("a", 3)
                    conv_tiles(2)
                    state_prompt("a", W)
                    conv_tiles(3)
                    outputs("a", 1, W)

                    def swap(x_, h):
                        pe.wait_ge(*at("act_dz", (x_, h)))
                        group("m", ("sw", x_, h), ("dve_dk", ("t2", x_, h)), [(cs("swapD"), tmp[:, h % 2, :])])
                    for x_ in ("dk", "dq", "dv", "dg"):
                        for j in (0, 2):
                            s = "act_dz" if x_ in ("dk", "dq") else "act_d"
                            in_tiles((f"{x_}{j}", f"{x_}{j + 1}"), [(s, (x_, j)), (s, (x_, j + 1))])
                            if (x_, j) == ("dk", 0):
                                for b in range(NB):
                                    state_sample("a", b, W)
                                for t in range(3):
                                    turn_heads("a", t)
                            if s == "act_dz":
                                swap(x_, j)
                                swap(x_, j + 1)

                    def channel_sum(name, src, k, ready, freed_by):
                        pe.wait_ge(*at(*ready))
                        group("m", name, freed_by, [(ones, src[:, j, :]) for j in range(k)])

                    def gate(n, i):
                        names = (f"g{n}_{i}", f"g{n}_{i + 1}")
                        if ("in",) + names in SPLIT:
                            q = SPLIT.index(("in",) + names)
                            k, w = weights(("in",) + names)
                            for j in range(2):
                                split_tile(q, k, j, names[j], ("act_gt", (n, i + j)), uhi, ulo, "dve_ul" if q == 0 and j == 0 else None)
                            block_end[k] = ("pe_z", names[1])
                            return
                        in_tiles((f"g{n}_{i}", f"g{n}_{i + 1}"), [("act_gt", (n, i)), ("act_gt", (n, i + 1))])

                    def branch(n, half):
                        k, w = weights(("branch", n, half))
                        pe.wait_ge(*at(*{0: ("dve_ay", 2), 2: ("act_cy", 3), 3: ("dve_dy", 2), 1: ("act_s", "ys")}[n]))
                        if n == 1:
                            pe.wait_ge(*at("act_pa", ("yb", BH - 1)))
                        for i in range(4):
                            group("z", ("br", n, half + i), ("dve_br", (n, half + i)),
                                  [(w[:, (i * 4 + c) * P:(i * 4 + c + 1) * P], y[:, n, c, :]) for c in range(4)])
                        block_end[k] = ("pe_z", ("br", n, half + 3))

                    def gated(n, half):
                        gate(n, half)
                        gate(n, half + 2)
                        branch(n, half)

                    def slot(b):
                        for kind, *which in SLOTS[b]:
                            if kind == "gate":
                                gate(*which)
                            elif kind == "branch":
                                branch(*which)
                            else:
                                ada(which[0], which[0] + 1, through=False)

                    def sample_scores(b):
                        r = b % 2
                        pe.wait_ge(C.sem(f"in_cache{r}"), 16 * NPG * (b // 2 + 1))
                        for g in range(2):
                            group("m", ("ss", b, g), ("act_s", ("e", b, g)),
                                  [(qabs[:, 0, b, :], cache[:, r, 4 * g:4 * g + 4, 0:P]),
                                   (qabs[:, 1, b, :], cache[:, r, 4 * g:4 * g + 4, P:2 * P]),
                                   (qpes[64:96, b, :], cache[64:96, r, 4 * g:4 * g + 4, 512:640])], lambda ps: ps[0:NS, :])
                        group("m", ("ss", b, 2), ("dve_s2", ("new", b)),
                              [(qabs[:, 0, b, :], ckv[:, 0, SAMP]), (qabs[:, 1, b, :], ckv[:, 1, SAMP]), (qpes[64:96, b, :], kpe[64:96, SAMP])],
                              lambda ps: ps[0:NS, 0:NS])

                    def sample_turn(b):
                        pe.wait_ge(*at("act_s", ("e", b, 2)))
                        ps = bank("m", ("sT", b), ("act_s", ("pT", b)))
                        for k in range(NPG):
                            last = nc.tensor.transpose(ps[:, k * NS:(k + 1) * NS], pb[0:NS, b % 2, k * P:(k + 1) * P], ident[0:NS, 0:NS])
                        last.then_inc(*ev("pe_m", ("sT", b)))
                        ps = bank("m", ("snT", b), ("dve_s2", ("pnT", b)))
                        nc.tensor.transpose(ps[0:NS, 0:NS], pb[0:NS, b % 2, PAST:PAST + NS], ident[0:NS, 0:NS]).then_inc(*ev("pe_m", ("snT", b)))

                    def sample_values(b):
                        r = b % 2
                        pe.wait_ge(*at("act_s", ("pT", b)))
                        pe.wait_ge(*at("dve_s2", ("pnT", b)))
                        group("m", ("so", b), ("dve_s2", ("o", b)),
                              [(pT[:, r, k * NS:(k + 1) * NS], cache[:, r, k, 2 * P:4 * P]) for k in range(NPG)]
                              + [(pT[0:NS, r, 512:576], ckvtok[0:NS, :])], lambda ps: ps[0:NS, 0:KVR])

                    def sample_back(b):
                        pe.wait_ge(*at("dve_s2", ("o", b)))
                        ps = bank("m", ("soT", b), ("act_s", ("oT", b)))
                        for c in range(2):
                            last = nc.tensor.transpose(ps[:, c * NS:(c + 1) * NS], olat[0:NS, b % 2, c * P:(c + 1) * P], ident[0:NS, 0:NS])
                        last.then_inc(*ev("pe_m", ("soT", b)))

                    def sample_out():
                        pe.wait_ge(*at("act_s", ("oT", NB - 1)))
                        ps = bank("m", "ys", ("act_s", "ys"))
                        for h in range(BH):
                            o = 64 * (h % 2)
                            for c in range(2):
                                last = nc.tensor.matmul(ps[o:o + 64, (h // 2) * NS:(h // 2 + 1) * NS], wuv[:, c, h * VD:(h + 1) * VD],
                                                        olatT[:, c, h, :], start=c == 0, stop=c == 1)
                        last.then_inc(*ev("pe_m", "ys"))

                    gated(0, 0)
                    for t in range(3):
                        to_tokens("d", t)
                    scores("d", 0)
                    scores("d", 1)
                    pe.wait_ge(*at("pool_c", ("sum", CW - 1)))
                    channel_sum("conv sum", y[:, 2], 4, ("dve_c", ("tap", 3, CW - 1)), ("dve_c", ("mu", 3)))
                    gated(0, 4)
                    outputs("d", 0, P)
                    scores("d", 2)
                    scores("d", 3)
                    channel_sum("conv var", sqc, 4, ("act_cy", ("sq", 3)), ("act_cy", "std"))
                    outputs("d", 1, P)
                    state_prompt("d", P)
                    gated(2, 0)
                    state_sample("d", 0, P)
                    gate(2, 4)
                    for b in range(1, NB):
                        state_sample("d", b, P)
                    for t in range(3):
                        turn_heads("d", t)
                    gate(2, 6)
                    branch(2, 4)
                    for b in range(NB):
                        if b >= 2:
                            sample_back(b - 2)
                        if b >= 1:
                            sample_turn(b - 1)
                        sample_scores(b)
                        if b >= 1:
                            sample_values(b - 1)
                        slot(b)
                    sample_back(NB - 2)
                    sample_turn(NB - 1)
                    sample_values(NB - 1)
                    slot(NB)
                    sample_back(NB - 1)
                    sample_out()
                    branch(1, 0)
                    branch(1, 4)

                    def mean_part(which, k):
                        if k == 0:
                            bank("m", ("mean", which), ("dve_r", ("mu", which, KC - 1)))
                        pe.wait_ge(*at("dve_r", ("r", which, k)))
                        nc.tensor.matmul(banks["mean", which][:, 0:T], ones, u[:, k, :], start=k == 0, stop=False)

                    def norm_sums(which, filler1, filler2):
                        ps = banks["mean", which]
                        pe.wait_ge(*at("dve_r", ("r", which, KC - 1)))
                        for k in range(KC - 2, KC):
                            last = nc.tensor.matmul(ps[:, 0:T], ones, u[:, k, :], start=False, stop=k == KC - 1)
                        last.then_inc(*ev("pe_m", ("mean", which)))
                        if filler1:
                            ada(*filler1)
                        ps = bank("m", ("var", which), ("act_n", ("std", which)))
                        for k in range(KC):
                            pe.wait_ge(*at("act_n", ("sq", which, k)))
                            last = nc.tensor.matmul(ps[:, 0:T], ones, acc[:, k, :], start=k == 0, stop=k == KC - 1)
                        last.then_inc(*ev("pe_m", ("var", which)))
                        if filler2:
                            ada(*filler2)

                    for i in range(4):
                        n, w = weights(("out", i))
                        q = SPLIT.index(("out", i))
                        for j in range(2):
                            d = 2 * i + j
                            split_tile(q, n, j, ("wo", d), ("dve_r", ("g", 1, d)), ghi, glo, "dve_gl" if d == 0 else None)
                            if d >= 2:
                                mean_part(1, d - 2)
                        block_end[n] = ("pe_z", ("wo", 2 * i + 1))

                    norm_sums(1, (18, 20), (20, 24))

                    def ffn_weights(q):
                        assert BLOCKS[bi[0]] == (("ffn", q) if q < FT else ("ffn2", q - FT))
                        bi[0] += 1
                        pe.wait_ge(*at("dve_w", q))
                        return whi[q % 2], wlo[q % 2]

                    def three(ps, hi, lo, k, xh, xl, start, stop):
                        o, cols = ps[:, 0:T], slice(k * P, (k + 1) * P)
                        nc.tensor.matmul(o, hi[:, cols], xh, start=start, stop=False)
                        nc.tensor.matmul(o, hi[:, cols], xl, start=False, stop=False)
                        return nc.tensor.matmul(o, lo[:, cols], xh, start=False, stop=stop)

                    for j in range(FT):
                        hi, lo = ffn_weights(j)
                        for i in range(2):
                            name = (("f1", "f3")[i], j)
                            ps = bank("z", name, ("act_f", j) if i == 0 else ("dve_f", ("h", j)))
                            if i == 1:
                                pe.wait_ge(*at("pool_w", j))
                            for k in range(KC):
                                if j == 0 and i == 0:
                                    pe.wait_ge(*at("dve_x", k))
                                last = three(ps, hi, lo, i * KC + k, xhi[:, k, :], xlo[:, k, :], k == 0, k == KC - 1)
                            last.then_inc(*ev("pe_z", name))
                    pe.wait_ge(*at("dve_f", FT - 1))
                    for d in range(KC):
                        ps = bank("z", ("fo", d), ("dve_r", ("g", 2, d)))
                        for j in range(FT):
                            i = d * FT + j
                            if i % 16 == 0:
                                hi, lo = ffn_weights(FT + i // 16)
                            if i % 16 == 8:
                                pe.wait_ge(*at("pool_w", FT + i // 16))
                            last = three(ps, hi, lo, i % 16, hhi[:, j, :], hlo[:, j, :], j == 0, j == FT - 1)
                            if j == FT - 1:
                                last.then_inc(*ev("pe_z", ("fo", d)))
                            elif i % 16 == 15:
                                last.then_inc(*ev("pe_z", ("ffn2", i // 16)))
                        if d >= 2:
                            mean_part(2, d - 2)
                    norm_sums(2, None, None)
                    assert bi[0] == NBLK

                @block.sync
                def _(sp):
                    lay = bass.ds(layer, 1)

                    def dram(name, *rest):
                        return a[name][(lay,) + tuple(slice(None) for _ in range(len(a[name].shape) - 1))]

                    def of(ap, names):
                        return ap.rearrange(f"l {names} -> (l {names.split()[0]}) " + " ".join(names.split()[1:]))


                    def load_block(n):
                        if n >= RING and n - RING < FIRST_FFN:
                            sp.wait_ge(*at(*block_end[n - RING]))
                        elif n >= RING:
                            sp.wait_ge(*at("dve_w", n - RING - FIRST_FFN))
                            sp.wait_ge(*at("pool_w", n - RING - FIRST_FFN))
                        src = a["wpack"][lay, n:n + 1, :, :].rearrange("l n p f -> (l n p) f")
                        sp.dma_start(ring[:, n % RING, :], src).then_inc(C.sem(f"w_landed{n % RING}"), 16)

                    def load_pages(b):
                        r = b % 2
                        if b >= 2:
                            sp.wait_ge(*at("pe_m", ("so", b - 2)))
                        else:
                            sp.wait_ge(*at("dve_dc", (NB - 1, 3)))
                            sp.wait_ge(*at("dve_dy", 2))
                            sp.wait_ge(C.sem("out_state_d"), 16 * 2)
                        for g in range(NPG):
                            pg = sp.value_load(pages[0:1, b * NPG + g:b * NPG + g + 1], min_val=0, max_val=POOL - 1)
                            sp.dma_start(cache[:, r, g, :], a["cache"][lay, bass.ds(pg, 1), :, :].rearrange("l n p f -> (l n p) f")
                                         ).then_inc(C.sem(f"in_cache{r}"), 16)

                    first_gate = BLOCKS.index(("in", "g0_0", "g0_1"))
                    for n in range(NBLK):
                        load_block(n)
                        if n == 0:
                            sp.dma_start(smallw[:], of(dram("small"), "p f")).then_inc(C.sem("in_small"), 16)
                        if n == 3:
                            sp.dma_start(m0[:], of(dram("m0"), "h b")).then_inc(C.sem("in_m0"), 16)
                            sp.dma_start(wuv[:], of(dram("wuv"), "p c f")).then_inc(C.sem("in_wuv"), 16)
                        if BLOCKS[n] == ("in", "ak0", "ak1"):
                            sp.dma_start(state[:], of(dram("stateA"), "p b h d")).then_inc(C.sem("in_state_a"), 16)
                        if BLOCKS[n] == ("in", "aq0", "aq1"):
                            sp.wait_ge(*at("dve_b", ("ckv", 1)))
                            sp.wait_ge(*at("dve_b", "kpe"))
                            sp.dma_start(of(dram("o_rows_c"), "p c t"), ckv[:]).then_inc(C.sem("out_rows"), 16)
                            sp.dma_start(of(dram("o_rows_k"), "p t"), kpe[64:96, :]).then_inc(C.sem("out_rows"), 16)
                        if BLOCKS[n] == ("in", "cg3", "ca3"):
                            sp.wait_ge(*at("pe_m", ("po", BH - 1)))
                            sp.dma_start(ucs[:, :, :, 0:CW - 1], of(dram("hist"), "p j b t")).then_inc(C.sem("in_hist"), 16)
                        if BLOCKS[n] == ("in", "dq0", "dq1"):
                            sp.wait_ge(*at("act_ac", 1))
                            sp.dma_start(of(dram("o_cn_p"), "p h d"), cnp).then_inc(C.sem("out_state_a"), 16)
                            sp.wait_ge(*at("dve_g", "mout"))
                            sp.dma_start(of(dram("o_m"), "h b"), mout[:]).then_inc(C.sem("out_m"), 16)
                            sp.wait_ge(*at("dve_c", ("glu2", 3)))
                            sp.wait_ge(C.sem("in_hist"), 16)
                            sp.dma_start(of(dram("o_conv_p"), "p j t"), ucp[:, :, SEQ:SEQ + CW - 1]).then_inc(C.sem("out_conv"), 16)
                            sp.dma_start(of(dram("o_conv_s"), "p j b t"), ucs[:, :, :, TS:TS + CW - 1]).then_inc(C.sem("out_conv"), 16)
                        if BLOCKS[n] == ("in", "dq2", "dq3"):
                            sp.wait_ge(*at("dve_ac", (NB - 1, 3)))
                            sp.dma_start(of(dram("o_cn_s"), "p b h d"), state[:]).then_inc(C.sem("out_state_a"), 16)
                        if BLOCKS[n] == ("in", "dg0", "dg1"):
                            sp.wait_ge(C.sem("out_state_a"), 32)
                            sp.dma_start(state[:, :, :, 0:P], of(dram("stateD"), "p b h d")).then_inc(C.sem("in_state_d"), 16)
                        if BLOCKS[n] == ("branch", 2, 4):
                            sp.wait_ge(*at("act_dc", 1))
                            sp.dma_start(of(dram("o_ret_p"), "p h d"), cnp[:, :, 0:P]).then_inc(C.sem("out_state_d"), 16)
                            sp.wait_ge(*at("dve_dc", (NB - 1, 3)))
                            sp.dma_start(of(dram("o_ret_s"), "p b h d"), state[:, :, :, 0:P]).then_inc(C.sem("out_state_d"), 16)
                            load_pages(0)
                        if BLOCKS[n] == ("out", 0):
                            sp.wait_ge(*at("pe_z", "g1_7"))
                            sp.dma_start(x[:], a["o_y"]).then_inc(C.sem("in_x"), 16)
                        if n == SLOT_START[0] + 1:
                            load_pages(1)
                        for b in range(2, NB):
                            if n == SLOT_START[b - 1] + RING - 1:
                                load_pages(b)
                    for k in (0, KC // 2):
                        sp.wait_ge(*at("act_n", ("x", 2, k + KC // 2 - 1)))
                        sp.dma_start(a["o_y"][:, k:k + KC // 2, :], x[:, k:k + KC // 2, :]).then_inc(C.sem("out_y"), 16)
                    sp.wait_ge(C.sem("out_y"), 32)
                    sp.wait_ge(C.sem("out_rows"), 32)
                    sp.wait_ge(C.sem("out_m"), 16)
                    sp.wait_ge(C.sem("out_conv"), 32)
                    sp.wait_ge(C.sem("out_state_a"), 32)
                    sp.wait_ge(C.sem("out_state_d"), 32)

                @block.scalar
                def _(act):
                    act.wait_ge(C.sem("in_small"), 16)

                    def go(sem, label, out, in_, func, **kw):
                        in_turn(act, "act")
                        return nc.scalar.activation(out, in_, func, **kw).then_inc(*ev(sem, label))

                    def z(name):
                        act.wait_ge(*at("pe_z", name))
                        return banks[name]

                    def m(name):
                        act.wait_ge(*at("pe_m", name))
                        return banks[name]

                    def ada(a0, a1):
                        for i in range(a0, a1):
                            ps = z(("ada", i))
                            if i >= 2:
                                act.wait_ge(*at("pe_m", ("adaT", i - 2)))
                            r = 18 if ("ada", i) in SPLIT else 9
                            go("act_mod", i, rowb[0:r, i % 2, :], ps[0:r, 0:256], ACT.Copy)

                    def high(q, halves=(0, 1)):
                        n = BLOCKS.index(SPLIT[q])
                        act.wait_ge(C.sem(f"w_landed{n % RING}"), 16 * (n // RING + 1))
                        before = [p for p in range(q) if high_buffer(p) is high_buffer(q)]
                        for i in halves:
                            if before and SPLIT[before[-1]][0] == "ada":
                                act.wait_ge(*at("pe_z", SPLIT[before[-1]]))
                            elif before:
                                act.wait_ge(*at("pe_h", (before[-1], i)))
                                act.wait_ge(*at("pool_l", (before[-1], i)))
                            elif high_buffer(q) is whx:
                                act.wait_ge(*at("dve_dc", (NB - 1, 3)))
                                act.wait_ge(*at("dve_dy", 2))
                            go("act_hq", (q, i), high_buffer(q)[i][:], ring[:, n % RING, i * 1024:(i + 1) * 1024], ACT.Copy)

                    ada(0, 8)
                    for i, name in enumerate(("kv0", "kv1", "bq0", "bq1", "bq2")):
                        ps = z(name)
                        go("act_b", ("z", i), ckv[:, i, :] if i < 2 else bqz[:, i - 2, :], ps[:, 0:T], ACT.Identity, bias=sw(name))
                        go("act_b", ("sq", i), sq5[:, i, :], ps[:, 0:T], ACT.Square, bias=sw(name))
                    go("act_b", "std kv", std[:], m("rms_kv")[:, 0:T], ACT.Sqrt, bias=cs("eps")[:, 1:2], scale=1.0 / KVR)
                    go("act_b", "std bq", tmp[:, 0, :], m("rms_bq")[:, 0:T], ACT.Sqrt, bias=cs("eps")[:, 1:2], scale=1.0 / QR)
                    for h in (0, 1):
                        go("act_a", ("ao", h), y[:, 0, h, :], z(f"ao{h}")[:, 0:T], ACT.Sigmoid, bias=sw(f"ao{h}"))
                    for j in range(4):
                        go("act_q", ("even", j), q96[0:64, 2 * j, :], z(("uq", j))[0:64, 0:T], ACT.Copy)
                    for r in range(2):
                        go("act_q", ("qr", r), qr[:, r, :], z(("uq", 4 + r))[:, 0:T], ACT.Copy)
                    go("act_q", "ckvtok", ckvtok[0:NS, :], m("ckvT")[0:NS, 0:KVR], ACT.Copy)
                    for j in range(4):
                        go("act_q", ("keven", j), k96[0:64, 2 * j, :], z(("kn", j))[0:64, 0:SEQ], ACT.Copy)
                    for t in range(2):
                        go("act_q", ("vlat", t), vlat[:, t, :], z(("vt", t))[:, :], ACT.Copy)
                    act.wait_ge(*at("dve_g", "abs"))
                    go("act_g", "e", grow[:, 2, :], grow[:, 1, :], ACT.Exp, scale=-1.0)
                    act.wait_ge(*at("act_g", "e"))
                    go("act_g", "ln", grow[:, 3, :], grow[:, 2, :], ACT.Ln, bias=cs("eps")[0:4, 2:3])

                    def prompt_exp(h):
                        for i in range(2):
                            act.wait_ge(*at("dve_pa", ("nm", h, i)))
                            go("act_pa", ("e", h, i), pp[:, i, 0:(i + 1) * P], pp[:, i, 0:(i + 1) * P], ACT.Exp,
                               bias=stats[:, 4 + i:5 + i], scale=BSCALE, accum_out=stats[:, 8 + i:9 + i])

                    def prompt_turned(h):
                        if h >= 2:
                            act.wait_ge(*at("pe_m", ("po", h - 2)))
                        go("act_pa", ("ppT", h, 0), ppT[:, h % 2, 0:P], m(("ppT", h, 0))[:, 0:P], ACT.Copy)
                        go("act_pa", ("ppT", h, 1), ppT[:, h % 2, P:3 * P], m(("ppT", h, 1))[:, 0:2 * P], ACT.Copy)

                    def prompt_y(h):
                        o = 64 * (h % 2)
                        go("act_pa", ("yb", h), y[o:o + 64, 1, h // 2, 0:SEQ], m(("po", h))[o:o + 64, 0:SEQ], ACT.Copy)

                    act.wait_ge(*at("pe_z", ("uq", 5)))
                    act.wait_ge(*at("dve_q", ("t1", 1)))
                    for i in range(BH):
                        xx, j = A_STREAM[i] if i < len(A_STREAM) else ("", 0)
                        for h in (j, j + 1):
                            if xx == "ak" or xx == "av":
                                dst = (km if xx == "ak" else vm)[:, h, :]
                                go("act_a", (xx, h), dst, z(f"{xx}{h}")[:, 0:T], ACT.Identity, bias=sw(f"{xx}{h}"))
                            elif xx == "ao":
                                go("act_a", (xx, h), y[:, 0, h, :], z(f"{xx}{h}")[:, 0:T], ACT.Sigmoid, bias=sw(f"{xx}{h}"))
                        prompt_exp(i)
                        if i >= 1:
                            prompt_turned(i - 1)
                        if i >= 2:
                            prompt_y(i - 2)

                    def conv_gate(j):
                        go("act_c", ("sg", j), gt[:, j, :], z(f"cg{j}")[:, 0:T], ACT.Sigmoid, bias=sw(f"cg{j}"))

                    conv_gate(0)
                    prompt_turned(BH - 1)
                    prompt_y(BH - 2)
                    prompt_y(BH - 1)

                    for t, (t0, tn) in enumerate(TOK):
                        ps = m(("g4T", t))
                        go("act_g", ("col", t), col4[0:tn, t, 0:32], ps[0:tn, 0:32], ACT.Copy)
                        go("act_g", ("exp", t), col4[0:tn, t, 32:100], ps[0:tn, 32:100], ACT.Exp)
                    go("act_g", "wint", wint[:].rearrange("p h t -> p (h t)"), m("wint")[:, 0:H * NS], ACT.Exp)

                    def tokens(X, t):
                        tn = TOK[t][1]
                        go(f"act_{X}t", ("k", t), ktok[0:tn, t].rearrange("p h d -> p (h d)"), m((X, "kT", t))[0:tn, :], ACT.Copy)

                    def decay(h):
                        act.wait_ge(*at("dve_aw", ("e2", h)))
                        go("act_aw", ("e1", h), eb[:, h % 2, 0:384], eb[:, h % 2, 0:384], ACT.Exp)
                        go("act_aw", ("e2", h), eb[0:NS, h % 2, 384:448], eb[0:NS, h % 2, 384:448], ACT.Exp)

                    def head_std(X, t):
                        tn = TOK[t][1]
                        act.wait_ge(*at(f"dve_{X}h", ("mv", t, 3)))
                        go(f"act_{X}h", t, stats[0:tn, 64 + 4 * t:68 + 4 * t], stats[0:tn, 32 + 8 * t:40 + 8 * t].rearrange("p (h s) -> p h s", h=H)[:, :, 1],
                           ACT.Sqrt, bias=cs("eps")[0:tn, 0:1])

                    def prompt_state(X, width):
                        for hp in range(2):
                            if hp == 0:
                                act.wait_ge(*at("pe_m", (X, "vT", 2)))
                            go(f"act_{X}c", hp, cnp[:, 2 * hp:2 * hp + 2, 0:width], m((X, "cp", hp))[:, 0:2 * width].rearrange("p (h d) -> p h d", h=2), ACT.Copy)

                    for t in range(3):
                        tokens("a", t)
                    decay(0)
                    decay(1)
                    conv_gate(1)
                    decay(2)
                    decay(3)
                    conv_gate(2)
                    prompt_state("a", W)
                    conv_gate(3)
                    for t in range(3):
                        head_std("a", t)

                    for x_ in ("dk", "dq", "dv", "dg"):
                        for h in range(H):
                            if x_ in ("dk", "dq"):
                                i = h + (4 if x_ == "dq" else 0)
                                if i >= 2:
                                    px, ph = ("dk", i - 2) if i < 6 else ("dq", i - 6)
                                    act.wait_ge(*at("dve_dk", ("t2", px, ph)))
                                    act.wait_ge(*at("pe_m", ("sw", px, ph)))
                                go("act_dz", (x_, h), tmp[:, h % 2, :], z(f"{x_}{h}")[:, 0:T], ACT.Identity, bias=sw(f"{x_}{h}"))
                            elif x_ == "dv":
                                if h == 0:
                                    act.wait_ge(C.sem("out_state_a"), 16 * 2)
                                go("act_d", (x_, h), vm[:, h, :], z(f"{x_}{h}")[:, 0:T], ACT.Identity, bias=sw(f"{x_}{h}"))
                            else:
                                go("act_d", (x_, h), y[:, 3, h, :], z(f"{x_}{h}")[:, 0:T], ACT.Silu, bias=sw(f"{x_}{h}"))

                    gate_seq = [(n, d) for n in GATE_ORDER[:3] for d in range(8)]

                    def gates(n, half, count=4):
                        for i in range(half, half + count):
                            block = ("in", f"g{n}_{i - i % 2}", f"g{n}_{i - i % 2 + 1}")
                            if block in SPLIT:
                                q = SPLIT.index(block) + 1
                                if SPLIT[q][0] == "in" and SPLIT[q][1] != "g3_0" and (q, i % 2) != (1, 0):
                                    high(q, (i % 2,))
                                elif SPLIT[q][0] == "ada" and i % 2 == 0:
                                    high(q)
                            if n == GATE_ORDER[3]:
                                dst = acc[:, i, :]
                            else:
                                k = gate_seq.index((n, i))
                                dst = gt[:, k % 4, :]
                                if k >= 4:
                                    act.wait_ge(*at("dve_br", gate_seq[k - 4]))
                                else:
                                    act.wait_ge(*at("dve_c", ("glu2", k)))
                            go("act_gt", (n, i), dst, z(f"g{n}_{i}")[:, 0:T], ACT.Sigmoid, bias=sw(f"g{n}_{i}"))

                    act.wait_ge(pre["pre_dma"], 80)
                    for k in range(KC):
                        act.wait_ge(*at("dve_u", ("p", KC - 1)))
                        go("act_uh", k, uhi[:, k, :], u[:, k, :], ACT.Copy)
                    gates(0, 0)
                    for t in range(3):
                        if t == 0:
                            act.wait_ge(*at("pe_m", ("a", "cp", 1)))
                        tokens("d", t)
                    gates(0, 4)
                    for j in range(4):
                        if j == 0:
                            act.wait_ge(C.sem("out_conv"), 32)
                        act.wait_ge(*at("dve_c", ("mu", j)))
                        go("act_cy", ("sq", j), sqc[:, j, :], y[:, 2, j, :], ACT.Square)
                    go("act_cy", "std", std[:], m("conv var")[:, 0:T], ACT.Sqrt, bias=cs("eps")[:, 0:1], scale=1.0 / CCH)
                    high(0)
                    prompt_state("d", P)
                    high(1, (0,))
                    for j in range(4):
                        act.wait_ge(*at("dve_c", ("xn", j)))
                        go("act_cy", j, y[:, 2, j, :], y[:, 2, j, :], ACT.Silu, bias=sw("clb", j), scale=sw("clg", j))
                    gates(2, 0)
                    for t in range(3):
                        head_std("d", t)
                    gates(2, 4)

                    def sample_exp(b):
                        r = b % 2
                        act.wait_ge(*at("dve_s2", ("nm", b)))
                        for g in range(2):
                            if g == 0 and b >= 2:
                                act.wait_ge(*at("pe_m", ("sT", b - 2)))
                            go("act_s", ("e", b, g), pb[0:NS, r, g * 512:(g + 1) * 512], m(("ss", b, g))[0:NS, :], ACT.Exp,
                               bias=stats[0:NS, 100 + r:101 + r], scale=BSCALE, accum_out=stats[0:NS, 104 + 4 * r + g:105 + 4 * r + g])
                        go("act_s", ("e", b, 2), pb[0:NS, r, PAST:PAST + NS], pb[0:NS, r, PAST:PAST + NS], ACT.Exp,
                           bias=stats[0:NS, 100 + r:101 + r], scale=BSCALE, accum_out=stats[0:NS, 106 + 4 * r:107 + 4 * r])

                    def sample_turned(b):
                        if b >= 2:
                            act.wait_ge(*at("pe_m", ("so", b - 2)))
                        go("act_s", ("pT", b), pT[:, b % 2, 0:512], m(("sT", b))[:, :], ACT.Copy)

                    def sample_back(b):
                        ps = m(("soT", b))
                        go("act_s", ("oT", b), olatT[:, :, :, b * TS:(b + 1) * TS], ps[:, 0:2 * NS].rearrange("p (c h t) -> p c h t", c=2, h=BH), ACT.Copy)

                    def slot(b):
                        for kind, *which in SLOTS[b]:
                            if kind == "gate":
                                gates(*which, count=2)
                            elif kind == "ada":
                                high(SPLIT.index((kind, which[0])) + 1)
                                ada(which[0], which[0] + 1)

                    for b in range(NB):
                        if b >= 2:
                            sample_back(b - 2)
                        if b >= 1:
                            sample_turned(b - 1)
                        if b == 0:
                            high(SPLIT.index(("in", "g3_0", "g3_1")))
                        sample_exp(b)
                        slot(b)
                    sample_back(NB - 2)
                    sample_turned(NB - 1)
                    slot(NB)
                    sample_back(NB - 1)
                    go("act_s", "ys", y[:, 1, :, SAMP], m("ys")[:, 0:4 * NS].rearrange("p (j t) -> p j t", j=4), ACT.Copy)

                    high(SPLIT.index(("out", 0)))
                    for k in range(KC):
                        act.wait_ge(*at("dve_br", (1, k)))
                        if k == 0:
                            act.wait_ge(*at("pe_m", ("so", NB - 1)))
                        go("act_go", k, ghi[:, k, :], gsum[:, k, :], ACT.Copy)
                    for i in range(1, 4):
                        high(SPLIT.index(("out", i)))

                    def norm(which, filler1, filler2):
                        if filler1:
                            ada(*filler1)
                        if which == 2:
                            go("act_n", "early", stats[:, 31:32], cs("ones")[:, 0:1], ACT.Sqrt)
                        for k in range(KC):
                            act.wait_ge(*at("dve_r", ("mu", which, k)))
                            nc.scalar.activation(acc[:, k, :], u[:, k, :], ACT.Square).then_inc(*ev("act_n", ("sq", which, k)))
                        go("act_n", ("std", which), std[:], m(("var", which))[:, 0:T], ACT.Sqrt, bias=cs("eps")[:, 0:1], scale=1.0 / D_MODEL)
                        for k in range(KC):
                            act.wait_ge(*at("dve_r", ("xn", which, k)))
                            nc.scalar.activation(x[:, k, :], u[:, k, :], ACT.Identity, bias=sw(f"ln{which}b", k)).then_inc(*ev("act_n", ("x", which, k)))
                        if filler2:
                            ada(*filler2)

                    def split(q):
                        n = FIRST_FFN + q
                        act.wait_ge(C.sem(f"w_landed{n % RING}"), 16 * (n // RING + 1))
                        if q >= 2:
                            act.wait_ge(*at(*ffn_done(q - 2)))
                        elif q == 0:
                            act.wait_ge(*at("pe_z", ("br", 1, 7)))
                        else:
                            act.wait_ge(*at("pe_z", ("wo", 7)))
                        for i in range(2):
                            go("act_w", (q, i), whi[q % 2][:, i * 1024:(i + 1) * 1024], ring[:, n % RING, i * 1024:(i + 1) * 1024], ACT.Copy)

                    norm(1, (18, 20), (20, 22))
                    for k in range(KC):
                        if k == KC // 2:
                            split(0)
                            ada(22, 24)
                        act.wait_ge(*at("dve_u2", ("p", k)))
                        go("act_x", k, xhi[:, k, :], acc[:, k, :], ACT.Copy)
                    for j in range(FT):
                        split(j + 1)
                        if j >= 2:
                            act.wait_ge(*at("dve_f", ("h", j - 2)))
                        go("act_f", j, gt[:, j % 2, :], z(("f1", j))[:, 0:T], ACT.Silu)
                        act.wait_ge(*at("dve_f", ("h", j)))
                        go("act_h", j, hhi[:, j, :], tmp[:, j % 2, :], ACT.Copy)
                    for q in range(FT + 1, FFN_BLOCKS):
                        split(q)
                    norm(2, None, None)

                @block.vector
                def _(dve):
                    dve.wait_ge(C.sem("in_small"), 16)

                    def V():
                        in_turn(dve, "dve")
                        return nc.vector

                    def z(name):
                        dve.wait_ge(*at("pe_z", name))
                        return banks[name]

                    def m(name):
                        dve.wait_ge(*at("pe_m", name))
                        return banks[name]

                    def bc(ap, shape):
                        return ap.to_broadcast(shape)

                    def ada(a0, a1):
                        for i in range(a0, a1):
                            ps = m(("adaT", i))
                            if ("ada", i) in SPLIT:
                                both = ps[:, 0:36].rearrange("p (j s c) -> p j s c", j=2, s=2)
                                to = mod[:, 2 * i:2 * i + 2, :]
                                V().tensor_tensor(to, both[:, :, 0, :], smallw[:, 2 * i:2 * i + 2].rearrange("p (j c) -> p j c", c=1).to_broadcast([P, 2, 9]),
                                                ALU.add).then_inc(*ev("dve_mod", ("high", i)))
                                V().tensor_tensor(to, to, both[:, :, 1, :], ALU.add).then_inc(*ev("dve_mod", i))
                                continue
                            V().tensor_tensor(mod[:, 2 * i:2 * i + 2, :], ps[:, 0:18].rearrange("p (j c) -> p j c", j=2),
                                            smallw[:, 2 * i:2 * i + 2].rearrange("p (j c) -> p j c", c=1).to_broadcast([P, 2, 9]),
                                            ALU.add).then_inc(*ev("dve_mod", i))

                    def modulate(sem, dst, sh, sc):
                        V().tensor_scalar_add(mod[:, sc:sc + 8, :], mod[:, sc:sc + 8, :], 1.0).then_inc(*ev(sem, "sc"))
                        dve.wait_ge(*at(sem, "sc"))

                        def per_batch(o):
                            return mod[:, o:o + 8, 1:9].rearrange("p k (b t) -> p k b t", t=1).to_broadcast([P, KC, NB, TS])
                        ds = dst[:, :, SAMP].rearrange("p k (b t) -> p k b t", b=NB)
                        V().tensor_tensor(ds, x[:, :, SAMP].rearrange("p k (b t) -> p k b t", b=NB), per_batch(sc), ALU.mult).then_inc(*ev(sem, "s1"))
                        dve.wait_ge(*at(sem, "s1"))
                        V().tensor_tensor(ds, ds, per_batch(sh), ALU.add).then_inc(*ev(sem, "s2"))
                        for k in range(KC):
                            V().tensor_scalar(dst[:, k, 0:SEQ], x[:, k, 0:SEQ], mod[:, sc + k, 0:1], mod[:, sh + k, 0:1], ALU.mult,
                                            ALU.add).then_inc(*ev(sem, ("p", k)))

                    ada(0, 8)
                    dve.wait_ge(*at("dve_mod", 7))
                    modulate("dve_u", u, 0, 8)

                    ps = z("small")
                    V().tensor_scalar_add(grow[:, 0, :], ps[0:4, 0:T], sw("small")[0:4]).then_inc(*ev("dve_s", "i"))
                    V().tensor_scalar_add(grow[:, 5, :], ps[32:36, 0:T], sw("small")[32:36]).then_inc(*ev("dve_s", "f"))
                    V().tensor_scalar_add(krz[64:96, :], ps[64:96, 0:T], sw("small")[64:96]).then_inc(*ev("dve_s", "kr"))
                    dve.wait_ge(*at("dve_s", "f"))
                    V().scalar_tensor_tensor(out=grow[:, 1, :], in0=grow[:, 5, :], scalar=-1.0, in1=grow[:, 5, :], op0=ALU.mult, op1=ALU.max).then_inc(*ev("dve_g", "abs"))
                    dve.wait_ge(*at("dve_s", "kr"))
                    V().tensor_tensor(kpe[64:96, :], krz[64:96, :], cs("cosB")[64:96, :], ALU.mult).then_inc(*ev("dve_b", "kr t1"))
                    V().tensor_tensor(krz[64:96, :], m("kr_swap")[64:96, 0:T], cs("sinB")[64:96, :], ALU.mult).then_inc(*ev("dve_b", "kr t2"))
                    dve.wait_ge(*at("dve_b", "kr t2"))
                    V().tensor_tensor(kpe[64:96, :], kpe[64:96, :], krz[64:96, :], ALU.add).then_inc(*ev("dve_b", "kpe"))
                    dve.wait_ge(*at("act_b", "std kv"))
                    V().reciprocal(std[:], std[:]).then_inc(*ev("dve_b", "r kv"))
                    dve.wait_ge(*at("dve_b", "r kv"))
                    for c in range(2):
                        V().scalar_tensor_tensor(out=ckv[:, c, :], in0=ckv[:, c, :], scalar=sw("kvn", c), in1=std[:], op0=ALU.mult,
                                               op1=ALU.mult).then_inc(*ev("dve_b", ("ckv", c)))
                    dve.wait_ge(*at("act_b", "std bq"))
                    V().reciprocal(tmp[:, 1, :], tmp[:, 0, :]).then_inc(*ev("dve_b", "r bq"))
                    dve.wait_ge(*at("dve_b", "r bq"))
                    for c in range(3):
                        V().scalar_tensor_tensor(out=bqz[:, c, :], in0=bqz[:, c, :], scalar=sw("qn", c), in1=tmp[:, 1, :], op0=ALU.mult,
                                               op1=ALU.mult).then_inc(*ev("dve_b", ("bq", c)))
                    for j in range(4):
                        ps = z(("uq", j))
                        dve.wait_ge(*at("act_q", ("even", j)))
                        V().tensor_copy(q96[0:64, 2 * j + 1, :], ps[64:128, 0:T]).then_inc(*ev("dve_q", ("odd", j)))
                    for j in range(4):
                        ps = z(("kn", j))
                        dve.wait_ge(*at("act_q", ("keven", j)))
                        V().tensor_copy(k96[0:64, 2 * j + 1, :], ps[64:128, 0:SEQ]).then_inc(*ev("dve_q", ("kodd", j)))
                    for r in range(2):
                        dve.wait_ge(*at("act_q", ("qr", r)))
                        ps = m(("qr_swap", r))
                        V().tensor_tensor(tmp[:, 1, :], ps[:, 0:T], cs("sinB"), ALU.mult).then_inc(*ev("dve_q", ("t2", r)))
                        V().tensor_tensor(tmp[:, 0, :], qr[:, r, :], cs("cosB"), ALU.mult).then_inc(*ev("dve_q", ("t1", r)))
                        dve.wait_ge(*at("dve_q", ("t1", r)))
                        for i in range(4):
                            V().tensor_tensor(q96[64:96, 4 * r + i, :], tmp[32 * i:32 * i + 32, 0, :], tmp[32 * i:32 * i + 32, 1, :],
                                            ALU.add).then_inc(*ev("dve_q", ("rot", r, i)))
                    for c in range(2):
                        ps = z(("qa", c))
                        V().tensor_copy(qabs[:, c, :, :].rearrange("p b (h t) -> p h b t", h=BH),
                                      ps[:, :].rearrange("p (h b t) -> p h b t", h=BH, b=NB)).then_inc(*ev("dve_q", ("qabs", c)))
                    dve.wait_ge(*at("dve_q", ("rot", 1, 3)))
                    V().tensor_copy(qpes[64:96, :, :].rearrange("p b (h t) -> p h b t", h=BH),
                                  q96[64:96, :, SAMP].rearrange("p h (b t) -> p h b t", b=NB)).then_inc(*ev("dve_q", "qpes"))

                    dve.wait_ge(*at("act_g", "ln"))
                    lf, g7 = grow[:, 1, :], grow[:, 5, :]
                    V().scalar_tensor_tensor(out=lf, in0=g7, scalar=0.0, in1=grow[:, 3, :], op0=ALU.min, op1=ALU.subtract).then_inc(*ev("dve_g", "lf"))
                    dve.wait_ge(*at("dve_g", "lf"))
                    V().tensor_tensor_scan(grow[:, 2, :], cs("reset")[0:4, :], lf, 0.0, ALU.mult, ALU.add).then_inc(*ev("dve_g", "b"))
                    dve.wait_ge(C.sem("in_m0"), 16)
                    V().tensor_copy(grow[:, 3, :], lf).then_inc(*ev("dve_g", "lf copy"))
                    V().tensor_copy(grow[:, 4, :], grow[:, 0, :]).then_inc(*ev("dve_g", "i copy"))
                    dve.wait_ge(*at("dve_g", "i copy"))
                    first = grow[:, 3, SEQ:T:TS]
                    V().tensor_tensor(mout[:, 1:9], first, m0[:], ALU.add).then_inc(*ev("dve_g", "lf m0"))
                    dve.wait_ge(*at("dve_g", "lf m0"))
                    V().tensor_tensor(grow[:, 4, SEQ:T:TS], mout[:, 1:9], grow[:, 0, SEQ:T:TS], ALU.max).then_inc(*ev("dve_g", "i first"))
                    V().memset(first, NEG).then_inc(*ev("dve_g", "lf first"))
                    dve.wait_ge(*at("dve_g", "lf first"))
                    V().tensor_tensor_scan(g7, grow[:, 3, :], grow[:, 4, :], 0.0, ALU.add, ALU.max).then_inc(*ev("dve_g", "m"))
                    dve.wait_ge(*at("dve_g", "m"))
                    V().tensor_copy(mout[:, 0:1], grow[:, 5, SEQ - 1:SEQ]).then_inc(*ev("dve_g", "mout p"))
                    V().tensor_copy(mout[:, 1:9], grow[:, 5, SEQ + TS - 1:T:TS]).then_inc(*ev("dve_g", "mout"))
                    V().tensor_tensor(growk[:, 0, :], grow[:, 2, :], g7, ALU.subtract).then_inc(*ev("dve_g", "b-m"))
                    dve.wait_ge(*at("dve_g", "b-m"))
                    V().tensor_tensor(growk[:, 1, SAMP].rearrange("p (b t) -> p b t", b=NB), growk[:, 0, SAMP].rearrange("p (b t) -> p b t", b=NB),
                                    m0[:].rearrange("p (b t) -> p b t", t=1).to_broadcast([4, NB, TS]), ALU.add).then_inc(*ev("dve_g", "b-m+m0"))
                    dve.wait_ge(*at("pool_z", "r4"))
                    V().tensor_tensor(grow[:, 3, :], grow[:, 0, :], grow[:, 2, :], ALU.subtract).then_inc(*ev("dve_g", "i-b"))
                    dve.wait_ge(*at("dve_g", "i-b"))
                    V().tensor_copy(r4[0:4, :], grow[:, 3, :]).then_inc(*ev("dve_g", "r4 a"))
                    V().tensor_scalar_mul(r4[64:68, :], g7, -1.0).then_inc(*ev("dve_g", "r4 b"))
                    V().tensor_scalar_add(r4[96:100, 0:SEQ], grow[:, 3, 0:SEQ], growk[:, 0, SEQ - 1:SEQ]).then_inc(*ev("dve_g", "r4 c"))
                    V().tensor_tensor(r4[96:100, SAMP].rearrange("p (b t) -> p b t", b=NB), grow[:, 3, SAMP].rearrange("p (b t) -> p b t", b=NB),
                                    growk[:, 0, SEQ + TS - 1:T:TS].rearrange("p (b t) -> p b t", t=1).to_broadcast([4, NB, TS]),
                                    ALU.add).then_inc(*ev("dve_g", "r4"))

                    def prompt_max(h):
                        for i in range(2):
                            n = (i + 1) * P
                            if h >= 1:
                                dve.wait_ge(*at("pe_m", ("ppT", h - 1, i)))
                            else:
                                dve.wait_ge(*at("pe_m", ("ps", h, i)))
                            V().tensor_tensor(pp[:, i, 0:n], m(("ps", h, i))[:, 0:n], cs("negP")[:, 256 - n:256], ALU.add).then_inc(*ev("dve_pa", ("s", h, i)))
                            dve.wait_ge(*at("dve_pa", ("s", h, i)))
                            V().reduce_max(stats[:, i:i + 1], pp[:, i, 0:n], AX).then_inc(*ev("dve_pa", ("max", h, i)))
                            dve.wait_ge(*at("dve_pa", ("max", h, i)))
                            V().tensor_scalar_mul(stats[:, 4 + i:5 + i], stats[:, i:i + 1], -BSCALE).then_inc(*ev("dve_pa", ("nm", h, i)))

                    def prompt_norm(h):
                        for i in range(2):
                            dve.wait_ge(*at("act_pa", ("e", h, i)))
                            V().reciprocal(stats[:, 12 + i:13 + i], stats[:, 8 + i:9 + i]).then_inc(*ev("dve_pa", ("r", h, i)))
                            dve.wait_ge(*at("dve_pa", ("r", h, i)))
                            V().tensor_scalar_mul(pp[:, i, 0:(i + 1) * P], pp[:, i, 0:(i + 1) * P], stats[:, 12 + i:13 + i]).then_inc(*ev("dve_pa", ("norm", h, i)))

                    for i in range(BH):
                        xx, j = A_STREAM[i] if i < len(A_STREAM) else ("", 0)
                        if xx == "aq":
                            for h in (j, j + 1):
                                V().tensor_scalar(qm[:, h, :], z(f"aq{h}")[:, 0:T], sw(f"aq{h}"), QSCALE, ALU.add, ALU.mult).then_inc(*ev("dve_a", ("aq", h)))
                        prompt_max(i)
                        prompt_norm(i)

                    def tokens(X, t):
                        tn = TOK[t][1]
                        V().tensor_copy(vtok[0:tn, t, :, 0:P], m((X, "vT", t))[0:tn, :].rearrange("p (h d) -> p h d", h=H)).then_inc(*ev(f"dve_{X}t", ("v", t)))

                    def conv_in(j):
                        if j == 0:
                            dve.wait_ge(*at("pe_m", ("po", BH - 1)))
                        dve.wait_ge(*at("act_c", ("sg", j)))
                        ps = z(f"ca{j}")
                        V().scalar_tensor_tensor(out=ucp[:, j, CW - 1:], in0=ps[:, 0:SEQ], scalar=sw(f"ca{j}"), in1=gt[:, j, 0:SEQ], op0=ALU.add,
                                               op1=ALU.mult).then_inc(*ev("dve_c", ("glu1", j)))
                        V().scalar_tensor_tensor(out=ucs[:, j, :, CW - 1:], in0=ps[:, SAMP].rearrange("p (b t) -> p b t", b=NB), scalar=sw(f"ca{j}"),
                                               in1=gt[:, j, SAMP].rearrange("p (b t) -> p b t", b=NB), op0=ALU.add, op1=ALU.mult).then_inc(*ev("dve_c", ("glu2", j)))

                    def decay(h):
                        ps = m(("rb", h))
                        if h >= 2:
                            dve.wait_ge(*at("dve_aw", ("w2", h - 2)))
                        for i, (o, n, src, t, rows_) in enumerate(((0, 256, 0, 0, P), (256, 128, P, 1, P), (384, NS, SEQ, 2, NS))):
                            if i == 0:
                                dve.wait_ge(*at("act_g", ("exp", 2)))
                            V().tensor_scalar(eb[0:rows_, h % 2, o:o + n], ps[0:rows_, src:src + n], col4[0:rows_, t, h:h + 1], 0.0, ALU.add,
                                            ALU.min).then_inc(*ev("dve_aw", (f"e{i}", h)))

                    def weigh(X, h):
                        ps = m((X, "st", h))
                        if X == "a":
                            dve.wait_ge(*at("pool_aw", ("e2", h)))
                            d = eb[:, h % 2, :]
                        else:
                            d = cs("decay")[:, h * 320:(h + 1) * 320]
                        if h >= 2:
                            dve.wait_ge(*at("pe_m", (X, "num", 2, 0)))
                        elif X == "d":
                            dve.wait_ge(*at("pe_m", ("a", "num", 2, 1)))
                        if X == "a":
                            V().tensor_tensor(wb[:, h % 2, 0:384], ps[:, 0:384], d[:, 0:384], ALU.mult).then_inc(*ev("dve_aw", ("w1", h)))
                            ds = d[0:NS, 384:448]
                        else:
                            V().tensor_tensor(wb[:, h % 2, 0:256], ps[:, 0:256], d[:, 0:256], ALU.mult).then_inc(*ev("dve_dw", ("w0", h)))
                            V().tensor_tensor(wb[:, h % 2, 256:384], ps[:, 256:384], d[:, 0:128], ALU.mult).then_inc(*ev("dve_dw", ("w1", h)))
                            ds = d[0:NS, 256:320]
                        V().tensor_tensor(wb[0:NS, h % 2, 384:448], ps[0:NS, 384:448], ds, ALU.mult).then_inc(*ev(f"dve_{X}w", ("w2", h)))

                    def spread_queries(X):
                        dve.wait_ge(*at("pool_z", "qz"))
                        dst = qz.rearrange("p (b x) -> p b x", x=264)[:, :, 0:256].rearrange("p b (h t) -> p h b t", h=H)[:, :, :, 0:TS]
                        src = qm[:, :, SAMP].rearrange("p h (b t) -> p h b t", b=NB)
                        if X == "a":
                            dve.wait_ge(*at("act_g", "wint"))
                            dve.wait_ge(*at("dve_a", ("aq", 3)))
                            w_ = wint[:].rearrange("p h (b t) -> p h b t", b=NB)
                            for h in range(H):
                                V().tensor_tensor(dst[:, h], src[:, h], w_[:, h], ALU.mult).then_inc(*ev("dve_aw", "qz" if h == 3 else ("qz", h)))
                        else:
                            dve.wait_ge(*at("dve_dk", ("dq", 3)))
                            dve.wait_ge(*at("pe_m", ("a", "num", 2, 1)))
                            for h in range(H):
                                w_ = cs("w_in_ret")[:, h * TS:(h + 1) * TS].rearrange("p (b t) -> p b t", b=1).to_broadcast([P, NB, TS])
                                V().tensor_tensor(dst[:, h], src[:, h], w_, ALU.mult).then_inc(*ev("dve_dw", "qz" if h == 3 else ("qz", h)))

                    def head_rows(X, hp, width):
                        for t, (t0, tn) in enumerate(TOK):
                            ps = m((X, "num", t, hp))
                            num = ps[0:tn, 0:2 * width].rearrange("p (h d) -> p h d", h=2)
                            s = f"dve_{X}h"
                            out = hh[0:tn, t, 2 * hp:2 * hp + 2, :]
                            if X == "a":
                                den, rec = stats[0:tn, 80:82], stats[0:tn, 82:84]
                                V().tensor_copy(rec, num[:, :, P]).then_inc(*ev(s, ("dc", t, hp)))
                                dve.wait_ge(*at(s, ("dc", t, hp)))
                                V().scalar_tensor_tensor(out=den, in0=rec, scalar=-1.0, in1=rec, op0=ALU.mult, op1=ALU.max).then_inc(*ev(s, ("abs", t, hp)))
                                dve.wait_ge(*at(s, ("abs", t, hp)))
                                V().tensor_tensor(den, den, col4[0:tn, t, 64 + 2 * hp:66 + 2 * hp], ALU.max).then_inc(*ev(s, ("den", t, hp)))
                                dve.wait_ge(*at(s, ("den", t, hp)))
                                V().reciprocal(rec, den).then_inc(*ev(s, ("rec", t, hp)))
                                dve.wait_ge(*at(s, ("rec", t, hp)))
                                V().tensor_tensor(out, num[:, :, 0:P], rec.rearrange("p (h d) -> p h d", d=1).to_broadcast([tn, 2, P]),
                                                ALU.mult).then_inc(*ev(s, ("h", t, hp)))
                            else:
                                if hp == 0:
                                    dve.wait_ge(*at("pe_m", ("a", "hT", t)))
                                V().tensor_copy(out, num).then_inc(*ev(s, ("h", t, hp)))
                            dve.wait_ge(*at(s, ("h", t, hp)))
                            for i in range(2):
                                h = 2 * hp + i
                                V().bn_stats(stats[0:tn, 112 + 6 * i:118 + 6 * i], hh[0:tn, t, h, :]).then_inc(*ev(s, ("bn", t, h)))
                                dve.wait_ge(*at(s, ("bn", t, h)))
                                V().bn_aggr(stats[0:tn, 32 + 8 * t + 2 * h:34 + 8 * t + 2 * h], stats[0:tn, 112 + 6 * i:118 + 6 * i]).then_inc(*ev(s, ("mv", t, h)))

                    def head_norm(X):
                        s = f"dve_{X}h"
                        for t, (t0, tn) in enumerate(TOK):
                            dve.wait_ge(*at(f"act_{X}h", t))
                            V().reciprocal(stats[0:tn, 64 + 4 * t:68 + 4 * t], stats[0:tn, 64 + 4 * t:68 + 4 * t]).then_inc(*ev(s, ("rs", t)))
                            dve.wait_ge(*at(s, ("rs", t)))
                            for h in range(H):
                                V().tensor_scalar(hh[0:tn, t, h, :], hh[0:tn, t, h, :], stats[0:tn, 32 + 8 * t + 2 * h:33 + 8 * t + 2 * h],
                                                stats[0:tn, 64 + 4 * t + h:65 + 4 * t + h], ALU.subtract, ALU.mult).then_inc(*ev(s, ("n", t, h)))

                    def head_gate(X, n):
                        if X == "a":
                            dve.wait_ge(*at("act_a", ("ao", 3)))
                        else:
                            dve.wait_ge(*at("act_d", ("dg", 3)))
                        for t, (t0, tn) in enumerate(TOK):
                            ps = m((X, "hT", t))[:, :].rearrange("p (h t) -> p h t", h=H)[:, :, 0:tn]
                            V().tensor_tensor(y[:, n, :, t0:t0 + tn], ps, y[:, n, :, t0:t0 + tn], ALU.mult).then_inc(*ev(f"dve_{X}y", t))

                    def state_update(X, width):
                        for b in range(NB):
                            for h in range(H):
                                ps = m((X, "cs", b, h // 2))
                                if X == "a":
                                    dec = wint[:, h, b * TS + TS - 1:b * TS + TS]
                                else:
                                    dec = WS_GAMMA[TS][h]
                                V().scalar_tensor_tensor(out=state[:, b, h, 0:width], in0=state[:, b, h, 0:width], scalar=dec,
                                                       in1=ps[:, (h % 2) * width:(h % 2 + 1) * width], op0=ALU.mult, op1=ALU.add
                                                       ).then_inc(*ev(f"dve_{X}c", (b, h)))

                    spread_queries("a")
                    conv_in(0)
                    for t in range(3):
                        tokens("a", t)
                    for h in (0, 1):
                        decay(h)
                        weigh("a", h)
                    conv_in(1)
                    head_rows("a", 0, W)
                    for h in (2, 3):
                        decay(h)
                        weigh("a", h)
                    conv_in(2)
                    conv_in(3)
                    head_rows("a", 1, W)
                    head_norm("a")
                    state_update("a", W)
                    head_gate("a", 0)

                    def rotate(x_, h):
                        dst = (qm if x_ == "dq" else km)[:, h, :]
                        if h == 0:
                            dve.wait_ge(*at("pe_m", ("a", "st", 3)))
                        dve.wait_ge(*at("act_dz", (x_, h)))
                        V().tensor_tensor(dst, tmp[:, h % 2, :], cs("cosD"), ALU.mult).then_inc(*ev("dve_dk", ("t1", x_, h)))
                        V().tensor_tensor(std[:], m(("sw", x_, h))[:, 0:T], cs("sinD"), ALU.mult).then_inc(*ev("dve_dk", ("t2", x_, h)))
                        dve.wait_ge(*at("dve_dk", ("t2", x_, h)))
                        V().tensor_tensor(dst, dst, std[:], ALU.add).then_inc(*ev("dve_dk", (x_, h)))

                    dve.wait_ge(C.sem("in_hist"), 16)
                    dve.wait_ge(*at("pool_z", "hist"))
                    dve.wait_ge(*at("pe_m", ("ps", BH - 1, 1)))

                    def taps(first, last):
                        for i in range(first, last):
                            j, k = 2 * (i // (2 * CW)) + i % 2, i % (2 * CW) // 2
                            wk = smallw[:, SM["cw"] + j * CW + k:SM["cw"] + j * CW + k + 1]
                            o, src = y[:, 2, j, 0:SEQ], ucp[:, j, k:k + SEQ]
                            if k == 0:
                                dve.wait_ge(*at("dve_c", ("glu1", j)))
                                nc.vector.tensor_scalar(o, src, wk, sw("cb", j), ALU.mult, ALU.add).then_inc(*ev("dve_c", ("tap", j, k)))
                            else:
                                dve.wait_ge(*at("dve_c", ("tap", j, k - 1)))
                                nc.vector.scalar_tensor_tensor(out=o, in0=src, scalar=wk, in1=o, op0=ALU.mult, op1=ALU.add).then_inc(*ev("dve_c", ("tap", j, k)))

                    for i, (x_, h) in enumerate([(x_, h) for x_ in ("dk", "dq") for h in (0, 2)]):
                        rotate(x_, h)
                        rotate(x_, h + 1)
                        taps(12 * i, 12 * (i + 1) if i < 3 else 4 * CW)

                    def gated(n, half):
                        for i in range(4):
                            d = half + i
                            k = d % 4
                            g = acc[:, d, :] if n == GATE_ORDER[3] else gt[:, k, :]
                            dve.wait_ge(*at("act_gt", (n, d)))
                            ps = z(("br", n, d))
                            if n == GATE_ORDER[0]:
                                V().tensor_tensor(gt[:, k, :], ps[:, 0:T], gt[:, k, :], ALU.mult).then_inc(*ev("dve_br", ("first", d)))
                                dve.wait_ge(*at("dve_br", ("first", d)))
                                V().tensor_copy(gsum[:, d, :], gt[:, k, :]).then_inc(*ev("dve_br", (n, d)))
                            else:
                                V().tensor_tensor(g, ps[:, 0:T], g, ALU.mult).then_inc(*ev("dve_br", ("t", n, d)))
                                dve.wait_ge(*at("dve_br", ("t", n, d)))
                                V().tensor_tensor(gsum[:, d, :], gsum[:, d, :], g, ALU.add).then_inc(*ev("dve_br", (n, d)))

                    gated(0, 0)
                    spread_queries("d")
                    for t in range(3):
                        tokens("d", t)
                    weigh("d", 0)
                    weigh("d", 1)
                    ps = m("conv sum")
                    for j in range(4):
                        V().scalar_tensor_tensor(out=y[:, 2, j, :], in0=ps[:, 0:T], scalar=-1.0 / CCH, in1=y[:, 2, j, :], op0=ALU.mult,
                                               op1=ALU.add).then_inc(*ev("dve_c", ("mu", j)))
                    gated(0, 4)
                    head_rows("d", 0, P)
                    weigh("d", 2)
                    weigh("d", 3)
                    dve.wait_ge(*at("pe_z", "g0_7"))
                    for k in range(KC):
                        dve.wait_ge(*at("act_uh", k))
                        nc.vector.tensor_tensor(ulo[:, k, :], u[:, k, :], uhi[:, k, :], ALU.subtract).then_inc(*ev("dve_ul", k))
                    head_rows("d", 1, P)
                    dve.wait_ge(*at("act_cy", "std"))
                    V().reciprocal(std[:], std[:]).then_inc(*ev("dve_c", "rs"))
                    dve.wait_ge(*at("dve_c", "rs"))
                    for j in range(4):
                        V().tensor_tensor(y[:, 2, j, :], y[:, 2, j, :], std[:], ALU.mult).then_inc(*ev("dve_c", ("xn", j)))
                    gated(2, 0)
                    head_norm("d")
                    state_update("d", P)
                    head_gate("d", 3)
                    gated(2, 4)

                    def sample_max(b):
                        r = b % 2
                        s = stats[0:NS, :]
                        if b == 0:
                            dve.wait_ge(*at("dve_dc", (NB - 1, 3)))
                        if b >= 2:
                            dve.wait_ge(*at("pe_m", ("snT", b - 2)))
                        V().tensor_tensor(pb[0:NS, r, PAST:PAST + NS], m(("ss", b, 2))[0:NS, 0:NS], cs("negS")[0:NS, b * NS:(b + 1) * NS],
                                        ALU.add).then_inc(*ev("dve_s2", ("new", b)))
                        for g in range(2):
                            V().reduce_max(s[:, 90 + g:91 + g], m(("ss", b, g))[0:NS, :], AX).then_inc(*ev("dve_s2", ("max", b, g)))
                        dve.wait_ge(*at("dve_s2", ("new", b)))
                        V().reduce_max(s[:, 92:93], pb[0:NS, r, PAST:PAST + NS], AX).then_inc(*ev("dve_s2", ("max", b, 2)))
                        dve.wait_ge(*at("dve_s2", ("max", b, 2)))
                        V().reduce_max(s[:, 93:94], s[:, 90:93], AX).then_inc(*ev("dve_s2", ("max", b)))
                        dve.wait_ge(*at("dve_s2", ("max", b)))
                        V().tensor_scalar_mul(s[:, 100 + r:101 + r], s[:, 93:94], -BSCALE).then_inc(*ev("dve_s2", ("nm", b)))

                    def sample_turned(b):
                        r = b % 2
                        if b >= 2:
                            dve.wait_ge(*at("pe_m", ("so", b - 2)))
                        V().tensor_copy(pT[0:NS, r, 512:576], m(("snT", b))[0:NS, 0:NS]).then_inc(*ev("dve_s2", ("pnT", b)))

                    def sample_scaled(b):
                        r = b % 2
                        s = stats[0:NS, :]
                        dve.wait_ge(*at("act_s", ("e", b, 2)))
                        V().reduce_sum(s[:, 94:95], s[:, 104 + 4 * r:107 + 4 * r], AX).then_inc(*ev("dve_s2", ("sum", b)))
                        dve.wait_ge(*at("dve_s2", ("sum", b)))
                        V().reciprocal(s[:, 96 + r:97 + r], s[:, 94:95]).then_inc(*ev("dve_s2", ("r", b)))
                        dve.wait_ge(*at("dve_s2", ("r", b)))
                        if b >= 2:
                            dve.wait_ge(*at("pe_m", ("soT", b - 2)))
                        V().tensor_scalar_mul(olat[0:NS, r, :], m(("so", b))[0:NS, 0:KVR], s[:, 96 + r:97 + r]).then_inc(*ev("dve_s2", ("o", b)))

                    def slot(b):
                        for kind, *which in SLOTS[b]:
                            if kind == "branch":
                                gated(*which)
                            elif kind == "ada" and which[0] > 8:
                                ada(which[0] - 1, which[0])

                    for b in range(NB):
                        if b >= 1:
                            sample_turned(b - 1)
                        sample_max(b)
                        if b >= 1:
                            sample_scaled(b - 1)
                        slot(b)
                    sample_turned(NB - 1)
                    sample_scaled(NB - 1)
                    slot(NB)
                    gated(1, 0)
                    gated(1, 4)

                    for k in range(KC):
                        dve.wait_ge(*at("act_go", k))
                        V().tensor_tensor(glo[:, k, :], gsum[:, k, :], ghi[:, k, :], ALU.subtract).then_inc(*ev("dve_gl", k))

                    def residual(which, name, g, src_x, split=None):
                        for d in range(KC):
                            if split:
                                for q in range(FT + 1, FFN_BLOCKS):
                                    if max(0, (16 * (q - FT - 1)) // FT) == d:
                                        split(q)
                            ps = z((name, d))
                            dve.wait_ge(*at("dve_mod", 11 if which == 1 else 23))
                            nc.vector.tensor_scalar_mul(tmp[:, d % 2, 0:SEQ], ps[:, 0:SEQ], mod[:, g + d, 0:1]).then_inc(*ev("dve_r", ("gp", which, d)))
                            nc.vector.tensor_tensor(tmp[:, d % 2, SAMP].rearrange("p (b t) -> p b t", b=NB), ps[:, SAMP].rearrange("p (b t) -> p b t", b=NB),
                                            mod[:, g + d, 1:9].rearrange("p (b t) -> p b t", t=1).to_broadcast([P, NB, TS]),
                                            ALU.mult).then_inc(*ev("dve_r", ("g", which, d)))
                            dve.wait_ge(*at("dve_r", ("g", which, d)))
                            V().scalar_tensor_tensor(out=u[:, d, :], in0=x[:, d, :], scalar=ALPHA, in1=tmp[:, d % 2, :], op0=ALU.mult,
                                                   op1=ALU.add).then_inc(*ev("dve_r", ("r", which, d)))

                    def norm(which, filler1, filler2):
                        ps = m(("mean", which))
                        for k in range(KC):
                            nc.vector.scalar_tensor_tensor(out=u[:, k, :], in0=ps[:, 0:T], scalar=-1.0 / D_MODEL, in1=u[:, k, :], op0=ALU.mult,
                                                   op1=ALU.add).then_inc(*ev("dve_r", ("mu", which, k)))
                        if filler1:
                            ada(filler1[0] - 1, filler1[1])
                        dve.wait_ge(*at("act_n", ("std", which)))
                        V().reciprocal(std[:], std[:]).then_inc(*ev("dve_r", ("rs", which)))
                        dve.wait_ge(*at("dve_r", ("rs", which)))
                        for k in range(KC):
                            nc.vector.scalar_tensor_tensor(out=u[:, k, :], in0=u[:, k, :], scalar=sw(f"ln{which}g", k), in1=std[:], op0=ALU.mult,
                                                   op1=ALU.mult).then_inc(*ev("dve_r", ("xn", which, k)))
                        if filler2:
                            ada(*filler2)

                    dve.wait_ge(C.sem("in_x"), 16)
                    residual(1, "wo", 16, x)
                    norm(1, (18, 20), (20, 20))

                    def split(q):
                        dve.wait_ge(*at("act_w", (q, 0)))
                        V().tensor_tensor(wlo[q % 2][:, 0:1024], ring[:, (FIRST_FFN + q) % RING, 0:1024], whi[q % 2][:, 0:1024],
                                        ALU.subtract).then_inc(*ev("dve_w", q))

                    V().tensor_scalar_add(mod[:, 32:40, :], mod[:, 32:40, :], 1.0).then_inc(*ev("dve_u2", "sc"))
                    dve.wait_ge(*at("pe_m", ("var", 1)))

                    def x_low(k):
                        dve.wait_ge(*at("act_x", k))
                        V().tensor_tensor(xlo[:, k, :], acc[:, k, :], xhi[:, k, :], ALU.subtract).then_inc(*ev("dve_x", k))

                    for k in range(KC):
                        if k == KC // 2 + 1:
                            split(0)
                        dve.wait_ge(*at("act_n", ("x", 1, k)))
                        xs, ds = (v[:, k, SAMP].rearrange("p (b t) -> p b t", b=NB) for v in (x, acc))
                        sc, sh = (mod[:, o + k, 1:9].rearrange("p (b t) -> p b t", t=1).to_broadcast([P, NB, TS]) for o in (32, 24))
                        V().tensor_tensor(ds, xs, sc, ALU.mult).then_inc(*ev("dve_u2", ("s1", k)))
                        V().tensor_scalar(acc[:, k, 0:SEQ], x[:, k, 0:SEQ], mod[:, 32 + k, 0:1], mod[:, 24 + k, 0:1], ALU.mult,
                                        ALU.add).then_inc(*ev("dve_u2", ("p1", k)))
                        dve.wait_ge(*at("dve_u2", ("s1", k)))
                        V().tensor_tensor(ds, ds, sh, ALU.add).then_inc(*ev("dve_u2", ("p", k)))
                        if k >= 1:
                            x_low(k - 1)
                    x_low(KC - 1)
                    ada(20, 24)
                    for j in range(FT):
                        split(j + 1)
                        dve.wait_ge(*at("act_f", j))
                        V().tensor_tensor(tmp[:, j % 2, :], z(("f3", j))[:, 0:T], gt[:, j % 2, :], ALU.mult).then_inc(*ev("dve_f", ("h", j)))
                        dve.wait_ge(*at("act_h", j))
                        V().tensor_tensor(hlo[:, j, :], tmp[:, j % 2, :], hhi[:, j, :], ALU.subtract).then_inc(*ev("dve_f", j))
                    residual(2, "fo", 40, x, split)
                    norm(2, None, None)

                @block.gpsimd
                def _(pool):
                    def G():
                        in_turn(pool, "pool")
                        return nc.gpsimd

                    G().memset(r4[:], 0.0).then_inc(*ev("pool_z", "r4"))
                    pool.wait_ge(*at("dve_b", "kpe"))
                    for h in range(BH):
                        G().tensor_copy(k96[64:96, h, :], kpe[64:96, 0:SEQ]).then_inc(*ev("pool_k", "kpe all" if h == BH - 1 else h))
                    G().memset(qz, 0.0).then_inc(*ev("pool_z", "qz"))
                    G().memset(vtok[:, :, :, P:W], 1.0).then_inc(*ev("pool_z", "ones"))
                    pool.wait_ge(*at("pe_m", ("po", BH - 1)))
                    G().memset(ucp[:, :, 0:CW - 1], 0.0).then_inc(*ev("pool_z", "hist"))

                    def weigh_keys(X):
                        for t, (t0, tn) in enumerate(TOK):
                            pool.wait_ge(*at(f"act_{X}t", ("k", t)))
                            if X == "a":
                                pool.wait_ge(*at("act_g", ("exp", t)))
                                w_ = col4[0:tn, t, 96:100]
                            else:
                                w_ = cs("w_st")[0:tn, H * t:H * t + H]
                            G().tensor_tensor(ktok[0:tn, t], ktok[0:tn, t], w_.rearrange("p (h d) -> p h d", d=1).to_broadcast([tn, H, P]),
                                            ALU.mult).then_inc(*ev(f"pool_{X}k", t))

                    def batch_keys(X, first=0, last=NB):
                        pool.wait_ge(*at(f"pool_{X}k", 2))
                        for b in range(first, last):
                            if b >= 2:
                                pool.wait_ge(*at("pe_m", (X, "cs", b - 2, 1)))
                            elif X == "d":
                                pool.wait_ge(*at("pe_m", ("a", "cs", NB - 2 + b, 1)))
                            G().tensor_scalar(kmb[0:NS, b % 2, :], ktok[0:NS, 2].rearrange("p h d -> p (h d)"), cs("batch")[0:NS, b:b + 1], None,
                                            ALU.mult).then_inc(*ev(f"pool_{X}m", b))

                    def mask(h):
                        pool.wait_ge(*at("act_aw", ("e2", h)))
                        G().tensor_tensor(eb[:, h % 2, 0:384], eb[:, h % 2, 0:384], cs("causal")[:, 0:384], ALU.mult).then_inc(*ev("pool_aw", ("e1", h)))
                        G().tensor_tensor(eb[0:NS, h % 2, 384:448], eb[0:NS, h % 2, 384:448], cs("causal")[0:NS, 384:448],
                                        ALU.mult).then_inc(*ev("pool_aw", ("e2", h)))

                    mask(0)
                    mask(1)
                    weigh_keys("a")
                    mask(2)
                    mask(3)
                    batch_keys("a")

                    pool.wait_ge(C.sem("in_hist"), 16)
                    pool.wait_ge(*at("dve_c", ("glu2", 3)))
                    pool.wait_ge(*at("dve_aw", ("w2", 3)))
                    conv_s = y[:, 2, :, SAMP].rearrange("p j (b t) -> p j b t", b=NB)
                    for k in range(CW):
                        wk = smallw[:, SM["cw"]:SM["cw"] + 4 * CW].rearrange("p (j b k) -> p j b k", j=4, b=1)[:, :, :, k:k + 1]
                        prod = eb[:, k % 2, 0:4 * NS].rearrange("p (j b t) -> p j b t", j=4, b=NB)
                        if k >= 2:
                            pool.wait_ge(*at("pool_c", ("sum", k - 2)))
                        nc.gpsimd.tensor_tensor(prod, ucs[:, :, :, k:k + TS], wk.to_broadcast([P, 4, NB, TS]), ALU.mult).then_inc(*ev("pool_c", ("prod", k)))
                        pool.wait_ge(*at("pool_c", ("prod", k)))
                        if k == 0:
                            bias = smallw[:, SM["cb"]:SM["cb"] + 4].rearrange("p (j b k) -> p j b k", b=1, k=1).to_broadcast([P, 4, NB, TS])
                            nc.gpsimd.tensor_tensor(conv_s, prod, bias, ALU.add).then_inc(*ev("pool_c", ("sum", k)))
                        else:
                            pool.wait_ge(*at("pool_c", ("sum", k - 1)))
                            nc.gpsimd.tensor_tensor(conv_s, conv_s, prod, ALU.add).then_inc(*ev("pool_c", ("sum", k)))
                    def low(q):
                        n = BLOCKS.index(SPLIT[q])
                        for i in range(2):
                            pool.wait_ge(*at("act_hq", (q, i)))
                            half = slice(i * 1024, (i + 1) * 1024)
                            G().tensor_tensor(wlx[:, n % RING, half], ring[:, n % RING, half], high_buffer(q)[i][:], ALU.subtract).then_inc(*ev("pool_l", (q, i)))

                    weigh_keys("d")
                    low(0)
                    low(1)
                    batch_keys("d", 0, 2)
                    low(2)
                    batch_keys("d", 2, NB)
                    for q in range(3, len(SPLIT)):
                        low(q)

                    for q in range(FFN_BLOCKS):
                        pool.wait_ge(*at("act_w", (q, 1)))
                        G().tensor_tensor(wlo[q % 2][:, 1024:2048], ring[:, (FIRST_FFN + q) % RING, 1024:2048], whi[q % 2][:, 1024:2048],
                                        ALU.subtract).then_inc(*ev("pool_w", q))

            nc.all_engine_barrier()
            numbers = sorted(s.num for s in C.sems.values())
            for first in (n for n in numbers if n - 1 not in numbers):
                end = first
                while end in numbers:
                    end += 1
                nc.gpsimd.sem_clear(range(first, end))
            nc.all_engine_barrier()
        return dict(C.value)


def _f(v):
    return np.asarray(v)


def pack(inp):
    g = {k: _f(v) for k, v in inp.items()}
    L, f = DEPTH, g["x_prompt"].dtype
    out = {}

    def feat(v):
        return v.T.reshape(-1, P, v.shape[0]).transpose(1, 0, 2)

    out["x"] = feat(np.concatenate([g["x_prompt"].reshape(SEQ, -1), g["x_sample"].reshape(NS, -1)]))
    out["c"] = feat(np.concatenate([g["c_prompt"], g["c_sample"]]))
    out["pages"] = g["page_table"].reshape(1, -1)
    out["consts"] = np.concatenate(list(CONST.values()), 1)

    def tiles(v):
        k, m = v.shape
        return v.reshape(k // P, P, m // P, P).transpose(1, 2, 0, 3)

    wp = np.zeros((L, NBLK, P, 2048), f)
    small = np.zeros((L, P, NSM), f)
    for l in range(L):
        w_in, b_in = g["w_in"][l], g["b_in"][l]
        uq = g["mla_w_uq"][l].reshape(QR, BH, NOPE + ROPE)
        uq = tiles(np.concatenate([uq[:, :, :NOPE].reshape(QR, -1), uq[:, :, NOPE:].reshape(QR, -1)], 1)).reshape(P, -1)
        uk = g["mla_w_uk"][l]
        ffn1, ffn3 = tiles(g["w_ffn1"][l]), tiles(g["w_ffn3"][l])
        ffn2 = tiles(g["w_ffn2"][l]).reshape(P, 11, 2048)
        wout = tiles(g["w_out"][l]).reshape(P, 4, 2048)
        for n, b in enumerate(BLOCKS):
            d = wp[l, n]
            if b[0] == "ada":
                d[:] = g["w_ada"][l][:, b[1] * 256:(b[1] + 1) * 256].reshape(KC, P, 256).transpose(1, 0, 2).reshape(P, -1)
            elif b[0] == "in":
                dd = d.reshape(P, 2, KC, P)
                for j, name in enumerate(b[1:]):
                    for at, col, cnt in tile_columns(name):
                        dd[:, j, :, at:at + cnt] = w_in[:, col:col + cnt].reshape(KC, P, cnt).transpose(1, 0, 2)
            elif b[0] == "uq":
                d[:] = uq[:, :2048]
            elif b[0] == "uk":
                d[:, :1024] = uk.reshape(2, P, 512).transpose(1, 0, 2).reshape(P, -1)
                d[:, 1024:1280] = uq[:, 2048:]
            elif b[0] == "ukT":
                d[:64] = uk.transpose(2, 1, 0).reshape(64, -1)
            elif b[0] == "branch":
                d[:] = tiles(g["w_branch"][l, b[1]])[:, b[2]:b[2] + 4].reshape(P, -1)
            elif b[0] == "out":
                d[:] = wout[:, b[1]]
            elif b[0] == "ffn":
                d[:, :1024] = ffn1[:, b[1]].reshape(P, -1)
                d[:, 1024:] = ffn3[:, b[1]].reshape(P, -1)
            elif b[0] == "ffn2":
                d[:] = ffn2[:, b[1]]
        s = small[l]
        s[:, 0:48] = g["b_ada"][l].reshape(48, P).T
        for name in TILES:
            for at, col, cnt in tile_columns(name):
                s[at:at + cnt, BIAS[name]] = b_in[col:col + cnt]
        for name, v in (("qn", "mla_q_norm"), ("kvn", "mla_kv_norm"), ("cb", "conv_b"), ("clg", "conv_ln_g"), ("clb", "conv_ln_b"),
                        ("ln1g", "ln1_g"), ("ln1b", "ln1_b"), ("ln2g", "ln2_g"), ("ln2b", "ln2_b")):
            w = g[v][l]
            s[:, SM[name]:SM[name] + w.size // P] = w.reshape(-1, P).T
        s[:, SM["cw"]:SM["cw"] + 4 * CW] = g["conv_w"][l].T.reshape(4, P, CW).transpose(1, 0, 2).reshape(P, -1)
    out["wpack"], out["small"] = wp, small
    out["wuv"] = g["mla_w_uv"].reshape(L, 2, P, 512).transpose(0, 2, 1, 3)
    cache = g["cache_mla"]
    lat = cache[..., :KVR]
    latT = lat.reshape(L, POOL, P, 2, P).transpose(0, 1, 4, 3, 2).reshape(L, POOL, P, 2 * P)
    turned = np.zeros(latT.shape[:3] + (P,), latT.dtype)
    turned[:, :, 64:96] = cache[..., KVR:].transpose(0, 1, 3, 2)
    out["cache"] = np.concatenate([latT, lat, turned], 3)
    out["stateA"] = np.concatenate([g["state_mlstm_C"], g["state_mlstm_n"][..., None]], 4).transpose(0, 3, 1, 2, 4)
    out["stateD"] = g["state_ret"].transpose(0, 3, 1, 2, 4)
    out["m0"] = g["state_mlstm_m"].transpose(0, 2, 1)
    out["hist"] = g["state_conv"].reshape(L, NB, CW - 1, 4, P).transpose(0, 4, 3, 1, 2)
    return {k: np.ascontiguousarray(v) for k, v in out.items()}


OUTS = {"o_y": (P, KC, T), "o_rows_c": (DEPTH, P, 2, T), "o_rows_k": (DEPTH, ROPE, T), "o_cn_p": (DEPTH, P, H, W),
        "o_cn_s": (DEPTH, P, NB, H, W), "o_m": (DEPTH, H, 9), "o_conv_p": (DEPTH, P, 4, CW - 1),
        "o_conv_s": (DEPTH, P, 4, NB, CW - 1), "o_ret_p": (DEPTH, P, H, P), "o_ret_s": (DEPTH, P, NB, H, P)}


def kernel(**inputs):
    import concourse.bacc as bacc
    from concourse.bass_utils import run_bass_kernel_spmd

    arrays = pack(inputs)

    def build(known):
        nc = bacc.Bacc("TRN2", target_bir_lowering=False, num_devices=1)
        a = {k: nc.dram_tensor(k + "_dram", v.shape, mybir.dt.from_np(v.dtype), kind="ExternalInput").ap() for k, v in arrays.items()}
        for k, s in OUTS.items():
            a[k] = nc.dram_tensor(k, s, F32, kind="ExternalOutput").ap()
        return nc, decoder_program(nc, a, known)

    _, counted = build({})
    nc, again = build(counted)
    assert counted == again
    r = run_bass_kernel_spmd(nc, [{k + "_dram": v for k, v in arrays.items()}], core_ids=[0]).results[0]

    L = DEPTH
    y = r["o_y"].transpose(2, 1, 0).reshape(T, D_MODEL)
    rows = np.concatenate([r["o_rows_c"].transpose(0, 3, 2, 1).reshape(L, T, KVR), r["o_rows_k"].transpose(0, 2, 1)], 2)
    cn_p, cn_s = r["o_cn_p"].transpose(0, 2, 1, 3)[:, None], r["o_cn_s"].transpose(0, 2, 3, 1, 4)
    m = r["o_m"].transpose(0, 2, 1)
    conv_p = r["o_conv_p"].transpose(0, 3, 2, 1).reshape(L, 1, CW - 1, CCH)
    conv_s = r["o_conv_s"].transpose(0, 3, 4, 2, 1).reshape(L, NB, CW - 1, CCH)
    got = (y[:SEQ].reshape(1, SEQ, D_MODEL), y[SEQ:].reshape(NB, TS, D_MODEL),
           rows[:, :SEQ].reshape(L, 1, SEQ, -1), rows[:, SEQ:].reshape(L, NB, TS, -1),
           cn_p[..., :P], cn_s[..., :P], cn_p[..., P], cn_s[..., P], m[:, 0:1], m[:, 1:], conv_p, conv_s,
           r["o_ret_p"].transpose(0, 2, 1, 3)[:, None], r["o_ret_s"].transpose(0, 2, 3, 1, 4))
    return tuple(np.ascontiguousarray(v) for v in got)
```
